# Optimizing a Trainium2 kernel written in Bass

```python
import jax, jax.numpy as jnp
from jax import lax
import numpy as np

D_MODEL = 1024
BATCH = 1
SEQ = 1024
DEPTH = 1
DEC_BATCH = 8
DEC_SEQ = 4
PAST_LEN = 8192
PAGE_SIZE = 128

GLA_HEADS = 4
GLA_DK = D_MODEL // 8
GLA_DV = D_MODEL // 4
GLA_KW = GLA_HEADS * GLA_DK
GLA_VW = GLA_HEADS * GLA_DV
GLA_GATE_RANK = 16
GLA_GATE_TAU = 16.0
GLA_CHUNK = 64
GLA_NORM_EPS = 1e-5

RW_HEAD = 64
RW_HEADS = D_MODEL // RW_HEAD
RW_W = RW_HEADS * RW_HEAD
RW_DECAY_RANK = 64
RW_A_RANK = 64
RW_GATE_RANK = 128
RW_SHIFT_W = 3 * RW_W + RW_DECAY_RANK + RW_A_RANK + RW_GATE_RANK
RW_GN_EPS = 64e-5

O_GQ = 0
O_GK = O_GQ + GLA_KW
O_GV = O_GK + GLA_KW
O_GG = O_GV + GLA_VW
O_GA = O_GG + GLA_VW
O_RW = O_GA + GLA_GATE_RANK
O_MG = O_RW + RW_SHIFT_W
PROJ_W = O_MG + 2 * D_MODEL

R_R = 0
R_K = RW_W
R_V = 2 * RW_W
R_WL = 3 * RW_W
R_AL = R_WL + RW_DECAY_RANK
R_GL = R_AL + RW_A_RANK

PEER_HEADS = 8
PEER_NKEYS = 128
PEER_N = PEER_NKEYS * PEER_NKEYS
PEER_QHALF = 128
PEER_TOPK = 16
PEER_BLOCK = 128

NORM_EPS = 1e-6

kernel_name = 'hybrid_gla_rwkv7_peer_step'

def rmsnorm(x, g):
    xf = x.astype(jnp.float32)
    y = xf * lax.rsqrt(jnp.mean(xf * xf, axis=-1, keepdims=True) + NORM_EPS)
    return (y * g).astype(x.dtype)

def gla_chunked(q, k, v, la, S0):
    B, T, H, DK = q.shape
    DV = v.shape[-1]
    C = min(GLA_CHUNK, T)
    n = -(-T // C)
    pad = n * C - T

    def prep(a):
        a = jnp.pad(a, ((0, 0), (0, pad), (0, 0), (0, 0)))
        return a.reshape(B, n, C, H, a.shape[-1]).transpose(1, 0, 3, 2, 4)

    qc, kc, vc, lc = prep(q), prep(k), prep(v), prep(la)
    mask = jnp.tril(jnp.ones((C, C), dtype=bool))

    def step(S, inp):
        qi, ki, vi, li = inp
        b = jnp.cumsum(li, axis=2)
        bl = b[:, :, -1:, :]
        qe = qi * jnp.exp(b)
        A = jnp.einsum('bhcd,bhsd->bhcs', qe, ki * jnp.exp(-b))
        A = jnp.where(mask, A, 0.0)
        o = jnp.einsum('bhcd,bhde->bhce', qe, S) + jnp.einsum('bhcs,bhse->bhce', A, vi)
        S = jnp.exp(bl[:, :, 0, :])[..., None] * S + jnp.einsum('bhsd,bhse->bhde', ki * jnp.exp(bl - b), vi)
        return S, o

    S, o = lax.scan(step, S0, (qc, kc, vc, lc))
    o = o.transpose(1, 0, 3, 2, 4).reshape(B, n * C, H, DV)[:, :T]
    return o, S

def rwkv7_scan(r, w, k, v, a, b, S0):
    seq = tuple(jnp.moveaxis(z, 1, 0) for z in (r, w, k, v, a, b))

    def step(S, inp):
        r_, w_, k_, v_, a_, b_ = inp
        sa = jnp.einsum('bhvk,bhk->bhv', S, a_)
        S = S * w_[:, :, None, :] + sa[..., :, None] * b_[..., None, :] + v_[..., :, None] * k_[..., None, :]
        return S, jnp.einsum('bhvk,bhk->bhv', S, r_)

    S, o = lax.scan(step, S0, seq)
    return jnp.moveaxis(o, 0, 1), S

def mixer(h, S_gla0, S_rw0, shift0, lp):
    B, T, _ = h.shape
    f32 = jnp.float32
    p = jnp.einsum('btd,de->bte', h, lp['w_in'])

    q = p[..., O_GQ:O_GK].reshape(B, T, GLA_HEADS, GLA_DK) * (GLA_DK ** -0.5)
    kg = p[..., O_GK:O_GV].reshape(B, T, GLA_HEADS, GLA_DK)
    vg = p[..., O_GV:O_GG].reshape(B, T, GLA_HEADS, GLA_DV)
    gg = p[..., O_GG:O_GA]
    z = p[..., O_GA:O_RW] @ lp['w_gla_gate'] + lp['b_gla_gate']
    la = (jax.nn.log_sigmoid(z.astype(f32)) / GLA_GATE_TAU).reshape(B, T, GLA_HEADS, GLA_DK)
    og, S_gla = gla_chunked(q.astype(f32), kg.astype(f32), vg.astype(f32), la, S_gla0.astype(f32))
    og = og * lax.rsqrt(jnp.mean(og * og, axis=-1, keepdims=True) + GLA_NORM_EPS)
    og = og.reshape(B, T, GLA_VW).astype(h.dtype) * lp['g_gla_norm'] * jax.nn.silu(gg)
    br_gla = og @ lp['w_b_gla']

    pr = p[..., O_RW:O_MG]
    prev = jnp.concatenate([shift0[:, None, :].astype(pr.dtype), pr[:, :-1]], axis=1)
    pm = pr + (prev - pr) * lp['mu_shift']
    r = pm[..., R_R:R_K]
    kr = pm[..., R_K:R_V]
    vr = pm[..., R_V:R_WL]
    wl = pm[..., R_WL:R_AL]
    al = pm[..., R_AL:R_GL]
    gl = pm[..., R_GL:]
    wlog = -jax.nn.softplus(-(lp['rw_w0'] + jnp.tanh(wl) @ lp['rw_w2']).astype(f32)) - 0.5
    decay = jnp.exp(-jnp.exp(wlog))
    a = jax.nn.sigmoid(lp['rw_a0'] + al @ lp['rw_a2'])
    gate = jax.nn.sigmoid(gl) @ lp['rw_g2']

    def hs(t):
        return t.reshape(B, T, RW_HEADS, RW_HEAD).astype(f32)

    kk = hs(kr * lp['rw_k_k'])
    kk = kk / jnp.maximum(jnp.sqrt(jnp.sum(kk * kk, axis=-1, keepdims=True)), 1e-12)
    kmod = hs(kr * (1.0 + (a - 1.0) * lp['rw_k_a']))
    rh, vh = hs(r), hs(vr)
    o_r, S_rw = rwkv7_scan(rh, hs(decay), kmod, vh, -kk, kk * hs(a), S_rw0.astype(f32))
    mu = jnp.mean(o_r, axis=-1, keepdims=True)
    var = jnp.mean((o_r - mu) ** 2, axis=-1, keepdims=True)
    o_r = ((o_r - mu) * lax.rsqrt(var + RW_GN_EPS)).reshape(B, T, RW_W) * lp['rw_gn_w'] + lp['rw_gn_b']
    bonus = jnp.sum(rh * kmod * lp['rw_r_k'], axis=-1, keepdims=True) * vh
    o_r = (o_r + bonus.reshape(B, T, RW_W)) * gate
    br_rw = o_r.astype(h.dtype) @ lp['w_b_rw']

    gates = jax.nn.sigmoid(p[..., O_MG:])
    merged = gates[..., :D_MODEL] * br_gla + gates[..., D_MODEL:] * br_rw
    y = merged @ lp['w_out']
    return y, S_gla.astype(S_gla0.dtype), S_rw.astype(S_rw0.dtype), pr[:, -1]

def peer(h, lp):
    B, T, D = h.shape
    M = B * T
    xt = h.reshape(M, D)
    q = (xt @ lp['peer_wq']).reshape(M, PEER_HEADS, 2, PEER_QHALF).astype(jnp.float32)
    s = jnp.einsum('mhpd,hpnd->mhpn', q, lp['peer_keys'].astype(jnp.float32))
    s1, i1 = lax.top_k(s[:, :, 0], PEER_TOPK)
    s2, i2 = lax.top_k(s[:, :, 1], PEER_TOPK)
    cand = (s1[..., :, None] + s2[..., None, :]).reshape(M, PEER_HEADS, PEER_TOPK * PEER_TOPK)
    cidx = (i1[..., :, None] * PEER_NKEYS + i2[..., None, :]).reshape(M, PEER_HEADS, PEER_TOPK * PEER_TOPK)
    top, j = lax.top_k(cand, PEER_TOPK)
    idx = jnp.take_along_axis(cidx, j, axis=-1).reshape(M, PEER_HEADS * PEER_TOPK)
    wts = jax.nn.softmax(top, axis=-1).reshape(M, PEER_HEADS * PEER_TOPK)
    nb = -(-M // PEER_BLOCK)
    pad = nb * PEER_BLOCK - M
    xb = jnp.pad(xt, ((0, pad), (0, 0))).reshape(nb, PEER_BLOCK, D)
    ib = jnp.pad(idx, ((0, pad), (0, 0))).reshape(nb, PEER_BLOCK, -1)
    wb = jnp.pad(wts, ((0, pad), (0, 0))).reshape(nb, PEER_BLOCK, -1)
    pu, pv = lp['peer_u'], lp['peer_v']

    def blk(args):
        xx, ii, ww = args
        u = jnp.take(pu, ii, axis=0)
        act = jax.nn.gelu(jnp.einsum('md,mkd->mk', xx, u), approximate=False)
        vv = jnp.take(pv, ii, axis=0)
        return jnp.einsum('mk,mkd->md', (act * ww).astype(xx.dtype), vv)

    out = lax.map(blk, (xb, ib, wb)).reshape(nb * PEER_BLOCK, D)[:M]
    return out.reshape(B, T, D)

def block(x, c, S_gla0, S_rw0, shift0, lp):
    mod = jax.nn.silu(c) @ lp['w_ada'] + lp['b_ada']
    shift1, scale1, gate1, shift2, scale2, gate2 = jnp.split(mod[:, None, :], 6, axis=-1)
    h = rmsnorm(x, lp['g_pre_mix']) * (1.0 + scale1) + shift1
    y, S_gla, S_rw, shift_new = mixer(h, S_gla0, S_rw0, shift0, lp)
    x = x + gate1 * rmsnorm(y, lp['g_post_mix'])
    h2 = rmsnorm(x, lp['g_pre_ffn']) * (1.0 + scale2) + shift2
    y2 = peer(h2, lp)
    x = x + gate2 * rmsnorm(y2, lp['g_post_ffn'])
    return x, S_gla, S_rw, shift_new

def setup_inputs(seed: int = 0) -> dict:
    key = jax.random.key(seed)
    ks = iter(jax.random.split(key, 48))
    f32 = jnp.float32

    def nrm(shape, scale):
        return jax.random.normal(next(ks), shape, f32) * scale

    def gain(shape):
        return 1.0 + 0.05 * jax.random.normal(next(ks), shape, f32)

    L, D = DEPTH, D_MODEL
    return {
        'x_prompt': nrm((BATCH, SEQ, D), 1.0),
        'x_sample': nrm((DEC_BATCH, DEC_SEQ, D), 1.0),
        'c_prompt': nrm((BATCH, D), 1.0),
        'c_sample': nrm((DEC_BATCH, D), 1.0),
        'state_gla': nrm((L, DEC_BATCH, GLA_HEADS, GLA_DK, GLA_DV), 0.5),
        'state_rwkv': nrm((L, DEC_BATCH, RW_HEADS, RW_HEAD, RW_HEAD), 0.5),
        'state_shift': nrm((L, DEC_BATCH, RW_SHIFT_W), 1.0),
        'w_ada': nrm((L, D, 6 * D), 0.5 * D ** -0.5),
        'b_ada': nrm((L, 6 * D), 0.01),
        'g_pre_mix': gain((L, D)),
        'g_post_mix': gain((L, D)),
        'g_pre_ffn': gain((L, D)),
        'g_post_ffn': gain((L, D)),
        'w_in': nrm((L, D, PROJ_W), D ** -0.5),
        'w_gla_gate': nrm((L, GLA_GATE_RANK, GLA_KW), GLA_GATE_RANK ** -0.5),
        'b_gla_gate': nrm((L, GLA_KW), 0.1),
        'g_gla_norm': gain((L, GLA_VW)),
        'mu_shift': jax.random.uniform(next(ks), (L, RW_SHIFT_W), f32),
        'rw_w0': jax.random.uniform(next(ks), (L, RW_W), f32, -6.0, -1.0),
        'rw_w2': nrm((L, RW_DECAY_RANK, RW_W), 0.1 * RW_DECAY_RANK ** -0.5),
        'rw_a0': nrm((L, RW_W), 0.1),
        'rw_a2': nrm((L, RW_A_RANK, RW_W), 0.5 * RW_A_RANK ** -0.5),
        'rw_g2': nrm((L, RW_GATE_RANK, RW_W), RW_GATE_RANK ** -0.5),
        'rw_k_k': 0.85 + nrm((L, RW_W), 0.05),
        'rw_k_a': 1.0 + nrm((L, RW_W), 0.05),
        'rw_r_k': nrm((L, RW_HEADS, RW_HEAD), 0.1),
        'rw_gn_w': gain((L, RW_W)),
        'rw_gn_b': nrm((L, RW_W), 0.01),
        'w_b_gla': nrm((L, GLA_VW, D), GLA_VW ** -0.5),
        'w_b_rw': nrm((L, RW_W, D), RW_W ** -0.5),
        'w_out': nrm((L, D, D), D ** -0.5),
        'peer_wq': nrm((L, D, PEER_HEADS * 2 * PEER_QHALF), D ** -0.5),
        'peer_keys': nrm((L, PEER_HEADS, 2, PEER_NKEYS, PEER_QHALF), PEER_QHALF ** -0.5),
        'peer_u': nrm((L, PEER_N, D), D ** -0.5),
        'peer_v': nrm((L, PEER_N, D), D ** -0.5),
    }

def reference(x_prompt, x_sample, c_prompt, c_sample, state_gla, state_rwkv, state_shift,
              w_ada, b_ada, g_pre_mix, g_post_mix, g_pre_ffn, g_post_ffn, w_in, w_gla_gate, b_gla_gate,
              g_gla_norm, mu_shift, rw_w0, rw_w2, rw_a0, rw_a2, rw_g2, rw_k_k, rw_k_a, rw_r_k, rw_gn_w,
              rw_gn_b, w_b_gla, w_b_rw, w_out, peer_wq, peer_keys, peer_u, peer_v):
    xp, xs = x_prompt, x_sample
    gla_p, rw_p, sh_p, gla_s, rw_s, sh_s = [], [], [], [], [], []
    for l in range(DEPTH):
        lp = dict(w_ada=w_ada[l], b_ada=b_ada[l], g_pre_mix=g_pre_mix[l], g_post_mix=g_post_mix[l],
                  g_pre_ffn=g_pre_ffn[l], g_post_ffn=g_post_ffn[l], w_in=w_in[l], w_gla_gate=w_gla_gate[l],
                  b_gla_gate=b_gla_gate[l], g_gla_norm=g_gla_norm[l], mu_shift=mu_shift[l], rw_w0=rw_w0[l],
                  rw_w2=rw_w2[l], rw_a0=rw_a0[l], rw_a2=rw_a2[l], rw_g2=rw_g2[l], rw_k_k=rw_k_k[l],
                  rw_k_a=rw_k_a[l], rw_r_k=rw_r_k[l], rw_gn_w=rw_gn_w[l], rw_gn_b=rw_gn_b[l],
                  w_b_gla=w_b_gla[l], w_b_rw=w_b_rw[l], w_out=w_out[l], peer_wq=peer_wq[l],
                  peer_keys=peer_keys[l], peer_u=peer_u[l], peer_v=peer_v[l])
        Bp = xp.shape[0]
        zg = jnp.zeros((Bp, GLA_HEADS, GLA_DK, GLA_DV), xp.dtype)
        zr = jnp.zeros((Bp, RW_HEADS, RW_HEAD, RW_HEAD), xp.dtype)
        zs = jnp.zeros((Bp, RW_SHIFT_W), xp.dtype)
        xp, g1, r1, s1 = block(xp, c_prompt, zg, zr, zs, lp)
        xs, g2, r2, s2 = block(xs, c_sample, state_gla[l], state_rwkv[l], state_shift[l], lp)
        gla_p.append(g1)
        rw_p.append(r1)
        sh_p.append(s1)
        gla_s.append(g2)
        rw_s.append(r2)
        sh_s.append(s2)
    return (xp, xs, jnp.stack(gla_p), jnp.stack(rw_p), jnp.stack(sh_p), jnp.stack(gla_s), jnp.stack(rw_s), jnp.stack(sh_s))


_drawn_inputs = setup_inputs


def setup_inputs(seed=0):
    import zlib

    import numpy as np

    out = dict(_drawn_inputs(seed))
    spreads = {}
    factors = {'g_post_ffn': 4.05, 'rw_w2': 4.184, 'rw_gn_b': 4.121}
    for name, (base, spread) in spreads.items():
        noise = np.random.default_rng([zlib.crc32(name.encode()), seed]).standard_normal(out[name].shape)
        drawn = base * np.exp(spread * noise) if base else spread * noise
        out[name] = __import__('jax').numpy.asarray(drawn.astype(out[name].dtype))
    for name, factor in factors.items():
        out[name] = (out[name] * factor).astype(out[name].dtype)
    return out
```

```python
from contextlib import ExitStack

import numpy as np

import concourse.bass as bass
from concourse import mybir

F32 = mybir.dt.float32
U32 = mybir.dt.uint32
ALU = mybir.AluOpType
ACT = mybir.ActivationFunctionType
AX = mybir.AxisListType

P = 128
D = 1024
KD = D // P
SEQ = 1024
NB, NT = 8, 4
NS = NB * NT
M = SEQ + NS
NSEQ = 1 + NB
G3 = M // 3
TILES = SEQ // P
NORM_EPS = 1e-6


S1, A1, G1, S2, A2, G2 = range(6)


class Stage:

    def __init__(self, nc, ctx, name):
        self.nc, self.ctx, self.name = nc, ctx, name

    def sb(self, name, shape, dtype=F32):
        return self.ctx.enter_context(self.nc.sbuf_tensor(f"{self.name}_{name}", shape, dtype))

    def ps(self, name, shape=(P, 512)):
        return self.ctx.enter_context(self.nc.psum_tensor(f"{self.name}_{name}", list(shape), F32))

    def sem(self, name):
        return self.nc.alloc_semaphore(name=f"{self.name}_{name}")


class Chain:

    def __init__(self, eng, sem):
        self.eng, self.sem, self.base, self.n = eng, sem, 0, 0

    def link(self, ins):
        self.n += 1
        ins.then_inc(self.sem, 1)
        self.eng.wait_ge(self.sem, self.base + self.n)

    def enter(self, i, per):
        self.before, self.per = self.n, per
        self.base, self.n = self.n + i * per, 0

    def leave(self, count):
        assert self.n == self.per, (self.n, self.per)
        self.base, self.n = 0, self.before + count * self.per


def modulation(nc, t):
    CG = 12
    with ExitStack() as ctx:
        s = Stage(nc, ctx, "mod")
        cT = s.sb("cT", [P, KD * NSEQ])
        sg = s.sb("sg", [P, KD * NSEQ])
        w = s.sb("w", [P, 3, KD * 512])
        bias = s.sb("bias", [1, 6 * D])
        ones = s.sb("ones", [1, NSEQ])
        gains = s.sb("gains", [NSEQ, 4, D])
        out = s.sb("out", [NSEQ, 6, D])
        acc = s.ps("acc", [P, 4, 512])
        small_in = s.sem("small_in")
        w_in = [s.sem(f"w_in{n}") for n in range(3)]
        ready = s.sem("silu_ready")
        expd = s.sem("exp_done")
        summed = s.sem("summed")
        copied = s.sem("copied")
        done = s.sem("combined")
        stored = s.sem("stored")
        own = s.sem("vector_chain")
        with nc.Block() as block:
            @block.sync
            def _(sp):
                sp.dma_start(cT[:, :], t["cT"]).then_inc(small_in, 16)
                sp.dma_start(bias[:, :], t["b_ada"]).then_inc(small_in, 16)
                for n in range(4):
                    sp.dma_start(gains[:, n, :], t["gains"][n:n + 1, :].broadcast_to([NSEQ, D])).then_inc(small_in, 16)
                for g in range(CG):
                    if g >= 3:
                        sp.wait_ge(summed, g - 2)
                    sp.dma_start(w[:, g % 3, :], t["w_ada"][g]).then_inc(w_in[g % 3], 16)
                sp.wait_ge(done, 1)
                sp.dma_start(t["mod"], out[:, :, :]).then_inc(stored, 16)
                sp.wait_ge(stored, 16)

            @block.scalar
            def _(act):
                act.wait_ge(small_in, 96)
                act.activation(sg[:, :], cT[:, :], ACT.Exp, scale=-1.0).then_inc(expd, 1)
                for g in range(CG):
                    act.wait_ge(summed, g + 1)
                    act.copy(out[:, g // 2, (g % 2) * 512:(g % 2) * 512 + 512],
                             acc[0:NSEQ, g % 4, :]).then_inc(copied, 1)

            @block.vector
            def _(dve):
                ch = Chain(dve, own)
                ch.link(dve.memset(ones[:, :], 1.0))
                dve.wait_ge(expd, 1)
                ch.link(dve.tensor_scalar_add(sg[:, :], sg[:, :], 1.0))
                ch.link(dve.reciprocal(sg[:, :], sg[:, :]))
                dve.tensor_tensor(sg[:, :], sg[:, :], cT[:, :], ALU.mult).then_inc(ready, 1)
                dve.wait_ge(copied, CG)
                for n, row in ((0, 1), (2, 4)):
                    ch.link(dve.scalar_tensor_tensor(out=out[:, row, :], in0=out[:, row, :], scalar=1.0,
                                                     in1=gains[:, n, :], op0=ALU.add, op1=ALU.mult))
                ch.link(dve.tensor_tensor(out[:, 2, :], out[:, 2, :], gains[:, 1, :], ALU.mult))
                dve.tensor_tensor(out[:, 5, :], out[:, 5, :], gains[:, 3, :], ALU.mult).then_inc(done, 1)

            @block.tensor
            def _(pe):
                pe.wait_ge(ready, 1)
                for g in range(CG):
                    pe.wait_ge(w_in[g % 3], 16 * (g // 3 + 1))
                    if g >= 4:
                        pe.wait_ge(copied, g - 3)
                    for k in range(KD):
                        pe.matmul(acc[0:NSEQ, g % 4, :], sg[:, k * NSEQ:(k + 1) * NSEQ],
                                  w[:, g % 3, k * 512:(k + 1) * 512], start=(k == 0), stop=False)
                    pe.matmul(acc[0:NSEQ, g % 4, :], ones[0:1, :], bias[0:1, g * 512:(g + 1) * 512],
                              start=False, stop=True).then_inc(summed, 1)


def load_mod(eng, t, dst, row, samples, sem):
    if not samples:
        eng.dma_start(dst[:, :], t["mod"][0:1, row, :].broadcast_to([P, D])).then_inc(sem, 16)
        return
    for b in range(NB):
        eng.dma_start(dst[b * NT:(b + 1) * NT, :],
                      t["mod"][1 + b:2 + b, row, :].broadcast_to([NT, D])).then_inc(sem, 16)


def projection(nc, t):
    PT = t["w_in"].shape[0]
    W = 2
    ITER = PT // W
    assert ITER * W == PT
    with ExitStack() as ctx:
        s = Stage(nc, ctx, "proj")
        x = s.sb("x", [P, TILES, D])
        xs = s.sb("xs", [NS, D])
        h = s.sb("h", [P, 2, D])
        A, S = s.sb("A", [P, D]), s.sb("S", [P, D])
        As, Ss = s.sb("As", [NS, D]), s.sb("Ss", [NS, D])
        ident = s.sb("ident", [P, P])
        ssq = s.sb("ssq", [P, TILES + 1])
        eps = s.sb("eps", [P, 1])
        hT = s.sb("hT", [P, KD, M])
        w = s.sb("w", [P, W, KD, P])
        wg = s.sb("wg", [P, KD, 16])
        o = s.sb("o", [P, W, M])
        og = s.sb("og", [16, M])
        acc = [s.ps(f"acc{n}", [P, 3, 512]) for n in range(W)]
        consts_in, x_in, wg_in = s.sem("consts_in"), s.sem("x_in"), s.sem("wg_in")
        w_in = [s.sem(f"w_in{n}") for n in range(W)]
        cleared = s.sem("cleared")
        squared = s.sem("squared")
        h_ready = s.sem("h_ready")
        turned = s.sem("turned")
        hT_lo, hT_hi = s.sem("hT_lo"), s.sem("hT_hi")
        tile_done = s.sem("tile_done")
        first_out = s.sem("first_out")
        rest_out = s.sem("rest_out")
        stored = [s.sem(f"stored{n}") for n in range(W)]
        own, own_act = s.sem("vector_chain"), s.sem("scalar_chain")

        with nc.Block() as block:
            @block.sync
            def _(sp):
                sp.dma_start(x[:, :, :], t["x"][0:SEQ, :].rearrange("(i p) d -> p i d", p=P)).then_inc(x_in, 16)
                sp.dma_start(xs[:, :], t["x"][SEQ:M, :]).then_inc(x_in, 16)
                sp.dma_start(ident[:, :], t["ident"]).then_inc(consts_in, 16)
                load_mod(sp, t, A, A1, False, consts_in)
                load_mod(sp, t, S, S1, False, consts_in)
                load_mod(sp, t, As, A1, True, consts_in)
                load_mod(sp, t, Ss, S1, True, consts_in)
                sp.dma_start(wg[:, :, :], t["w_ga"]).then_inc(wg_in, 16)
                for n in range(W):
                    sp.dma_start(w[:, n, :, :], t["w_in"][n]).then_inc(w_in[n], 16)
                with sp.Fori(0, ITER - 1) as i:
                    for n in range(W):
                        sp.wait_ge(tile_done, i * W + n + 1)
                        sp.dma_start(w[:, n, :, :], t["w_in"][i * W + (W + n)]).then_inc(w_in[n], 16)
                        sp.wait_ge(first_out, i * W + n + 1)
                        sp.wait_ge(rest_out, i * W + n + 1)
                        sp.dma_start(t["pT"][i * W + n], o[:, n, :]).then_inc(stored[n], 16)
                for n in range(W):
                    sp.wait_ge(first_out, (ITER - 1) * W + n + 1)
                    sp.wait_ge(rest_out, (ITER - 1) * W + n + 1)
                    sp.dma_start(t["pT"][PT - W + n], o[:, n, :]).then_inc(stored[n], 16)
                sp.wait_ge(first_out, PT + 1)
                sp.wait_ge(rest_out, PT + 1)
                sp.dma_start(t["gaT"], og[:, :]).then_inc(stored[0], 16)
                for n in range(W):
                    sp.wait_ge(stored[n], 16 * (ITER + (n == 0)))

            @block.scalar
            def _(act):
                ch = Chain(act, own_act)
                act.wait_ge(x_in, 32)
                act.wait_ge(cleared, 2)
                for i in range(TILES):
                    ch.link(act.activation(h[:, 0, :], x[:, i, :], ACT.Square, accum_out=ssq[:, i:i + 1]))
                ch.link(act.activation(h[0:NS, 0, :], xs[:, :], ACT.Square, accum_out=ssq[0:NS, TILES:TILES + 1]))
                ch.link(act.activation(ssq[:, :], ssq[:, :], ACT.Ln, bias=eps[:, :], scale=1.0 / D))
                act.activation(ssq[:, :], ssq[:, :], ACT.Exp, scale=-0.5).then_inc(squared, 1)
                with act.Fori(0, TILES // 2) as i:
                    for n in range(2):
                        act.wait_ge(turned, i * 2 + n + 1)
                        act.copy(hT[:, 0:4, bass.ts(i * 2 + n, P)],
                                 acc[n][:, 0, :].rearrange("p (k c) -> p k c", k=4)).then_inc(hT_lo, 1)
                act.wait_ge(turned, TILES + 1)
                act.copy(hT[:, 0:4, SEQ:M], acc[0][:, 0, 0:4 * NS].rearrange("p (k c) -> p k c", k=4)).then_inc(hT_lo, 1)

                def evacuate(i, first):
                    for n in range(W):
                        act.wait_ge(tile_done, i * W + n + 1)
                        if not first:
                            act.wait_ge(stored[n], i * 16)
                        act.copy(o[:, n, 0:G3], acc[n][:, 0, 0:G3]).then_inc(first_out, 1)

                evacuate(0, True)
                with act.Fori(1, ITER) as i:
                    evacuate(i, False)
                act.wait_ge(tile_done, PT + 1)
                act.copy(og[:, 0:G3], acc[0][0:16, 0, 0:G3]).then_inc(first_out, 1)

            @block.vector
            def _(dve):
                ch = Chain(dve, own)
                dve.memset(eps[:, :], NORM_EPS).then_inc(cleared, 1)
                dve.memset(ssq[:, :], 1.0).then_inc(cleared, 1)
                dve.wait_ge(consts_in, 16 * (3 + 2 * NB))
                dve.wait_ge(squared, 1)
                PER = 1

                def hidden(xi, r, Ai, Si, rows, n):
                    ch.link(dve.scalar_tensor_tensor(out=h[0:rows, n, :], in0=xi, scalar=r, in1=Ai,
                                                     op0=ALU.mult, op1=ALU.mult))
                    dve.tensor_tensor(h[0:rows, n, :], h[0:rows, n, :], Si, ALU.add).then_inc(h_ready, 1)

                def copy_hT(dst, n, cols):
                    dve.tensor_copy(dst, acc[n][:, 1, 0:4 * cols].rearrange("p (k c) -> p k c", k=4)).then_inc(hT_hi, 1)

                for n in range(2):
                    hidden(x[:, n, :], ssq[:, n:n + 1], A[:, :], S[:, :], P, n)
                with dve.Fori(0, TILES // 2 - 1) as i:
                    ch.enter(i, 2)
                    for n in range(2):
                        dve.wait_ge(turned, i * 2 + n + 1)
                        copy_hT(hT[:, 4:8, bass.ts(i * 2 + n, P)], n, P)
                        hidden(x[:, i * 2 + (2 + n), :], ssq[:, bass.ds(i * 2 + (2 + n), 1)], A[:, :], S[:, :], P, n)
                    ch.leave(TILES // 2 - 1)
                dve.wait_ge(turned, TILES - 1)
                copy_hT(hT[:, 4:8, SEQ - 2 * P:SEQ - P], 0, P)
                hidden(xs[:, :], ssq[0:NS, TILES:TILES + 1], As[:, :], Ss[:, :], NS, 0)
                dve.wait_ge(turned, TILES)
                copy_hT(hT[:, 4:8, SEQ - P:SEQ], 1, P)
                dve.wait_ge(turned, TILES + 1)
                copy_hT(hT[:, 4:8, SEQ:M], 0, NS)

                def evacuate(i, first):
                    for n in range(W):
                        dve.wait_ge(tile_done, i * W + n + 1)
                        if not first:
                            dve.wait_ge(stored[n], i * 16)
                        dve.tensor_copy(o[:, n, G3:M].rearrange("p (g c) -> p g c", g=2),
                                        acc[n][:, 1:3, 0:G3]).then_inc(rest_out, 1)

                evacuate(0, True)
                with dve.Fori(1, ITER) as i:
                    evacuate(i, False)
                dve.wait_ge(tile_done, PT + 1)
                dve.tensor_copy(og[:, G3:M].rearrange("p (g c) -> p g c", g=2),
                                acc[0][0:16, 1:3, 0:G3]).then_inc(rest_out, 1)

            @block.tensor
            def _(pe):
                def turn(n, rows):
                    for k in range(KD):
                        last = pe.transpose(acc[n][:, k // 4, (k % 4) * rows:(k % 4 + 1) * rows],
                                            h[0:rows, n, k * P:(k + 1) * P], ident[0:rows, 0:rows])
                    last.then_inc(turned, 1)

                for n in range(2):
                    pe.wait_ge(h_ready, n + 1)
                    turn(n, P)
                with pe.Fori(0, TILES // 2 - 1) as i:
                    for n in range(2):
                        pe.wait_ge(h_ready, i * 2 + (3 + n))
                        pe.wait_ge(hT_lo, i * 2 + (n + 1))
                        pe.wait_ge(hT_hi, i * 2 + (n + 1))
                        turn(n, P)
                pe.wait_ge(h_ready, TILES + 1)
                pe.wait_ge(hT_lo, TILES - 1)
                pe.wait_ge(hT_hi, TILES - 1)
                turn(0, NS)
                pe.wait_ge(hT_lo, TILES + 1)
                pe.wait_ge(hT_hi, TILES + 1)

                def project(n, wn, m):
                    for g in range(3):
                        for k in range(KD):
                            last = pe.matmul(acc[n][0:m, g, 0:G3], wn[:, k, :], hT[:, k, g * G3:(g + 1) * G3],
                                             start=(k == 0), stop=(k == KD - 1))
                    last.then_inc(tile_done, 1)

                def tiles(i, first):
                    for n in range(W):
                        pe.wait_ge(w_in[n], i * 16 + 16)
                        if not first:
                            pe.wait_ge(first_out, (i - 1) * W + (n + 1))
                            pe.wait_ge(rest_out, (i - 1) * W + (n + 1))
                        project(n, w[:, n, :, :], P)

                tiles(0, True)
                with pe.Fori(1, ITER) as i:
                    tiles(i, False)
                pe.wait_ge(first_out, PT - W + 1)
                pe.wait_ge(rest_out, PT - W + 1)
                pe.wait_ge(wg_in, 16)
                project(0, wg[:, :, :], 16)


GH, GV, GC = 4, 256, 64


def gla(nc, t):
    with ExitStack() as ctx:
        s = Stage(nc, ctx, "gla")
        ident = s.sb("ident", [P, P])
        mask = s.sb("mask", [P, P])
        mask_s = s.sb("mask_s", [NS, NS])
        seq_rows = s.sb("seq_rows", [NS, NB])
        starts = s.sb("starts", [P, M])
        gaT = s.sb("gaT", [16, M])
        wz = s.sb("wz", [16, P])
        cst = s.sb("cst", [P, 3])
        qkv = s.sb("qkv", [P, 4, M])
        gate = s.sb("gate", [P, 2, M])
        S_in = s.sb("S_in", [P, NB, GV])
        S_out = s.sb("S_out", [P, NB, GV])
        z = s.sb("z", [P, M])
        sp_ = s.sb("softplus", [P, M])
        B = s.sb("B", [P, M])
        up, dn, rest = s.sb("exp_up", [P, M]), s.sb("exp_down", [P, M]), s.sb("exp_rest", [P, M])
        ends = s.sb("ends", [P, SEQ // GC + NB])
        qe, ke, k2 = s.sb("qe", [P, M]), s.sb("ke", [P, M]), s.sb("k2", [P, M])
        S = s.sb("S", [P, 4, GV])
        kv = s.sb("kv", [P, 2, 3 * P])
        k2s = s.sb("k2s", [NS, NB, P])
        at = s.sb("at", [P, 2, P])
        o = s.sb("o", [P, 2, M])
        ones = s.sb("ones", [P, P])
        eps = s.sb("eps", [P, 1])
        zero = s.sb("zero", [P, 2 * M])
        zb = s.ps("zb", [P, 3, 512])
        at_b = s.ps("at_b")
        turn_b = s.ps("turn_b")
        o_b = s.ps("o_b")
        s_b = [s.ps(f"s_b{n}") for n in range(2)]
        N = TILES + 1
        CH = SEQ // GC
        consts_in, head_in = s.sem("consts_in"), s.sem("head_in")
        cleared = s.sem("cleared")
        z_summed, z_ready, softplus_ready = s.sem("z_summed"), s.sem("z_ready"), s.sem("softplus_ready")
        B_ready, exps_ready, scaled = s.sem("B_ready"), s.sem("exps_ready"), s.sem("scaled")
        turned, kv_ready = s.sem("turned"), s.sem("kv_ready")
        at_summed, at_ready = s.sem("at_summed"), s.sem("at_ready")
        k2s_ready = s.sem("k2s_ready")
        s_summed, S_ready = s.sem("s_summed"), s.sem("S_ready")
        o_summed, o_ready = s.sem("o_summed"), s.sem("o_ready")
        squares_ready, ms_summed, rstd_ready = s.sem("squares_ready"), s.sem("ms_summed"), s.sem("rstd_ready")
        og_ready, stored = s.sem("og_ready"), s.sem("stored")
        own, own_act = s.sem("vector_chain"), s.sem("scalar_chain")
        LOADS = 10
        STORES = 3
        US = CH + NB

        with nc.Block() as block:
            @block.sync
            def _(sp):
                for dst, name in ((ident, "ident"), (mask, "gla_mask"), (mask_s, "gla_mask_s"),
                                  (seq_rows, "seq_rows"), (starts, "starts"), (gaT, "gaT")):
                    src = t[name]
                    if name == "starts":
                        src = src[:, 0:M].broadcast_to([P, M])
                    sp.dma_start(dst[:, :], src).then_inc(consts_in, 16)

                def load(h):
                    sp.dma_start(wz[:, :], t["w_gate"][h]).then_inc(head_in, 16)
                    sp.dma_start(cst[:, :], t["gla_cst"][h]).then_inc(head_in, 16)
                    sp.dma_start(qkv[:, 0, :], t["pT"][h]).then_inc(head_in, 16)
                    sp.dma_start(qkv[:, 1, :], t["pT"][h + GH]).then_inc(head_in, 16)
                    for n in range(2):
                        sp.dma_start(qkv[:, 2 + n, :], t["pT"][h * 2 + (2 * GH + n)]).then_inc(head_in, 16)
                        sp.dma_start(gate[:, n, :], t["pT"][h * 2 + (4 * GH + n)]).then_inc(head_in, 16)
                    sp.dma_start(S_in[:, 0:4, :], t["state_gla"][h][:, 0:4, :]).then_inc(head_in, 16)
                    sp.dma_start(S_in[:, 4:8, :], t["state_gla"][h][:, 4:8, :]).then_inc(head_in, 16)

                def store(h):
                    sp.wait_ge(S_ready, (h + 1) * (US + 1))
                    sp.dma_start(t["new_gla_p"][h], S[:, CH % 4, :]).then_inc(stored, 16)
                    sp.dma_start(t["new_gla_s"][h], S_out[:, :, :]).then_inc(stored, 16)
                    sp.wait_ge(og_ready, h + 1)
                    sp.dma_start(t["ogT"][h], o[:, :, :]).then_inc(stored, 16)

                load(0)
                store(0)
                with sp.Fori(1, GH) as h:
                    load(h)
                    store(h)
                sp.wait_ge(stored, 16 * STORES * GH)

            @block.scalar
            def _(act):
                ch = Chain(act, own_act)
                act.wait_ge(cleared, 4)

                def head(h):
                    act.wait_ge(z_ready, h + 1)
                    ch.link(act.activation(sp_[:, :], z[:, :], ACT.Abs))
                    ch.link(act.activation(sp_[:, :], sp_[:, :], ACT.Exp, scale=-1.0))
                    act.activation(sp_[:, :], sp_[:, :], ACT.Ln, bias=1.0).then_inc(softplus_ready, 1)
                    act.wait_ge(B_ready, h + 1)
                    act.activation(up[:, :], B[:, :], ACT.Exp, scale=1.0 / 16)
                    act.activation(dn[:, :], B[:, :], ACT.Exp, scale=-1.0 / 16)
                    act.activation(rest[:, :], rest[:, :], ACT.Exp, scale=1.0 / 16)
                    act.activation(ends[:, 0:CH], B[:, 0:SEQ].rearrange("p (j c) -> p j c", c=GC)[:, :, GC - 1],
                                   ACT.Exp, scale=1.0 / 16)
                    act.activation(ends[:, CH:CH + NB], B[:, SEQ:M].rearrange("p (j c) -> p j c", c=NT)[:, :, NT - 1],
                                   ACT.Exp, scale=1.0 / 16).then_inc(exps_ready, 1)
                    for i in range(N):
                        act.wait_ge(turned, h * N + i + 1)
                        if i >= 2:
                            act.wait_ge(o_summed, h * N + i - 1)
                            act.wait_ge(s_summed, h * US + 2 * (i - 1))
                        rows = P if i < TILES else NS
                        act.copy(kv[0:rows, i % 2, :], turn_b[0:rows, 0:3 * P]).then_inc(kv_ready, 1)
                        if i:
                            copy_o(h, i - 1)
                    copy_o(h, N - 1)
                    act.wait_ge(o_ready, h * N + N)
                    act.activation(zero[:, :], o[:, :, :].rearrange("p a m -> p (a m)"), ACT.Square).then_inc(squares_ready, 1)
                    act.wait_ge(ms_summed, h + 1)
                    ch.link(act.activation(z[:, :].rearrange("p (g c) -> p g c", g=3), zb[:, :, 0:G3], ACT.Ln, bias=eps[:, :]))
                    act.activation(z[:, :], z[:, :], ACT.Exp, scale=-0.5)
                    act.activation(zero[:, :], gate[:, :, :].rearrange("p a m -> p (a m)"), ACT.Sigmoid).then_inc(rstd_ready, 1)

                def copy_o(h, i):
                    act.wait_ge(o_summed, h * N + i + 1)
                    rows = P if i < TILES else NS
                    act.copy(o[:, :, i * P:i * P + rows],
                             o_b[:, 0:2 * rows].rearrange("p (a c) -> p a c", a=2)).then_inc(o_ready, 1)

                ch.enter(0, 3)
                head(0)
                ch.leave(1)
                with act.Fori(1, GH) as h:
                    ch.enter(h - 1, 3)
                    act.wait_ge(stored, h * 16 * STORES)
                    head(h)
                    ch.leave(GH - 1)

            @block.vector
            def _(dve):
                ch = Chain(dve, own)
                dve.memset(ones[:, :], 1.0 / GV).then_inc(cleared, 1)
                dve.memset(eps[:, :], 1e-5).then_inc(cleared, 1)
                dve.memset(kv[:, :, :], 0.0).then_inc(cleared, 1)
                dve.memset(zero[:, :], 0.0).then_inc(cleared, 1)
                dve.wait_ge(consts_in, 16 * 6)
                PER = 6

                def head(h):
                    dve.wait_ge(head_in, (h + 1) * 16 * LOADS)
                    dve.wait_ge(z_summed, h + 1)
                    zv = z[:, :].rearrange("p (g c) -> p g c", g=3)
                    ch.link(dve.tensor_scalar(zv, zb[:, :, 0:G3], cst[:, 0:1], None, ALU.add))
                    dve.sem_inc(z_ready, 1)
                    dve.wait_ge(softplus_ready, h + 1)
                    ch.link(dve.scalar_tensor_tensor(out=sp_[:, :], in0=z[:, :], scalar=0.0, in1=sp_[:, :],
                                                     op0=ALU.min, op1=ALU.subtract))
                    ch.link(dve.tensor_tensor_scan(B[:, :], starts[:, :], sp_[:, :], 0.0, ALU.mult, ALU.add))
                    for c0, c1, c in ((0, SEQ, GC), (SEQ, M, NT)):
                        Bc = B[:, c0:c1].rearrange("p (j c) -> p j c", c=c)
                        last = dve.tensor_tensor(rest[:, c0:c1].rearrange("p (j c) -> p j c", c=c),
                                                 Bc[:, :, c - 1:c].broadcast_to([P, (c1 - c0) // c, c]), Bc, ALU.subtract)
                    ch.link(last)
                    dve.sem_inc(B_ready, 1)
                    dve.wait_ge(exps_ready, h + 1)
                    dve.scalar_tensor_tensor(out=qe[:, :], in0=qkv[:, 0, :], scalar=float(P) ** -0.5, in1=up[:, :],
                                             op0=ALU.mult, op1=ALU.mult).then_inc(scaled, 1)
                    dve.tensor_tensor(ke[:, :], qkv[:, 1, :], dn[:, :], ALU.mult).then_inc(scaled, 1)
                    dve.tensor_tensor(k2[:, :], qkv[:, 1, :], rest[:, :], ALU.mult).then_inc(scaled, 1)
                    dve.memset(S[:, 0, :], 0.0).then_inc(S_ready, 1)
                    for i in range(TILES):
                        dve.wait_ge(at_summed, h * N + i + 1)
                        if i >= 2:
                            dve.wait_ge(o_summed, h * N + i - 1)
                        dve.tensor_tensor(at[:, i % 2, :], at_b[:, 0:P], mask[:, :], ALU.mult).then_inc(at_ready, 1)
                        for j in (2 * i, 2 * i + 1):
                            dve.wait_ge(s_summed, h * US + j + 1)
                            dve.wait_ge(S_ready, h * (US + 1) + j + 1)
                            if j >= 4:
                                dve.wait_ge(o_summed, h * N + (j - 4) // 2 + 1)
                            dve.scalar_tensor_tensor(out=S[:, (j + 1) % 4, :], in0=S[:, j % 4, :],
                                                     scalar=ends[:, j:j + 1], in1=s_b[j % 2][:, 0:GV],
                                                     op0=ALU.mult, op1=ALU.add).then_inc(S_ready, 1)
                    dve.wait_ge(at_summed, h * N + N)
                    dve.tensor_tensor(at[0:NS, 0, 0:NS], at_b[0:NS, 0:NS], mask_s[:, :], ALU.mult).then_inc(at_ready, 1)
                    dve.wait_ge(kv_ready, h * N + N)
                    dve.tensor_tensor(k2s[:, :, :], kv[0:NS, 0, 0:P].unsqueeze(1).broadcast_to([NS, NB, P]),
                                      seq_rows[:, :].unsqueeze(2).broadcast_to([NS, NB, P]),
                                      ALU.mult).then_inc(k2s_ready, 1)
                    for b in range(NB):
                        dve.wait_ge(s_summed, h * US + CH + b + 1)
                        dve.scalar_tensor_tensor(out=S_out[:, b, :], in0=S_in[:, b, :], scalar=ends[:, CH + b:CH + b + 1],
                                                 in1=s_b[b % 2][:, 0:GV], op0=ALU.mult, op1=ALU.add).then_inc(S_ready, 1)
                    dve.wait_ge(rstd_ready, h + 1)
                    for n in range(2):
                        last = dve.scalar_tensor_tensor(out=gate[:, n, :], in0=gate[:, n, :], scalar=cst[:, 1 + n:2 + n],
                                                        in1=z[:, :], op0=ALU.mult, op1=ALU.mult)
                    ch.link(last)
                    gv = gate[:, :, :].rearrange("p a m -> p (a m)")
                    ov = o[:, :, :].rearrange("p a m -> p (a m)")
                    ch.link(dve.tensor_tensor(ov, ov, gv, ALU.mult))
                    dve.tensor_tensor(ov, ov, zero[:, :], ALU.mult).then_inc(og_ready, 1)

                ch.enter(0, PER)
                head(0)
                ch.leave(1)
                with dve.Fori(1, GH) as h:
                    dve.wait_ge(stored, h * 16 * STORES)
                    ch.enter(h - 1, PER)
                    head(h)
                    ch.leave(GH - 1)

            @block.tensor
            def _(pe):
                pe.wait_ge(consts_in, 16 * 6)
                pe.wait_ge(cleared, 4)

                def head(h, first):
                    pe.wait_ge(head_in, (h + 1) * 16 * LOADS)
                    if not first:
                        pe.wait_ge(rstd_ready, h)
                    for g in range(3):
                        last = pe.matmul(zb[:, g, 0:G3], wz[:, :], gaT[:, g * G3:(g + 1) * G3], start=True, stop=True)
                    last.then_inc(z_summed, 1)
                    pe.wait_ge(scaled, h * 3 + 3)

                    def start(i):
                        c0, rows = i * P, P if i < TILES else NS
                        if not first or i:
                            pe.wait_ge(kv_ready, h * N + i)
                            pe.wait_ge(at_ready, h * N + i)
                        for n, src in enumerate((k2[:, c0:c0 + rows], qkv[:, 2, c0:c0 + rows], qkv[:, 3, c0:c0 + rows])):
                            last = pe.transpose(turn_b[0:rows, n * P:(n + 1) * P], src, ident[:, :])
                        last.then_inc(turned, 1)
                        pe.matmul(at_b[0:rows, 0:rows], ke[:, c0:c0 + rows], qe[:, c0:c0 + rows],
                                  start=True, stop=True).then_inc(at_summed, 1)

                    def state(j, lhsT, rhs, k):
                        if not first or k >= 2:
                            done = h * (US + 1) + k if k >= 2 else h * (US + 1) - 2 + k + 1
                            pe.wait_ge(S_ready, done)
                        pe.matmul(s_b[k % 2][:, 0:GV], lhsT, rhs, start=True, stop=True).then_inc(s_summed, 1)

                    def finish(i):
                        pe.wait_ge(kv_ready, h * N + i + 1)
                        a = kv[:, i % 2, :]
                        if i < TILES:
                            for n in range(2):
                                state(n, a[64 * n:64 * n + 64, 0:P], a[64 * n:64 * n + 64, P:3 * P], 2 * i + n)
                        pe.wait_ge(at_ready, h * N + i + 1)
                        if not first or i:
                            pe.wait_ge(o_ready, h * N + i)
                        rows, c0 = (P, i * P) if i < TILES else (NS, SEQ)
                        for n in range(2):
                            pe.matmul(o_b[:, n * rows:(n + 1) * rows], a[0:rows, (1 + n) * P:(2 + n) * P],
                                      at[0:rows, i % 2, 0:rows], start=(n == 0), stop=False, skip_group_check=True)
                        if i < TILES:
                            for j in (2 * i, 2 * i + 1):
                                pe.wait_ge(S_ready, h * (US + 1) + j + 1)
                                for n in range(2):
                                    c = (j % 2) * GC
                                    last = pe.matmul(o_b[:, n * rows + c:n * rows + c + GC], S[:, j % 4, n * P:(n + 1) * P],
                                                     qe[:, j * GC:(j + 1) * GC], start=False, stop=True,
                                                     skip_group_check=True)
                        else:
                            for b in range(NB):
                                for n in range(2):
                                    last = pe.matmul(o_b[:, n * rows + b * NT:n * rows + (b + 1) * NT],
                                                     S_in[:, b, n * P:(n + 1) * P], qe[:, c0 + b * NT:c0 + (b + 1) * NT],
                                                     start=False, stop=True, skip_group_check=True)
                        last.then_inc(o_summed, 1)
                        if i == TILES:
                            pe.wait_ge(k2s_ready, h + 1)
                            for b in range(NB):
                                state(b, k2s[:, b, :], a[0:NS, P:3 * P], CH + b)

                    start(0)
                    for i in range(N):
                        if i + 1 < N:
                            start(i + 1)
                        finish(i)
                    pe.wait_ge(squares_ready, h + 1)
                    for g in range(3):
                        for n in range(2):
                            last = pe.matmul(zb[:, g, 0:G3], ones[:, :], zero[:, n * M + g * G3:n * M + (g + 1) * G3],
                                             start=(n == 0), stop=(n == 1))
                    last.then_inc(ms_summed, 1)

                head(0, True)
                with pe.Fori(1, GH) as h:
                    head(h, False)


RC, RH = 64, 64
PAIRS = 8
RW0 = 24
CHUNKS = SEQ // RC + 1
MW = CHUNKS * RC
QUADS = ((0, 4), (4, 4), (8, 4), (12, 4), (16, 1))
LEVELS = 5
DECAY = -float(np.exp(-0.5))


def rw_levels(q):
    return LEVELS if q < 4 else 1


def rw_schedule():
    def free(q):
        yield ("gen", q, 0)
        for r in range(3):
            yield ("turn", q, r)
        for l in range(rw_levels(q)):
            yield ("P", q, l)
            yield ("T", q, l)

    def sequential(q):
        c0, n = QUADS[q]
        for c in range(c0, c0 + n):
            for kind in "XUS":
                yield (kind, q, c)

    steps = list(free(0))
    for q in range(len(QUADS)):
        a, b = list(sequential(q)), list(free(q + 1)) if q + 1 < len(QUADS) else []
        while a or b:
            if b:
                steps.append(b.pop(0))
            if a:
                steps.append(a.pop(0))
    return steps


def rwkv(nc, t):
    with ExitStack() as ctx:
        s = Stage(nc, ctx, "rw")
        ident = s.sb("ident", [P, P])
        strict = s.sb("strict", [P, 2, P])
        incl = s.sb("incl", [P, 2, RC])
        first_l = s.sb("first_l", [P, P])
        first_u = s.sb("first_u", [P, P])
        join = s.sb("join", [P, LEVELS, P])
        seq_cols = s.sb("seq_cols", [P, NB, P])
        seq_rows = s.sb("seq_rows", [P, NB])
        starts = s.sb("starts", [P, MW])
        heads = s.sb("heads", [P, P])
        mean = s.sb("mean", [P, P])
        cst_all = s.sb("cst_all", [P, PAIRS, 10])
        cst = s.sb("cst", [P, 11])
        mu_wg, sh_wg = s.sb("mu_wg", [P, 2]), s.sb("sh_wg", [P, 2, NB])
        raw = s.sb("raw", [P, 3, M])
        sh = s.sb("sh", [P, 3, NB])
        sho = s.sb("sho", [P, 3, NSEQ])
        wa = s.sb("wa", [P, M])
        gl = s.sb("gl", [P, M])
        w2a2, g2 = s.sb("w2a2", [P, P]), s.sb("g2", [P, P])
        rkv = s.sb("rkv", [P, 3, MW])
        d = s.sb("d", [P, M])
        sg, av, gt = s.sb("sg", [P, MW]), s.sb("av", [P, M]), s.sb("gt", [P, M])
        Ls, Lp = s.sb("Ls", [P, MW]), s.sb("Lp", [P, MW])
        Ei, Ed = s.sb("Ei", [P, MW]), s.sb("Ed", [P, MW])
        ends = s.sb("ends", [P, SEQ // RC + NB])
        kk, rn = s.sb("kk", [P, MW]), s.sb("rn", [P, M])
        km = s.sb("km", [P, M])
        bv = s.sb("bv", [P, M])
        ar = s.sb("ar", [P, 2, MW])
        aB, bB, kB, vB = (s.sb(n, [P, CHUNKS, P]) for n in ("aB", "bB", "kB", "vB"))
        abT = s.sb("abT", [P, 4, P])
        akT = s.sb("akT", [P, 2, 4, P])
        rbT, rkT = s.sb("rbT", [P, 2, 4, RC]), s.sb("rkT", [P, 2, 4, RC])
        nat = s.sb("nat", [P, 2, 3, 4, P])
        Tf = s.sb("Tf", [P, 2, 4, P])
        T, TT, Pm = s.sb("T", [P, 4, P]), s.sb("TT", [P, 4, P]), s.sb("Pm", [P, 4, P])
        An = s.sb("An", [P, LEVELS, 4, P])
        Xs, Us = s.sb("Xs", [P, P]), s.sb("Us", [P, P])
        S, Su = s.sb("S", [P, 2, P]), s.sb("Su", [P, P])
        S_in, S_out = s.sb("S_in", [P, NB, P]), s.sb("S_out", [P, NB, P])
        a_seq = s.sb("a_seq", [P, NB, P])
        bk_seq = s.sb("bk_seq", [P, 2, NB, P])
        oT = Ls
        eps = s.sb("eps", [P, 2])
        zb = s.ps("zb", [P, 3, 512])
        turn_b, x_b, u_b, s_b, o_b = (s.ps(n) for n in ("turn_b", "x_b", "u_b", "s_b", "o_b"))

        NAMES = ("consts_in pair_in states_in cleared sho_ready lerped sg_ready av_ready gt_ready exps_ready "
                 "squares rn_ready vB_ready aB_ready kk_ready L_ready ss_ready km_ready scaled ar_ready bv_ready "
                 "w_summed gen_summed gen_ready abT_ready joins_ready turned nat_ready p_summed p_ready t_summed "
                 "T_ready x_summed x_ready u_summed u_ready s_summed S_ready o_summed o_ready a_seq_ready "
                 "bk_seq_ready d_ready rstd_ready out_ready shift_stored stored own own_act own_pool wa_ready "
                 "norm_summed").split()
        sem = {n: s.sem(n) for n in NAMES}
        (consts_in, pair_in, states_in, cleared, sho_ready, lerped, sg_ready, av_ready, gt_ready, exps_ready,
         squares, rn_ready, vB_ready, aB_ready, kk_ready, L_ready, ss_ready, km_ready, scaled, ar_ready, bv_ready,
         w_summed, gen_summed, gen_ready, abT_ready, joins_ready, turned, nat_ready, p_summed, p_ready, t_summed,
         T_ready, x_summed, x_ready, u_summed, u_ready, s_summed, S_ready, o_summed, o_ready, a_seq_ready,
         bk_seq_ready, d_ready, rstd_ready, out_ready, shift_stored, stored, own, own_act, own_pool, wa_ready,
         norm_summed) = (sem[n] for n in NAMES)

        steps = rw_schedule()
        NQ, C = len(QUADS), CHUNKS
        NP = sum(rw_levels(q) for q in range(NQ))
        NTR = NP + NQ
        NSR = 1 + (C - 1) + NB
        ZS = 5
        CONSTS = 15

        def p_at(q, l):
            return 5 * q + l + 1

        def T_at(q, l):
            return 6 * q + l + 2

        def lv(buf, q, n):
            return buf[:, 0:n, :]

        with nc.Block() as block:
            @block.sync
            def _(sp):
                for dst, name in ((ident, "ident"), (strict, "rw_strict"), (incl, "rw_incl"), (first_l, "rw_first_l"),
                                  (first_u, "rw_first_u"), (join, "rw_join"), (seq_cols, "rw_seq_cols"),
                                  (seq_rows, "rw_seq_rows"), (starts, "starts"), (heads, "rw_heads"), (mean, "rw_mean"),
                                  (cst_all, "rw_cst"), (mu_wg, "rw_mu_wg"), (sh_wg, "rw_sh_wg")):
                    src = t[name]
                    if name == "starts":
                        src = src.broadcast_to([P, MW])
                    if len(src.shape) == 3:
                        sp.dma_start(dst[:, :, :], src).then_inc(consts_in, 16)
                    else:
                        sp.dma_start(dst[:, :], src).then_inc(consts_in, 16)
                sp.dma_start(raw[:, 0:2, :], t["pT"][RW0 + 24:RW0 + 26].rearrange("n p m -> p n m")).then_inc(consts_in, 16)
                sp.wait_ge(sho_ready, 1)
                sp.dma_start(t["new_shift_wg"].rearrange("n p b -> p n b"), sho[:, 0:2, :]).then_inc(shift_stored, 16)
                sp.wait_ge(wa_ready, 1)
                sp.wait_ge(cleared, 12)

                def load(j):
                    for n in range(3):
                        sp.dma_start(raw[:, n, :], t["pT"][j + (RW0 + 8 * n)]).then_inc(pair_in, 16)
                    sp.dma_start(sh[:, :, :], t["rw_sh"][j]).then_inc(pair_in, 16)
                    sp.dma_start(w2a2[:, :], t["w2a2"][j]).then_inc(pair_in, 16)
                    sp.dma_start(g2[:, :], t["g2"][j]).then_inc(pair_in, 16)

                def load_states(j):
                    for n in range(2):
                        sp.dma_start(S_in[64 * n:64 * n + 64, :, 64 * n:64 * n + 64],
                                     t["state_rwkv"][j][n]).then_inc(states_in, 16)

                def middle(j):
                    sp.wait_ge(sho_ready, j + 2)
                    sp.dma_start(t["new_shift"][j].rearrange("n p b -> p n b"), sho[:, :, :]).then_inc(shift_stored, 16)

                def store(j):
                    sp.wait_ge(S_ready, (j + 1) * NSR)
                    for n in range(2):
                        a, b = 64 * n, 64 * n + 64
                        sp.dma_start(t["new_rw_p"][j][n], S[a:b, 0, a:b]).then_inc(stored, 16)
                        sp.dma_start(t["new_rw_s"][j][n], S_out[a:b, :, a:b]).then_inc(stored, 16)
                    sp.wait_ge(out_ready, j + 1)
                    sp.dma_start(t["orT"][j], d[:, :]).then_inc(stored, 16)

                load(0)
                load_states(0)
                middle(0)
                with sp.Fori(1, PAIRS) as j:
                    sp.wait_ge(bv_ready, j)
                    sp.wait_ge(gt_ready, j)
                    load(j)
                    store(j - 1)
                    load_states(j)
                    middle(j)
                store(PAIRS - 1)
                sp.wait_ge(shift_stored, 16 * (PAIRS + 1))
                sp.wait_ge(stored, 16 * 5 * PAIRS)

            def samples(ap, last):
                return ap[:, SEQ:M].rearrange("p (b c) -> p b c", c=NT)

            @block.scalar
            def _(act):
                ch = Chain(act, own_act)
                act.wait_ge(consts_in, 16 * CONSTS)
                act.copy(sho[:, 0:2, :], raw[:, 0:2, SEQ - 1:M:NT]).then_inc(sho_ready, 1)
                act.wait_ge(wa_ready, 1)
                act.activation(wa[0:64, :], wa[0:64, :], ACT.Tanh).then_inc(own_act, 1)
                act.activation(gl[:, :], gl[:, :], ACT.Sigmoid).then_inc(own_act, 1)

                def pair(j, first):
                    act.wait_ge(pair_in, (j + 1) * 16 * 6)
                    act.wait_ge(shift_stored, (j + 1) * 16)
                    act.copy(sho[:, :, :], raw[:, :, SEQ - 1:M:NT]).then_inc(sho_ready, 1)
                    act.wait_ge(lerped, (j + 1) * 3)
                    for n in range(2):
                        a = 64 * n
                        act.copy(vB[a:a + 64, :, a:a + 64],
                                 rkv[a:a + 64, 2, :].rearrange("p (c s) -> p c s", s=RC)).then_inc(vB_ready, 1)
                    act.wait_ge(w_summed, j * ZS + 1)
                    act.activation(sg[:, 0:M].rearrange("p (g c) -> p g c", g=3), zb[:, :, 0:G3], ACT.Sigmoid,
                                   bias=cst[:, 3:4]).then_inc(sg_ready, 1)
                    act.wait_ge(w_summed, j * ZS + 2)
                    act.activation(av[:, :].rearrange("p (g c) -> p g c", g=3), zb[:, :, 0:G3], ACT.Sigmoid,
                                   bias=cst[:, 4:5]).then_inc(av_ready, 1)
                    act.wait_ge(w_summed, j * ZS + 3)
                    act.copy(gt[:, :].rearrange("p (g c) -> p g c", g=3), zb[:, :, 0:G3]).then_inc(gt_ready, 1)
                    act.wait_ge(kk_ready, j + 1)
                    act.activation(rn[:, :], kk[:, 0:M], ACT.Square).then_inc(squares, 1)
                    act.wait_ge(L_ready, j + 1)
                    act.activation(Ei[:, :], Ls[:, :], ACT.Exp, scale=DECAY)
                    act.activation(Ed[:, :], Ls[:, :], ACT.Exp, scale=-DECAY)
                    act.activation(Lp[:, :], Lp[:, :], ACT.Exp, scale=DECAY)
                    act.activation(ends[:, 0:C - 1], Ls[:, RC - 1:SEQ:RC], ACT.Exp, scale=DECAY)
                    act.activation(ends[:, C - 1:C - 1 + NB], Ls[:, SEQ + NT - 1:M:NT], ACT.Exp,
                                   scale=DECAY).then_inc(exps_ready, 1)
                    act.wait_ge(ss_ready, j + 1)
                    ch.link(act.activation(rn[:, :], rn[:, :], ACT.Ln, scale=2.0 ** 32))
                    act.activation(rn[:, :], rn[:, :], ACT.Exp, scale=-0.5, bias=eps[:, 1:2]).then_inc(rn_ready, 1)
                    act.wait_ge(ar_ready, j + 1)
                    for n in range(2):
                        a = 64 * n
                        act.copy(aB[a:a + 64, :, a:a + 64],
                                 ar[a:a + 64, 0, :].rearrange("p (c s) -> p c s", s=RC)).then_inc(aB_ready, 1)
                    for kind, q, c in steps:
                        n = QUADS[q][1]
                        if kind == "turn":
                            act.wait_ge(turned, j * 3 * NQ + 3 * q + c + 1)
                            if q >= 2 and c == 0:
                                act.wait_ge(o_summed, j * C + 4 * (q - 1))
                            act.copy(nat[:, q % 2, c, 0:n, :],
                                     turn_b[:, 0:n * P].rearrange("p (i s) -> p i s", i=n)).then_inc(nat_ready, 1)
                        elif kind == "P":
                            act.wait_ge(p_summed, j * NP + p_at(q, c))
                            act.copy(lv(Pm, q, n), zb[:, 0, 0:n * P].rearrange("p (i s) -> p i s", i=n)).then_inc(p_ready, 1)
                        elif kind == "X":
                            act.wait_ge(x_summed, j * C + c + 1)
                            act.copy(Xs[:, :], x_b[:, 0:P]).then_inc(x_ready, 1)
                        elif kind == "S" and (c % 8 == 7 or c == C - 1):
                            act.wait_ge(o_summed, j * C + c + 1)
                            c0 = c // 8 * 8
                            act.copy(oT[:, c0 * RC:(c + 1) * RC], o_b[:, 0:(c + 1 - c0) * RC]).then_inc(o_ready, 1)
                    act.wait_ge(d_ready, j + 1)
                    act.activation(rn[:, :], d[:, :], ACT.Square).then_inc(squares, 1)
                    act.wait_ge(norm_summed, 2 * j + 2)
                    ch.link(act.activation(rn[:, :].rearrange("p (g c) -> p g c", g=3), zb[:, :, 0:G3], ACT.Ln,
                                           bias=eps[:, 0:1]))
                    act.activation(rn[:, :], rn[:, :], ACT.Exp, scale=-0.5).then_inc(rstd_ready, 1)

                ch.n = 2
                ch.enter(0, 2)
                pair(0, True)
                ch.leave(1)
                with act.Fori(1, PAIRS) as j:
                    ch.enter(j - 1, 2)
                    pair(j, False)
                    ch.leave(PAIRS - 1)

            @block.vector
            def _(dve):
                ch = Chain(dve, own)
                for buf in (aB, bB, kB, vB, S_in):
                    dve.memset(buf[:, :, :], 0.0).then_inc(cleared, 1)
                for buf in (rkv[:, 0, M:MW], rkv[:, 1, M:MW], rkv[:, 2, M:MW], sg[:, M:MW], kk[:, M:MW]):
                    dve.memset(buf, 0.0).then_inc(cleared, 1)
                dve.memset(eps[:, 0:1], 64e-5).then_inc(cleared, 1)
                dve.memset(eps[:, 1:2], 16.0 * float(np.log(2.0))).then_inc(cleared, 1)
                dve.wait_ge(consts_in, 16 * CONSTS)
                dve.wait_ge(cleared, 12)

                def lerp(out, x, shift, mu):
                    dve.tensor_tensor(d[:, 1:SEQ], x[:, 0:SEQ - 1], x[:, 1:SEQ], ALU.subtract)
                    dve.tensor_scalar(d[:, 0:1], x[:, 0:1], -1.0, None, ALU.mult)
                    xs, ds = samples(x, 0), samples(d, 0)
                    dve.tensor_tensor(ds[:, :, 1:NT], xs[:, :, 0:NT - 1], xs[:, :, 1:NT], ALU.subtract)
                    ch.link(dve.tensor_tensor(ds[:, :, 0], shift, xs[:, :, 0], ALU.subtract))
                    return dve.scalar_tensor_tensor(out=out, in0=d[:, :], scalar=mu, in1=x, op0=ALU.mult, op1=ALU.add)

                ch.link(lerp(wa[:, :], raw[:, 0, :], sh_wg[:, 0, :], mu_wg[:, 0:1]))
                ch.link(lerp(gl[:, :], raw[:, 1, :], sh_wg[:, 1, :], mu_wg[:, 1:2]))
                dve.wait_ge(sho_ready, 1)
                dve.sem_inc(wa_ready, 1)

                def halves(out, x, y):
                    for n in range(2):
                        a = 64 * n
                        last = dve.tensor_tensor(out[a:a + 64, :, a:a + 64],
                                                 x[a:a + 64, :].rearrange("p (c s) -> p c s", s=RC),
                                                 y[a:a + 64, :].rearrange("p (c s) -> p c s", s=RC), ALU.mult)
                    return last

                def pair(j, first):
                    g3 = lambda x: x.rearrange("p (g c) -> p g c", g=3)
                    ch.link(dve.tensor_copy(cst[:, 0:10], cst_all[:, 0 if first else j, :] if first else
                                            cst_all[:, bass.ds(j, 1), :].rearrange("p o c -> p (o c)")))
                    ch.link(dve.tensor_scalar(cst[:, 10:11], cst[:, 6:7], -1.0, 1.0, ALU.mult, ALU.add))
                    dve.wait_ge(pair_in, (j + 1) * 16 * 6)
                    if not first:
                        dve.wait_ge(stored, j * 16 * 5)
                    for n in range(3):
                        ch.link(lerp(rkv[:, n, 0:M], raw[:, n, :], sh[:, n, :], cst[:, n:n + 1]))
                        dve.sem_inc(lerped, 1)
                    R, K, V = rkv[:, 0, :], rkv[:, 1, :], rkv[:, 2, :]
                    dve.tensor_scalar(kk[:, 0:M], K[:, 0:M], cst[:, 5:6], None, ALU.mult).then_inc(kk_ready, 1)
                    dve.wait_ge(sg_ready, j + 1)
                    ch.link(dve.tensor_tensor_scan(Ls[:, :], starts[:, :], sg[:, :], 0.0, ALU.mult, ALU.add))
                    dve.tensor_tensor(Lp[:, :], Ls[:, :], sg[:, :], ALU.subtract).then_inc(L_ready, 1)
                    dve.wait_ge(av_ready, j + 1)
                    ch.link(dve.tensor_scalar(km[:, :], av[:, :], cst[:, 6:7], cst[:, 10:11], ALU.mult, ALU.add))
                    ch.link(dve.tensor_tensor(K[:, 0:M], K[:, 0:M], km[:, :], ALU.mult))
                    dve.scalar_tensor_tensor(out=km[:, :], in0=R[:, 0:M], scalar=cst[:, 7:8], in1=K[:, 0:M],
                                             op0=ALU.mult, op1=ALU.mult).then_inc(km_ready, 1)
                    dve.wait_ge(exps_ready, j + 1)
                    dve.tensor_tensor(ar[:, 1, :], R, Ei[:, :], ALU.mult).then_inc(scaled, 1)
                    halves(kB, K, Ed).then_inc(scaled, 1)
                    dve.wait_ge(w_summed, j * ZS + 4)
                    dve.tensor_scalar(g3(rn[:, :]), zb[:, :, 0:G3], 1e-24, None, ALU.max).then_inc(ss_ready, 1)
                    dve.wait_ge(rn_ready, j + 1)
                    ch.link(dve.tensor_tensor(kk[:, 0:M], kk[:, 0:M], rn[:, :], ALU.mult))
                    dve.scalar_tensor_tensor(out=ar[:, 0, :], in0=kk[:, :], scalar=-1.0, in1=Lp[:, :],
                                             op0=ALU.mult, op1=ALU.mult).then_inc(ar_ready, 1)
                    dve.wait_ge(ar_ready, j + 1)
                    ch.link(dve.tensor_tensor(kk[:, 0:M], kk[:, 0:M], av[:, :], ALU.mult))
                    halves(bB, kk, Ed).then_inc(scaled, 1)
                    dve.wait_ge(w_summed, j * ZS + 5)
                    dve.tensor_tensor(g3(bv[:, :]), g3(V[:, 0:M]), zb[:, :, 0:G3], ALU.mult).then_inc(bv_ready, 1)
                    dve.memset(S[:, 0, :], 0.0).then_inc(S_ready, 1)
                    for kind, q, c in steps:
                        n = QUADS[q][1]
                        smp = q == NQ - 1
                        b4 = lambda ap: ap.rearrange("p (i s) -> p i s", i=n)
                        if kind == "gen":
                            dve.wait_ge(gen_summed, j * NQ + q + 1)
                            if q >= 2:
                                dve.wait_ge(o_summed, j * C + 4 * (q - 1))
                            if q or not first:
                                dve.wait_ge(joins_ready, j * NQ + q)
                            for bank, big, small in ((0, abT[:, 0:n, :], rbT), (1, akT[:, q % 2, 0:n, :], rkT)):
                                src = zb[:, bank, 0:n * P].rearrange("p (i a s) -> p i a s", i=n, a=2)
                                if n > 1:
                                    for h2 in range(2):
                                        last = dve.tensor_tensor(big[:, :, h2 * RC:(h2 + 1) * RC], src[:, :, 0, :],
                                                                 strict[:, 0, h2 * RC:(h2 + 1) * RC].unsqueeze(1).broadcast_to([P, n, RC]),
                                                                 ALU.mult)
                                    last2 = dve.tensor_tensor(small[:, q % 2, 0:n, :], src[:, :, 1, :],
                                                              incl[:, 0, :].unsqueeze(1).broadcast_to([P, n, RC]), ALU.mult)
                                else:
                                    for h2 in range(2):
                                        last = dve.tensor_tensor(big[:, 0, h2 * RC:(h2 + 1) * RC], src[:, 0, 0, :],
                                                                 strict[:, 1, h2 * RC:(h2 + 1) * RC], ALU.mult)
                                    last2 = dve.tensor_tensor(small[:, q % 2, 0, :], src[:, 0, 1, :], incl[:, 1, :], ALU.mult)
                                if bank == 0:
                                    ch.link(last)
                                    dve.sem_inc(abT_ready, 1)
                            one = ident[:, :].unsqueeze(1).broadcast_to([P, n, P])
                            dve.tensor_tensor(T[:, 0:n, :], b4(zb[:, 2, 0:n * P]),
                                              first_l[:, :].unsqueeze(1).broadcast_to([P, n, P]), ALU.mult)
                            ch.link(dve.tensor_tensor(TT[:, 0:n, :], abT[:, 0:n, :],
                                                      first_u[:, :].unsqueeze(1).broadcast_to([P, n, P]), ALU.mult))
                            dve.sem_inc(gen_ready, 1)
                            dve.tensor_tensor(T[:, 0:n, :], T[:, 0:n, :], one, ALU.add)
                            dve.tensor_tensor(TT[:, 0:n, :], TT[:, 0:n, :], one, ALU.add).then_inc(T_ready, 1)
                        elif kind == "T":
                            dve.wait_ge(t_summed, j * NP + p_at(q, c))
                            if c + 1 < rw_levels(q):
                                dve.tensor_tensor(T[:, 0:n, :], T[:, 0:n, :], b4(zb[:, 1, 0:n * P]), ALU.add)
                                dve.tensor_tensor(TT[:, 0:n, :], TT[:, 0:n, :], b4(zb[:, 2, 0:n * P]),
                                                  ALU.add).then_inc(T_ready, 1)
                            else:
                                dve.tensor_tensor(Tf[:, q % 2, 0:n, :], TT[:, 0:n, :], b4(zb[:, 2, 0:n * P]),
                                                  ALU.add).then_inc(T_ready, 1)
                        elif kind == "U":
                            dve.wait_ge(u_summed, j * C + c + 1)
                            dve.tensor_copy(Us[:, :], u_b[:, 0:P]).then_inc(u_ready, 1)
                        elif kind == "S" and not smp:
                            dve.wait_ge(s_summed, j * (C - 1 + NB) + c + 1)
                            ch.link(dve.tensor_tensor(Su[:, :], S[:, c % 2, :], s_b[:, 0:P], ALU.add))
                            dve.tensor_scalar(S[:, (c + 1) % 2, :], Su[:, :], ends[:, c:c + 1], None,
                                              ALU.mult).then_inc(S_ready, 1)
                        elif kind == "S":
                            for b in range(NB):
                                dve.wait_ge(s_summed, j * (C - 1 + NB) + c + b + 1)
                                ch.link(dve.tensor_tensor(Su[:, :], S_in[:, b, :], s_b[:, 0:P], ALU.add))
                                dve.tensor_scalar(S_out[:, b, :], Su[:, :], ends[:, C - 1 + b:C + b], None,
                                                  ALU.mult).then_inc(S_ready, 1)
                    dve.wait_ge(norm_summed, 2 * j + 1)
                    dve.tensor_tensor(g3(d[:, :]), g3(oT[:, 0:M]), zb[:, :, 0:G3], ALU.subtract).then_inc(d_ready, 1)
                    dve.wait_ge(rstd_ready, j + 1)
                    ch.link(dve.tensor_tensor(d[:, :], d[:, :], rn[:, :], ALU.mult))
                    ch.link(dve.tensor_scalar(d[:, :], d[:, :], cst[:, 8:9], cst[:, 9:10], ALU.mult, ALU.add))
                    ch.link(dve.tensor_tensor(d[:, :], d[:, :], bv[:, :], ALU.add))
                    dve.tensor_tensor(d[:, :], d[:, :], gt[:, :], ALU.mult).then_inc(out_ready, 1)

                PER = 50
                ch.enter(0, PER)
                pair(0, True)
                ch.leave(1)
                with dve.Fori(1, PAIRS) as j:
                    ch.enter(j - 1, PER)
                    pair(j, False)
                    ch.leave(PAIRS - 1)

            @block.gpsimd
            def _(pool):
                pool.wait_ge(consts_in, 16 * CONSTS)

                def pair(j, first):
                    for kind, q, c in steps:
                        n = QUADS[q][1]
                        if kind == "gen":
                            pool.wait_ge(abT_ready, j * NQ + q + 1)
                            if q or not first:
                                pool.wait_ge(p_summed, j * NP + 5 * q)
                            for l in range(rw_levels(q)):
                                last = pool.tensor_tensor(An[:, l, 0:n, :], abT[:, 0:n, :],
                                                          join[:, l, :].unsqueeze(1).broadcast_to([P, n, P]), ALU.mult)
                            last.then_inc(joins_ready, 1)
                    pool.wait_ge(aB_ready, 2 * (j + 1))
                    if not first:
                        pool.wait_ge(s_summed, j * (C - 1 + NB))
                    pool.tensor_tensor(a_seq[:, :, :], aB[:, C - 1, :].unsqueeze(1).broadcast_to([P, NB, P]),
                                       seq_cols[:, :, :], ALU.mult).then_inc(a_seq_ready, 1)
                    pool.wait_ge(nat_ready, (j + 1) * 3 * NQ)
                    for n in range(2):
                        last = pool.tensor_tensor(bk_seq[:, n, :, :],
                                                  nat[:, (NQ - 1) % 2, n, 0, :].unsqueeze(1).broadcast_to([P, NB, P]),
                                                  seq_rows[:, :].unsqueeze(2).broadcast_to([P, NB, P]), ALU.mult)
                    last.then_inc(bk_seq_ready, 1)

                pair(0, True)
                with pool.Fori(1, PAIRS) as j:
                    pair(j, False)

            @block.tensor
            def _(pe):
                pe.wait_ge(consts_in, 16 * CONSTS)
                pe.wait_ge(cleared, 12)
                pe.wait_ge(own_act, 2)

                def sum3(lhsT, rhs, sem):
                    for g in range(3):
                        last = pe.matmul(zb[:, g, 0:G3], lhsT, rhs[:, g * G3:(g + 1) * G3], start=True, stop=True)
                    last.then_inc(sem, 1)

                def pair(j, first):
                    pe.wait_ge(pair_in, (j + 1) * 16 * 6)
                    if not first:
                        pe.wait_ge(rstd_ready, j)
                    sum3(w2a2[0:64, :], wa[0:64, :], w_summed)
                    pe.wait_ge(sg_ready, j + 1)
                    sum3(w2a2[64:128, :], wa[64:128, :], w_summed)
                    pe.wait_ge(av_ready, j + 1)
                    sum3(g2[:, :], gl[:, :], w_summed)
                    pe.wait_ge(gt_ready, j + 1)
                    pe.wait_ge(squares, 2 * j + 1)
                    sum3(heads[:, :], rn[:, :], w_summed)
                    pe.wait_ge(ss_ready, j + 1)
                    pe.wait_ge(km_ready, j + 1)
                    sum3(heads[:, :], km[:, :], w_summed)
                    pe.wait_ge(bv_ready, j + 1)
                    pe.wait_ge(scaled, 3 * (j + 1))
                    pe.wait_ge(aB_ready, 2 * (j + 1))
                    pe.wait_ge(vB_ready, 2 * (j + 1))
                    for kind, q, c in steps:
                        c0, n = QUADS[q]
                        if kind == "gen":
                            if q:
                                pe.wait_ge(p_ready, j * NP + 5 * q)
                                pe.wait_ge(T_ready, j * NTR + 6 * q)
                            for i in range(n):
                                cols = slice((c0 + i) * RC, (c0 + i + 1) * RC)
                                dst = slice(i * P, (i + 1) * P)
                                pe.matmul(zb[:, 0, dst], bB[:, c0 + i, :], ar[:, :, cols], start=True, stop=True)
                                pe.matmul(zb[:, 1, dst], kB[:, c0 + i, :], ar[:, :, cols], start=True, stop=True)
                                last = pe.matmul(zb[:, 2, dst], aB[:, c0 + i, :], bB[:, c0 + i, :], start=True, stop=True)
                            last.then_inc(gen_summed, 1)
                        elif kind == "turn":
                            if q or c or not first:
                                pe.wait_ge(nat_ready, j * 3 * NQ + 3 * q + c)
                            for i in range(n):
                                last = pe.transpose(turn_b[:, i * P:(i + 1) * P], (bB, kB, vB)[c][:, c0 + i, :], ident[:, :])
                            last.then_inc(turned, 1)
                        elif kind == "P":
                            pe.wait_ge(gen_ready, j * NQ + q + 1)
                            pe.wait_ge(joins_ready, j * NQ + q + 1)
                            pe.wait_ge(T_ready, j * NTR + T_at(q, c - 1))
                            for i in range(n):
                                last = pe.matmul(zb[:, 0, i * P:(i + 1) * P], An[:, c, i, :], T[:, i, :], start=True, stop=True)
                            last.then_inc(p_summed, 1)
                        elif kind == "T":
                            pe.wait_ge(p_ready, j * NP + p_at(q, c))
                            for i in range(n):
                                if c + 1 < rw_levels(q):
                                    pe.matmul(zb[:, 1, i * P:(i + 1) * P], TT[:, i, :], Pm[:, i, :], start=True, stop=True)
                                last = pe.matmul(zb[:, 2, i * P:(i + 1) * P], Pm[:, i, :], TT[:, i, :], start=True, stop=True)
                            last.then_inc(t_summed, 1)
                        elif kind == "X":
                            i, b2 = c - c0, q % 2
                            pe.wait_ge(T_ready, j * NTR + T_at(q, rw_levels(q) - 1))
                            pe.wait_ge(nat_ready, j * 3 * NQ + 3 * q + 3)
                            if c or not first:
                                pe.wait_ge(x_ready, j * C + c)
                            if c < C - 1:
                                pe.wait_ge(S_ready, j * NSR + c + 1)
                                pe.matmul(x_b[:, 0:P], aB[:, c, :], S[:, c % 2, :], start=True, stop=False)
                            else:
                                pe.wait_ge(states_in, (j + 1) * 32)
                                pe.wait_ge(a_seq_ready, j + 1)
                                for b in range(NB):
                                    pe.matmul(x_b[:, 0:P], a_seq[:, b, :], S_in[:, b, :], start=(b == 0), stop=False)
                            pe.matmul(x_b[:, 0:P], akT[:, b2, i, :], nat[:, b2, 2, i, :], start=False,
                                      stop=True).then_inc(x_summed, 1)
                        elif kind == "U":
                            pe.wait_ge(x_ready, j * C + c + 1)
                            if c or not first:
                                pe.wait_ge(u_ready, j * C + c)
                            pe.matmul(u_b[:, 0:P], Tf[:, q % 2, c - c0, :], Xs[:, :], start=True, stop=True).then_inc(u_summed, 1)
                        elif kind == "S":
                            i, b2, o0 = c - c0, q % 2, (c % 8) * RC
                            pe.wait_ge(u_ready, j * C + c + 1)
                            if c < C - 1:
                                pe.matmul(s_b[:, 0:P], nat[:, b2, 0, i, :], Us[:, :], start=True, stop=False)
                                pe.matmul(s_b[:, 0:P], nat[:, b2, 1, i, :], nat[:, b2, 2, i, :], start=False,
                                          stop=True).then_inc(s_summed, 1)
                            if c % 8 == 0 and (c or not first):
                                pe.wait_ge(o_ready, 3 * j + c // 8)
                            cols = slice(c * RC, (c + 1) * RC)
                            pe.matmul(o_b[:, o0:o0 + RC], Us[:, :], rbT[:, b2, i, :], start=True, stop=False)
                            if c < C - 1:
                                pe.matmul(o_b[:, o0:o0 + RC], S[:, c % 2, :], ar[:, 1, cols], start=False, stop=False)
                            else:
                                for b in range(NB):
                                    pe.matmul(o_b[:, b * NT:(b + 1) * NT], S_in[:, b, :],
                                              ar[:, 1, SEQ + b * NT:SEQ + (b + 1) * NT], start=False, stop=False,
                                              skip_group_check=True)
                            pe.matmul(o_b[:, o0:o0 + RC], nat[:, b2, 2, i, :], rkT[:, b2, i, :], start=False,
                                      stop=True).then_inc(o_summed, 1)
                            if c == C - 1:
                                pe.wait_ge(bk_seq_ready, j + 1)
                                for b in range(NB):
                                    pe.wait_ge(S_ready, j * NSR + c + 1 + b)
                                    pe.matmul(s_b[:, 0:P], bk_seq[:, 0, b, :], Us[:, :], start=True, stop=False)
                                    pe.matmul(s_b[:, 0:P], bk_seq[:, 1, b, :], nat[:, b2, 2, i, :], start=False,
                                              stop=True).then_inc(s_summed, 1)
                    pe.wait_ge(o_ready, 3 * (j + 1))
                    pe.wait_ge(T_ready, (j + 1) * NTR)
                    pe.wait_ge(p_ready, (j + 1) * NP)
                    sum3(mean[:, :], oT[:, 0:M], norm_summed)
                    pe.wait_ge(squares, 2 * (j + 1))
                    sum3(mean[:, :], rn[:, :], norm_summed)

                pair(0, True)
                with pe.Fori(1, PAIRS) as j:
                    pair(j, False)


MP = (TILES + 1) * P


def merge(nc, t):
    with ExitStack() as ctx:
        s = Stage(nc, ctx, "mg")
        br = s.sb("br", [P, 2, KD, M])
        mT = s.sb("mT", [P, KD, M])
        w = s.sb("w", [P, 2, 2, KD, P])
        gt = s.sb("gt", [P, 2, M])
        tmp = s.sb("tmp", [P, 2, M])
        MW_ = [s.ps(f"acc{n}", [P, 3, 512]) for n in range(2)]
        acc = MW_
        consts_in, g_in = s.sem("consts_in"), s.sem("g_in")
        w_in = [s.sem(f"w_in{n}") for n in range(2)]
        gates_ready, gated, merged = s.sem("gates_ready"), s.sem("gated"), s.sem("merged")
        summed = [s.sem(f"summed{n}") for n in range(2)]
        own, own_act = s.sem("vector_chain"), s.sem("scalar_chain")
        with nc.Block() as block:
            @block.sync
            def _(sp):
                sp.dma_start(br[:, 0, :, :].rearrange("p (h a) m -> p h a m", a=2),
                             t["ogT"].rearrange("h p a m -> p h a m")).then_inc(consts_in, 16)
                sp.dma_start(br[:, 1, :, :], t["orT"].rearrange("j p m -> p j m")).then_inc(consts_in, 16)
                for n in range(2):
                    sp.dma_start(w[:, n, :, :, :], t["w_br"][n]).then_inc(w_in[n], 16)

                def gates(j):
                    for b in range(2):
                        sp.dma_start(gt[:, b, :], t["pT"][j + (50 + KD * b)]).then_inc(g_in, 16)

                gates(0)
                with sp.Fori(0, KD // 2 - 1) as i:
                    for n in range(2):
                        sp.wait_ge(merged, i * 2 + n + 1)
                        gates(i * 2 + (n + 1))
                        sp.dma_start(w[:, n, :, :, :], t["w_br"][i * 2 + (n + 2)]).then_inc(w_in[n], 16)
                sp.wait_ge(merged, KD - 1)
                gates(KD - 1)

            @block.scalar
            def _(act):
                with act.Fori(0, KD) as i:
                    act.wait_ge(g_in, i * 32 + 32)
                    act.activation(gt[:, :, :], gt[:, :, :], ACT.Sigmoid).then_inc(gates_ready, 1)

            @block.vector
            def _(dve):
                g3 = lambda x: x.rearrange("p (g c) -> p g c", g=3)
                with dve.Fori(0, KD) as i:
                    dve.wait_ge(gates_ready, i + 1)
                    for b in range(2):
                        dve.wait_ge(summed[b], i + 1)
                        dve.tensor_tensor(g3(tmp[:, b, :]), acc[b][:, :, 0:G3], g3(gt[:, b, :]), ALU.mult).then_inc(gated, 1)
                    dve.wait_ge(gated, i * 2 + 2)
                    dve.tensor_tensor(mT[:, i, :], tmp[:, 0, :], tmp[:, 1, :], ALU.add).then_inc(merged, 1)
                    dve.wait_ge(merged, i + 1)

            @block.tensor
            def _(pe):
                pe.wait_ge(consts_in, 32)

                def tiles(i, first):
                    for n in range(2):
                        pe.wait_ge(w_in[n], i * 16 + 16)
                        for b in range(2):
                            if not first or n:
                                pe.wait_ge(gated, i * 4 + (2 * n - 1 + b))
                            for g in range(3):
                                for k in range(KD):
                                    last = pe.matmul(acc[b][:, g, 0:G3], w[:, n, b, k, :],
                                                     br[:, b, k, g * G3:(g + 1) * G3], start=(k == 0), stop=(k == KD - 1))
                            last.then_inc(summed[b], 1)

                tiles(0, True)
                with pe.Fori(1, KD // 2) as i:
                    tiles(i, False)

        with ExitStack() as ctx2:
            s = Stage(nc, ctx2, "out")
            w_out = w[:, :, :, :, :].rearrange("p a b k c -> p (a b k c)")[:, 0:4 * D]
            w_hi = s.sb("w_hi", [P, 4, D])
            rhs = lambda k, c: (w_out[:, k * D + c:k * D + c + 512] if k < 4 else w_hi[:, k - 4, c:c + 512])
            mod = s.sb("mod", [P, 3, D])
            free = br[:, :, :, :].rearrange("p a k m -> p (a k m)")
            mod_s = free[0:NS, 0:3 * D].rearrange("p (r c) -> p r c", r=3)
            x = free[:, 3 * D:5 * D].rearrange("p (n c) -> p n c", n=2)
            mt = free[:, 5 * D:7 * D].rearrange("p (n k c) -> p n k c", n=2, k=KD)
            x2 = free[:, 7 * D:9 * D].rearrange("p (n c) -> p n c", n=2)
            h2 = free[:, 9 * D:11 * D].rearrange("p (n c) -> p n c", n=2)
            sq = free[:, 11 * D:12 * D]
            ss = s.sb("ss", [P, 2])
            eps = s.sb("eps", [P, 1])
            (c_in, cleared, turned, y_summed, rstd1, rstd2, x2_ready, h2_ready, y_read, oc, oa) = (
                s.sem(n) for n in ("consts_in", "cleared", "mt_ready", "y_summed", "rstd1", "rstd2", "x2_ready",
                                   "h2_ready", "y_read", "vector_chain", "scalar_chain"))
            x_in = [s.sem(f"x_in{n}") for n in range(2)]
            stored = [s.sem(f"stored{n}") for n in range(2)]
            with nc.Block() as block:
                @block.sync
                def _(sp):
                    sp.dma_start(w_out, t["w_out"][0]).then_inc(c_in, 16)
                    sp.dma_start(w_hi[:, :, :], t["w_out"][1].rearrange("p (k c) -> p k c", k=4)).then_inc(c_in, 16)
                    for n, row in enumerate((G1, A2, S2)):
                        load_mod(sp, t, mod[:, n, :], row, False, c_in)
                        load_mod(sp, t, mod_s[:, n, :], row, True, c_in)
                    for n in range(2):
                        sp.dma_start(x[:, n, :], t["x"][n * P:(n + 1) * P, :]).then_inc(x_in[n], 16)

                    def out(row0, rows, n):
                        sp.dma_start(t["x2"][bass.ds(row0, rows), :], x2[0:rows, n, :]).then_inc(stored[n], 16)
                        sp.dma_start(t["h2"][bass.ds(row0, rows), :], h2[0:rows, n, :]).then_inc(stored[n], 16)

                    with sp.Fori(0, TILES // 2 - 1) as i:
                        for n in range(2):
                            sp.wait_ge(h2_ready, i * 2 + n + 1)
                            out(i * (2 * P) + n * P, P, n)
                            sp.dma_start(x[:, n, :], t["x"][bass.ds(i * (2 * P) + (n + 2) * P, P), :]).then_inc(x_in[n], 16)
                    for n in range(2):
                        sp.wait_ge(h2_ready, TILES - 1 + n)
                        out(SEQ - (2 - n) * P, P, n)
                        if n == 0:
                            sp.dma_start(x[0:NS, 0, :], t["x"][SEQ:M, :]).then_inc(x_in[0], 16)
                    sp.wait_ge(h2_ready, TILES + 1)
                    out(SEQ, NS, 0)
                    for g in range(1, P // NS):
                        sp.dma_start(t["h2"][SEQ + g * NS:SEQ + (g + 1) * NS, :], h2[0:NS, 0, :]).then_inc(stored[0], 16)
                    sp.wait_ge(stored[0], 32 * (TILES // 2 + 1) + 16 * (P // NS - 1))
                    sp.wait_ge(stored[1], 32 * (TILES // 2))

                @block.scalar
                def _(act):
                    ch = Chain(act, oa)
                    act.wait_ge(cleared, 1)
                    act.copy(mt[:, 0, :, :], mT[:, :, 0:P]).then_inc(turned, 1)

                    def tile(i, n, rows, nxt):
                        if nxt is not None:
                            c0, r = nxt
                            if n is not None:
                                act.wait_ge(y_summed, i) if not (isinstance(i, int) and i == 0) else None
                            act.copy(mt[:, 1 - n, :, 0:r], mT[:, :, bass.ds(c0, r)]).then_inc(turned, 1)
                        act.wait_ge(y_summed, i + 1)
                        ch.link(act.activation(sq[0:rows, :].rearrange("p (g c) -> p g c", g=2), acc[n][0:rows, 0:2, :],
                                               ACT.Square, accum_out=ss[0:rows, 0:1]))
                        ch.link(act.activation(ss[0:rows, 0:1], ss[0:rows, 0:1], ACT.Ln, bias=eps[0:rows, :], scale=1.0 / D))
                        act.activation(ss[0:rows, 0:1], ss[0:rows, 0:1], ACT.Exp, scale=-0.5).then_inc(rstd1, 1)
                        act.wait_ge(x2_ready, i + 1)
                        ch.link(act.activation(sq[0:rows, :], x2[0:rows, n, :], ACT.Square, accum_out=ss[0:rows, 1:2]))
                        ch.link(act.activation(ss[0:rows, 1:2], ss[0:rows, 1:2], ACT.Ln, bias=eps[0:rows, :], scale=1.0 / D))
                        act.activation(ss[0:rows, 1:2], ss[0:rows, 1:2], ACT.Exp, scale=-0.5).then_inc(rstd2, 1)

                    tile(0, 0, P, (P, P))
                    ch.enter(0, 8) if False else None
                    base = ch.n
                    with act.Fori(0, TILES // 2 - 1) as i:
                        ch.enter(i, 8)
                        for n in (1, 0):
                            j = i * 2 + (1 if n else 2)
                            tile(j, n, P, (j * P + P, P))
                        ch.leave(TILES // 2 - 1)
                    tile(TILES - 1, 1, P, (SEQ, NS))
                    tile(TILES, 0, NS, None)

                @block.vector
                def _(dve):
                    ch = Chain(dve, oc)
                    dve.memset(eps[:, :], NORM_EPS).then_inc(cleared, 1)
                    dve.wait_ge(c_in, 16 * (2 + 3 * (1 + NB)))

                    def tile(i, n, rows, m, first=False):
                        xr, x2r, h2r = x[0:rows, n, :], x2[0:rows, n, :], h2[0:rows, n, :]
                        dve.wait_ge(rstd1, i + 1)
                        if not first:
                            dve.wait_ge(stored[n], (i // 2) * 32 if isinstance(i, int) else first_stored[0])
                        g2 = lambda v: v.rearrange("p (g c) -> p g c", g=2)
                        ch.link(dve.scalar_tensor_tensor(out=g2(x2r), in0=acc[n][0:rows, 0:2, :], scalar=ss[0:rows, 0:1],
                                                         in1=g2(m[:, 0, :]), op0=ALU.mult, op1=ALU.mult))
                        dve.sem_inc(y_read, 1)
                        dve.wait_ge(x_in[n], 16 * (i // 2 + 1) if isinstance(i, int) else first_stored[1])
                        dve.tensor_tensor(x2r, x2r, xr, ALU.add).then_inc(x2_ready, 1)
                        dve.wait_ge(rstd2, i + 1)
                        ch.link(dve.scalar_tensor_tensor(out=h2r, in0=x2r, scalar=ss[0:rows, 1:2], in1=m[:, 1, :],
                                                         op0=ALU.mult, op1=ALU.mult))
                        dve.tensor_tensor(h2r, h2r, m[:, 2, :], ALU.add).then_inc(h2_ready, 1)

                    first_stored = [0, 0]
                    for n in range(2):
                        tile(n, n, P, mod[:, :, :], True)
                    with dve.Fori(1, TILES // 2) as i:
                        ch.enter(i - 1, 4)
                        for n in range(2):
                            first_stored = [i * 32, i * 16 + 16]
                            tile(i * 2 + n, n, P, mod[:, :, :])
                        ch.leave(TILES // 2 - 1)
                    tile(TILES, 0, NS, mod_s)

                @block.tensor
                def _(pe):
                    pe.wait_ge(c_in, 16 * (2 + 3 * (1 + NB)))

                    def tile(i, n, rows, first=False):
                        pe.wait_ge(turned, i + 1)
                        if not first:
                            pe.wait_ge(y_read, i - 1)
                        for c in range(2):
                            for k in range(KD):
                                last = pe.matmul(acc[n][0:rows, c, :], mt[:, n, k, 0:rows], rhs(k, c * 512),
                                                 start=(k == 0), stop=(k == KD - 1))
                        last.then_inc(y_summed, 1)

                    tile(0, 0, P, True)
                    tile(1, 1, P, True)
                    with pe.Fori(1, TILES // 2) as i:
                        for n in range(2):
                            tile(i * 2 + n, n, P)
                    tile(TILES, 0, NS)


HEADS, KEYS, TOP = 8, 128, 16
RING = TOP
GROUPS = P // NS
UNITS = TILES * HEADS
S_UNITS = HEADS // GROUPS
HALF = TOP // 2
LOWEST = -3.0e38


def peer(nc, t):
    with ExitStack() as ctx:
        s = Stage(nc, ctx, "peer")
        ident = s.sb("ident", [P, P])
        fold = s.sb("fold", [P, NS])
        iota = s.sb("iota", [P, TOP])
        zeros = s.sb("zeros", [1, 512])
        wq = s.sb("wq", [P, KD, 2 * HEADS * P])
        keys = s.sb("keys", [P, 2 * HEADS, KEYS])
        G2p, G2s = s.sb("G2p", [P, D]), s.sb("G2s", [NS, D])
        ring = s.sb("ring", [P, RING, D])
        h_next, h_now, hT = s.sb("h_next", [P, D]), s.sb("h_now", [P, D]), s.sb("hT", [P, KD, P])
        x2 = s.sb("x2", [P, D])
        acc = s.sb("acc", [P, 2, D])
        y, sq = s.sb("y", [P, D]), s.sb("sq", [P, D])
        EXPERTS = (TILES + 1) * HEADS * TOP
        idx_all, w_all = s.sb("idx_all", [P, EXPERTS], U32), s.sb("w_all", [P, EXPERTS])
        idx_smp, w_smp = s.sb("idx_smp", [P, S_UNITS * TOP], U32), s.sb("w_smp", [P, S_UNITS * TOP])
        idx = [s.sb(f"idx{n}", [P, TOP], U32) for n in range(2)]
        dots, act_d, coef = s.sb("dots", [P, TOP]), s.sb("act_d", [P, TOP]), s.sb("coef", [P, TOP])
        diag = s.sb("diag", [P, HALF, P])
        q, qT, sc = s.sb("q", [P, 2 * P]), s.sb("qT", [P, 2 * P]), s.sb("sc", [P, 2, KEYS])
        top, pos = s.sb("top", [P, 2, TOP]), s.sb("pos", [P, 2, TOP], U32)
        posf = s.sb("posf", [P, 2, TOP])
        cand = s.sb("cand", [P, TOP, TOP])
        best, j16, j2 = s.sb("best", [P, TOP]), s.sb("j16", [P, TOP], U32), s.sb("j2", [P, 2, TOP], U32)
        jf = s.sb("jf", [P, 2, TOP])
        hot = s.sb("hot", [P, 2, TOP, TOP])
        sel = s.sb("sel", [P, 2, TOP])
        ex, z = s.sb("ex", [P, TOP]), s.sb("z", [P, 2])
        ss, eps = s.sb("ss", [P, 1]), s.sb("eps", [P, 1])
        q_b, qT_b, s_b = s.ps("q_b"), s.ps("qT_b"), s.ps("s_b")
        h_b = [s.ps(f"h_b{n}") for n in range(2)]
        v_b = s.ps("v_b", [P, 2, 512])
        (consts_in, wq_in, cleared, h_in, x2_in, h_turned, hT_ready, h_moved, u_used, v_used, pe_used, dots_ready,
         gelu_ready, coef_ready, diag_ready, q_summed, q_ready, q_turned, qT_ready, s_summed, s_ready, best_ready,
         ex_ready, routed, idx_ready, issued, v_summed, v_read, total_ready, folded, acc_ready, ms_ready, y_ready,
         y_stored, y_free, passed, passed_pe, own, own_act) = (s.sem(n) for n in (
             "consts_in wq_in cleared h_in x2_in h_turned hT_ready h_moved u_used v_used pe_used dots_ready "
             "gelu_ready coef_ready diag_ready q_summed q_ready q_turned qT_ready s_summed s_ready best_ready "
             "ex_ready routed idx_ready issued v_summed v_read total_ready folded acc_ready ms_ready y_ready "
             "y_stored y_free passed passed_pe own own_act").split())
        landed = [s.sem(f"landed{n}") for n in range(RING)]
        CONSTS = 4 + NB

        with nc.Block() as block:
            @block.sync
            def _(sp):
                sp.dma_start(h_next[:, :], t["h2"][0:P, :]).then_inc(h_in, 16)
                sp.dma_start(ident[:, :], t["ident"]).then_inc(consts_in, 16)
                sp.dma_start(wq[:, :, :], t["peer_wq"]).then_inc(wq_in, 16)
                sp.dma_start(keys[:, :, :], t["peer_keys"]).then_inc(wq_in, 16)
                sp.dma_start(iota[:, :], t["iota"].broadcast_to([P, TOP])).then_inc(consts_in, 16)
                sp.dma_start(fold[:, :], t["fold"]).then_inc(consts_in, 16)
                load_mod(sp, t, G2p, G2, False, consts_in)
                load_mod(sp, t, G2s, G2, True, consts_in)
                sp.dma_start(x2[:, :], t["x2"][0:P, :]).then_inc(x2_in, 16)

                def tile(i, rows):
                    sp.wait_ge(h_moved, i + 1)
                    if rows == P:
                        sp.dma_start(h_next[:, :], t["h2"][bass.ds((i + 1) * P, P), :]).then_inc(h_in, 16)
                    sp.wait_ge(y_ready, i + 1)
                    sp.dma_start(t["y"][bass.ds(i * P, rows), :], y[0:rows, :]).then_inc(y_stored, 16)

                sp.sem_inc(y_free, 1)
                with sp.Fori(0, TILES - 1) as i:
                    tile(i, P)
                    sp.dma_start(x2[:, :], t["x2"][bass.ds((i + 1) * P, P), :]).then_inc(x2_in, 16)
                    sp.wait_ge(y_stored, i * 16 + 16)
                    sp.sem_inc(y_free, 1)
                tile(TILES - 1, P)
                sp.dma_start(x2[0:NS, :], t["x2"][SEQ:M, :]).then_inc(x2_in, 16)
                sp.wait_ge(y_stored, 16 * TILES)
                sp.sem_inc(y_free, 1)
                tile(TILES, NS)
                sp.wait_ge(y_stored, 16 * (TILES + 1))

            @block.gpsimd
            def _(pool):
                def unit(U, par):
                    pool.wait_ge(idx_ready, U + 1)
                    for k in range(TOP):
                        pool.wait_ge(pe_used if k % 2 else v_used, U * HALF + (k // 2 + 1))
                        pool.sem_inc(issued, 1)
                        pool.indirect_dma_start(
                            out=ring[:, k, :], out_offset=None, in_=t["peer_u"],
                            in_offset=bass.IndirectOffsetOnAxis(ap=idx[par][:, k:k + 1], axis=0)).then_inc(landed[k], 16)
                    for k in range(TOP):
                        pool.wait_ge(u_used, U * TOP + (k + 1))
                        pool.sem_inc(issued, 1)
                        pool.indirect_dma_start(
                            out=ring[:, k, :], out_offset=None, in_=t["peer_v"],
                            in_offset=bass.IndirectOffsetOnAxis(ap=idx[par][:, k:k + 1], axis=0)).then_inc(landed[k], 16)

                with pool.Fori(0, (UNITS + S_UNITS) // 2) as m:
                    for n in range(2):
                        unit(m * 2 + n, n)

            @block.scalar
            def _(act):
                ch = Chain(act, own_act)
                act.sem_inc(diag_ready, HALF)
                act.wait_ge(cleared, 2)
                act.wait_ge(consts_in, 16 * CONSTS)

                def turn_h(i):
                    act.wait_ge(h_turned, i + 1)
                    for n in range(2):
                        act.copy(hT[:, 4 * n:4 * n + 4, :],
                                 h_b[n][:, :].rearrange("p (k c) -> p k c", k=4)).then_inc(hT_ready, 1)

                def copy_q(R):
                    act.wait_ge(q_summed, R + 1)
                    act.copy(q[:, :], q_b[:, 0:2 * P]).then_inc(q_ready, 1)
                    act.wait_ge(q_turned, R + 1)
                    act.copy(qT[:, :], qT_b[:, 0:2 * P]).then_inc(qT_ready, 1)

                def copy_s(R):
                    act.wait_ge(s_summed, R + 1)
                    act.copy(sc[:, :, :].rearrange("p a n -> p (a n)"), s_b[:, 0:2 * KEYS]).then_inc(s_ready, 1)

                def exps(R):
                    act.activation(ex[:, :], best[:, :], ACT.Exp, bias=z[:, 1:2], accum_out=z[:, 0:1]).then_inc(ex_ready, 1)

                def weigh(U):
                    act.wait_ge(dots_ready, U + 1)
                    act.wait_ge(diag_ready, U * HALF + HALF)
                    act.activation(act_d[:, :], dots[:, :], ACT.Gelu).then_inc(gelu_ready, 1)
                    act.wait_ge(coef_ready, U + 1)
                    for j in range(HALF):
                        act.wait_ge(pe_used, U * HALF + (j + 1))
                        act.activation(diag[:, j, :], ident[:, :], ACT.Copy,
                                       scale=coef[:, 2 * j + 1:2 * j + 2]).then_inc(diag_ready, 1)

                def finish(i, rows):
                    act.wait_ge(acc_ready, i + 1)
                    ch.link(act.activation(sq[0:rows, :], acc[0:rows, 0, :], ACT.Square, accum_out=ss[0:rows, :]))
                    ch.link(act.activation(ss[0:rows, :], ss[0:rows, :], ACT.Ln, bias=eps[0:rows, :], scale=1.0 / D))
                    act.activation(ss[0:rows, :], ss[0:rows, :], ACT.Exp, scale=-0.5).then_inc(ms_ready, 1)

                turn_h(0)
                copy_q(0)
                copy_s(0)
                with act.Fori(0, HEADS - 1) as h:
                    copy_q(h + 1)
                    act.wait_ge(best_ready, h + 1)
                    copy_s(h + 1)
                    exps(h)
                act.wait_ge(best_ready, HEADS)
                exps(HEADS - 1)
                act.copy(h_now[:, :], h_next[:, :]).then_inc(h_moved, 1)
                with act.Fori(0, TILES) as i:
                    ch.enter(i, 2)
                    turn_h(i + 1)
                    with act.Fori(0, HEADS) as h:
                        copy_q(i * HEADS + h + HEADS)
                        copy_s(i * HEADS + h + HEADS)
                        weigh(i * HEADS + h)
                        act.wait_ge(best_ready, i * HEADS + h + (HEADS + 1))
                        exps(i * HEADS + h + HEADS)
                    act.copy(h_now[:, :], h_next[:, :]).then_inc(h_moved, 1)
                    finish(i, P)
                    ch.leave(TILES)
                for n in range(S_UNITS):
                    weigh(UNITS + n)
                finish(TILES, NS)

            @block.vector
            def _(dve):
                ch = Chain(dve, own)
                dve.memset(eps[:, :], NORM_EPS).then_inc(cleared, 1)
                dve.memset(zeros[:, :], 0.0).then_inc(cleared, 1)
                dve.sem_inc(v_used, HALF)
                dve.wait_ge(consts_in, 16 * CONSTS)

                def alone(ins):
                    ch.link(ins)
                    dve.sem_inc(passed, 1)

                def top16(vals, val, place):
                    for n in range(2):
                        o8 = slice(8 * n, 8 * n + 8)
                        alone(dve.max(val[:, o8], vals))
                        last = dve.max_index(place[:, o8], val[:, o8], vals)
                        if n == 0:
                            alone(last)
                            alone(dve.match_replace(vals, val[:, o8], vals, LOWEST))
                    return last

                def route_keys(R):
                    dve.wait_ge(s_ready, R + 1)
                    dve.sem_inc(passed, 1)
                    for n in range(2):
                        last = top16(sc[:, n, :], top[:, n, :], pos[:, n, :])
                    ch.link(last)

                def route_pairs(R):
                    dve.tensor_copy(posf[:, :, :], pos[:, :, :])
                    alone(dve.tensor_tensor(cand[:, :, :], top[:, 0, :].unsqueeze(2).broadcast_to([P, TOP, TOP]),
                                            top[:, 1, :].unsqueeze(1).broadcast_to([P, TOP, TOP]), ALU.add))
                    ch.link(top16(cand[:, :, :].rearrange("p a b -> p (a b)"), best, j16))
                    dve.tensor_scalar(z[:, 1:2], best[:, 0:1], -1.0, None, ALU.mult).then_inc(best_ready, 1)
                    dve.tensor_scalar(j2[:, 0, :], j16[:, :], 4, None, ALU.logical_shift_right)
                    ch.link(dve.tensor_scalar(j2[:, 1, :], j16[:, :], TOP - 1, None, ALU.bitwise_and))
                    ch.link(dve.tensor_copy(jf[:, :, :], j2[:, :, :]))
                    for n in range(2):
                        last = dve.tensor_tensor(hot[:, n, :, :], jf[:, n, :].unsqueeze(2).broadcast_to([P, TOP, TOP]),
                                                 iota[:, :].unsqueeze(1).broadcast_to([P, TOP, TOP]), ALU.is_equal)
                    ch.link(last)
                    for n in range(2):
                        last = dve.tensor_tensor(hot[:, n, :, :], hot[:, n, :, :],
                                                 posf[:, n, :].unsqueeze(1).broadcast_to([P, TOP, TOP]), ALU.mult)
                    ch.link(last)
                    ch.link(dve.tensor_reduce(sel[:, :, :], hot[:, :, :, :], AX.X, ALU.add))
                    dve.scalar_tensor_tensor(out=idx_all[:, bass.ds(R * TOP, TOP)], in0=sel[:, 0, :], scalar=float(KEYS),
                                             in1=sel[:, 1, :], op0=ALU.mult, op1=ALU.add).then_inc(routed, 1)
                    dve.wait_ge(ex_ready, R + 1)
                    ch.link(dve.reciprocal(z[:, 0:1], z[:, 0:1]))
                    dve.tensor_scalar(w_all[:, bass.ds(R * TOP, TOP)], ex[:, :], z[:, 0:1], None, ALU.mult).then_inc(routed, 1)
                    dve.wait_ge(routed, R * 2 + 2)

                def hand_idx(par, src):
                    dve.tensor_copy(idx[par][:, :], src).then_inc(idx_ready, 1)

                def unit(U, weights, R=None):
                    for k in range(TOP):
                        dve.wait_ge(landed[k], U * 32 + 16)
                        dve.tensor_tensor_reduce(ring[:, k, :], ring[:, k, :], h_now[:, :], 1.0, 0.0,
                                                 ALU.mult, ALU.add, dots[:, k:k + 1]).then_inc(u_used, 1)
                    dve.wait_ge(u_used, U * TOP + TOP)
                    dve.sem_inc(dots_ready, 1)
                    if R is not None:
                        route_keys(R)
                    dve.wait_ge(gelu_ready, U + 1)
                    dve.wait_ge(v_used, U * HALF + HALF)
                    dve.tensor_tensor(coef[:, :], act_d[:, :], weights, ALU.mult).then_inc(coef_ready, 1)
                    if R is not None:
                        route_pairs(R)

                def add_v(U):
                    dve.wait_ge(coef_ready, U + 1)
                    for j in range(HALF):
                        k = 2 * j
                        dve.wait_ge(landed[k], U * 32 + 32)
                        if j < 2:
                            dve.wait_ge(v_used, U * HALF + HALF)
                        else:
                            dve.wait_ge(v_used, U * HALF + (HALF + j - 1))
                        dve.scalar_tensor_tensor(out=acc[:, j % 2, :], in0=ring[:, k, :], scalar=coef[:, k:k + 1],
                                                 in1=acc[:, j % 2, :], op0=ALU.mult, op1=ALU.add).then_inc(v_used, 1)

                def clear():
                    dve.memset(acc[:, :, :], 0.0).then_inc(own, 1)
                    ch.n += 1
                    dve.wait_ge(own, ch.base + ch.n)
                    dve.sem_inc(passed, 1)

                def total(i, units):
                    dve.wait_ge(v_used, units * HALF + HALF)
                    ch.link(dve.tensor_tensor(acc[:, 0, :], acc[:, 0, :], acc[:, 1, :], ALU.add))
                    dve.wait_ge(v_summed, i + 1)
                    ch.link(dve.tensor_tensor(acc[:, 0, :].rearrange("p (g c) -> p g c", g=2),
                                              acc[:, 0, :].rearrange("p (g c) -> p g c", g=2), v_b[:, :, :], ALU.add))

                def finish(i, rows, gain):
                    dve.sem_inc(acc_ready, 1)
                    dve.wait_ge(ms_ready, i + 1)
                    dve.wait_ge(x2_in, i * 16 + 16)
                    dve.wait_ge(y_free, i + 1)
                    ch.link(dve.scalar_tensor_tensor(out=y[0:rows, :], in0=acc[0:rows, 0, :], scalar=ss[0:rows, 0:1],
                                                     in1=gain, op0=ALU.mult, op1=ALU.mult))
                    dve.tensor_tensor(y[0:rows, :], y[0:rows, :], x2[0:rows, :], ALU.add).then_inc(y_ready, 1)

                cols = lambda U: bass.ds(U * TOP, TOP)
                ROUTE = 21
                route_keys(0)
                route_pairs(0)
                hand_idx(0, idx_all[:, 0:TOP])
                assert ch.n == ROUTE, ch.n
                with dve.Fori(1, HEADS) as h:
                    ch.enter(h - 1, ROUTE)
                    route_keys(h)
                    route_pairs(h)
                    ch.leave(HEADS - 1)
                ch0 = ch.n
                PER = 1 + HEADS * ROUTE + 3

                def pair(i, m, link0, odd=None):
                    ch.base, ch.n = link0, 0
                    for n in range(2):
                        U = i * HEADS + m * 2 + n
                        unit(U, w_all[:, cols(U)], U + HEADS)
                        if n and odd:
                            odd()
                        else:
                            hand_idx(1 - n, idx_all[:, cols(U + 1)])
                        add_v(U)
                    assert ch.n == 2 * ROUTE, ch.n

                def tile_end(i):
                    ch.base, ch.n = ch0 + i * PER + 1 + HEADS * ROUTE, 0
                    total(i, i * HEADS + HEADS)
                    dve.sem_inc(v_read, 1)
                    finish(i, P, G2p[:, :])
                    assert ch.n == 3

                with dve.Fori(0, TILES - 1) as i:
                    dve.wait_ge(h_moved, i + 1)
                    ch.base, ch.n = ch0 + i * PER, 0
                    clear()
                    with dve.Fori(0, HEADS // 2) as m:
                        pair(i, m, ch0 + i * PER + 1 + m * (2 * ROUTE))
                    tile_end(i)

                def deal():
                    for g in range(GROUPS):
                        rows = slice(g * NS, (g + 1) * NS)
                        e0 = UNITS * TOP + g
                        dve.tensor_copy(idx_smp[rows, :], idx_all[rows, e0:EXPERTS:GROUPS]).then_inc(routed, 1)
                        dve.tensor_copy(w_smp[rows, :], w_all[rows, e0:EXPERTS:GROUPS]).then_inc(routed, 1)
                    dve.wait_ge(routed, (TILES + 1) * HEADS * 2 + 2 * GROUPS)
                    hand_idx(0, idx_smp[:, 0:TOP])

                last = TILES - 1
                dve.wait_ge(h_moved, TILES)
                ch.base, ch.n = ch0 + last * PER, 0
                clear()
                with dve.Fori(0, HEADS // 2 - 1) as m:
                    pair(last, m, ch0 + last * PER + 1 + m * (2 * ROUTE))
                pair(last, HEADS // 2 - 1, ch0 + last * PER + 1 + (HEADS - 2) * ROUTE, deal)
                tile_end(last)

                dve.wait_ge(h_moved, TILES + 1)
                ch.base, ch.n = ch0 + TILES * PER, 0
                clear()
                for n in range(S_UNITS):
                    unit(UNITS + n, w_smp[:, cols(n)])
                    if n + 1 < S_UNITS:
                        hand_idx(1 - n, idx_smp[:, cols(n + 1)])
                    add_v(UNITS + n)
                total(TILES, UNITS + S_UNITS)
                dve.sem_inc(total_ready, 1)
                dve.wait_ge(folded, 1)
                ch.link(dve.tensor_copy(acc[0:NS, 0, :].rearrange("p (g c) -> p g c", g=2), v_b[0:NS, :, :]))
                finish(TILES, NS, G2s[:, :])

            @block.tensor
            def _(pe):
                pe.sem_inc(pe_used, HALF)
                pe.wait_ge(cleared, 2)
                pe.wait_ge(consts_in, 16 * CONSTS)

                def turn_h(i):
                    pe.wait_ge(h_in, i * 16 + 16)
                    for k in range(KD):
                        last = pe.transpose(h_b[k // 4][:, (k % 4) * P:(k % 4 + 1) * P], h_next[:, k * P:(k + 1) * P],
                                            ident[:, :])
                    last.then_inc(h_turned, 1)
                    pe.wait_ge(hT_ready, i * 2 + 2)
                    pe.sem_inc(passed_pe, 1)

                def route(R, h):
                    for k in range(KD):
                        last = pe.matmul(q_b[:, 0:2 * P], hT[:, k, :], wq[:, k, bass.ds(h * (2 * P), 2 * P)],
                                         start=(k == 0), stop=(k == KD - 1))
                    last.then_inc(q_summed, 1)
                    pe.wait_ge(q_ready, R + 1)
                    for n in range(2):
                        last = pe.transpose(qT_b[:, n * P:(n + 1) * P], q[:, n * P:(n + 1) * P], ident[:, :])
                    last.then_inc(q_turned, 1)
                    pe.wait_ge(qT_ready, R + 1)
                    for n in range(2):
                        last = pe.matmul(s_b[:, n * KEYS:(n + 1) * KEYS], qT[:, n * P:(n + 1) * P],
                                         keys[:, bass.ds(h * 2 + n, 1), :].rearrange("p o n -> p (o n)"), start=True, stop=True)
                    last.then_inc(s_summed, 1)
                    pe.wait_ge(s_ready, R + 1)

                def zero_banks(start):
                    for c in range(2):
                        last = pe.matmul(v_b[:, c, :], zeros[:, 0:P], zeros[:, :], start=start, stop=not start)
                    return last

                def add_v(U):
                    for j in range(HALF):
                        k = 2 * j + 1
                        pe.wait_ge(diag_ready, U * HALF + (HALF + j + 1))
                        pe.wait_ge(landed[k], U * 32 + 32)
                        for c in range(2):
                            last = pe.matmul(v_b[:, c, :], diag[:, j, :], ring[:, k, c * 512:(c + 1) * 512],
                                             start=False, stop=False)
                        last.then_inc(pe_used, 1)

                pe.wait_ge(wq_in, 32)
                turn_h(0)
                with pe.Fori(0, HEADS) as h:
                    route(h, h)
                zero_banks(True)
                with pe.Fori(0, TILES) as i:
                    turn_h(i + 1)
                    with pe.Fori(0, HEADS) as h:
                        route(i * HEADS + h + HEADS, h)
                        add_v(i * HEADS + h)
                    zero_banks(False).then_inc(v_summed, 1)
                    pe.wait_ge(v_read, i + 1)
                    zero_banks(True)
                for n in range(S_UNITS):
                    add_v(UNITS + n)
                zero_banks(False).then_inc(v_summed, 1)
                pe.wait_ge(total_ready, 1)
                for c in range(2):
                    last = pe.matmul(v_b[0:NS, c, :], fold[:, :], acc[:, 0, c * 512:(c + 1) * 512], start=True, stop=True)
                last.then_inc(folded, 1)


def scratch(nc, t):
    for name, shape in {"mod": [NSEQ, 6, D], "pT": [66, P, M], "gaT": [16, M],
                        "ogT": [GH, P, 2, M], "orT": [PAIRS, P, M],
                        "x2": [M, D], "h2": [MP, D]}.items():
        t[name] = nc.dram_tensor(name, shape, F32, kind="Internal").ap()


def build(nc, t):
    scratch(nc, t)
    for stage in (modulation, projection, gla, rwkv, merge, peer):
        with nc.cleanup_on_exit():
            stage(nc, t)


OUTPUTS = {"y": [M, D], "new_gla_p": [GH, P, GV], "new_gla_s": [GH, P, NB, GV],
           "new_rw_p": [PAIRS, 2, RH, RH], "new_rw_s": [PAIRS, 2, RH, NB, RH],
           "new_shift": [PAIRS, 3, P, NSEQ], "new_shift_wg": [2, P, NSEQ]}


def masks():
    f = np.float32
    s, q = np.arange(P), np.arange(NS)
    same_chunk = s[:, None] // GC == s[None] // GC
    same_seq = q[:, None] // NT == q[None] // NT
    tok = np.arange(MW)
    head, pos = s // RH, s % RH
    same_head = head[:, None] == head[None]
    before = pos[:, None] < pos[None]
    seq_pos = (pos[:, None] // NT == pos[None] // NT) & (pos[:, None] < NS) & (pos[None] < NS)
    t = np.arange(RC)
    upto = pos[:, None] <= t[None]
    ones_joined = same_head & (pos[:, None] == pos[None] + 1) & (pos[None] % 2 == 0)
    joins = [same_head & (pos[:, None] // (2 * n) == pos[None] // (2 * n)) & (pos[:, None] // n % 2 == 0)
             & (pos[None] // n % 2 == 1) for n in (2 ** (l + 1) for l in range(LEVELS))]
    c = {
        "ident": s[:, None] == s[None],
        "iota": np.arange(TOP)[None],
        "fold": s[:, None] % NS == q[None],
        "starts": np.where(tok < SEQ, tok % GC != 0, tok % NT != 0)[None],
        "gla_mask": same_chunk & (s[:, None] <= s[None]),
        "gla_mask_s": same_seq & (q[:, None] <= q[None]),
        "seq_rows": q[:, None] // NT == np.arange(NB)[None],
        "rw_strict": np.stack([same_head & before, same_head & before & seq_pos], 1),
        "rw_incl": np.stack([upto, upto & (pos[:, None] // NT == t[None] // NT)], 1),
        "rw_first_l": ones_joined,
        "rw_first_u": ones_joined.T,
        "rw_join": np.stack(joins, 1),
        "rw_seq_cols": np.broadcast_to((pos[None] // NT == np.arange(NB)[:, None])[None], (P, NB, P)),
        "rw_seq_rows": pos[:, None] // NT == np.arange(NB)[None],
        "rw_heads": same_head,
    }
    c = {k: np.ascontiguousarray(v.astype(f)) for k, v in c.items()}
    c["rw_mean"] = c["rw_heads"] / f(RH)
    return c


def layout(i):
    o = {}
    o["x"] = np.concatenate([i["x_prompt"].reshape(SEQ, D), i["x_sample"].reshape(NS, D)])
    c = np.concatenate([i["c_prompt"], i["c_sample"]])
    o["cT"] = c.T.reshape(KD, P, NSEQ).transpose(1, 0, 2).reshape(P, KD * NSEQ)
    o["w_ada"] = i["w_ada"][0].reshape(KD, P, 12, 512).transpose(2, 1, 0, 3).reshape(12, P, KD * 512)
    o["b_ada"] = i["b_ada"]
    o["gains"] = np.concatenate([i["g_pre_mix"], i["g_post_mix"], i["g_pre_ffn"], i["g_post_ffn"]])
    w = i["w_in"][0]
    ga0 = 2 * GH * P + 2 * GH * GV
    rest = np.concatenate([w[:, :ga0], w[:, ga0 + 16:]], 1)
    o["w_in"] = rest.reshape(KD, P, 66, P).transpose(2, 1, 0, 3)
    o["w_ga"] = w[:, ga0:ga0 + 16].reshape(KD, P, 16).transpose(1, 0, 2)
    o["w_gate"] = i["w_gla_gate"][0].reshape(16, GH, P).transpose(1, 0, 2)
    o["gla_cst"] = np.concatenate([i["b_gla_gate"][0].reshape(GH, P, 1),
                                   i["g_gla_norm"][0].reshape(GH, 2, P).transpose(0, 2, 1)], 2)
    o["state_gla"] = i["state_gla"][0].transpose(1, 2, 0, 3)
    mu = i["mu_shift"][0].reshape(26, P)
    vec = [i[k][0].reshape(PAIRS, P) for k in ("rw_w0", "rw_a0", "rw_k_k", "rw_k_a", "rw_r_k", "rw_gn_w", "rw_gn_b")]
    o["rw_cst"] = np.stack([mu[0:8], mu[8:16], mu[16:24]] + vec).transpose(2, 1, 0)
    o["rw_mu_wg"] = mu[24:26].T
    sh = i["state_shift"][0].reshape(NB, 26, P)
    o["rw_sh_wg"] = sh[:, 24:26].transpose(2, 1, 0)
    o["rw_sh"] = sh[:, :24].reshape(NB, 3, PAIRS, P).transpose(2, 3, 1, 0)
    o["w2a2"] = np.concatenate([i["rw_w2"][0], i["rw_a2"][0]]).reshape(P, PAIRS, P).transpose(1, 0, 2)
    o["g2"] = i["rw_g2"][0].reshape(P, PAIRS, P).transpose(1, 0, 2)
    o["state_rwkv"] = i["state_rwkv"][0].reshape(NB, PAIRS, 2, RH, RH).transpose(1, 2, 4, 0, 3)
    wb = np.stack([i["w_b_gla"][0], i["w_b_rw"][0]])
    o["w_br"] = wb.reshape(2, KD, P, KD, P).transpose(3, 2, 0, 1, 4)
    o["w_out"] = i["w_out"][0].reshape(2, 4, P, D).transpose(0, 2, 1, 3).reshape(2, P, 4 * D)
    o["peer_wq"] = i["peer_wq"][0].reshape(KD, P, 2 * HEADS * P).transpose(1, 0, 2)
    o["peer_keys"] = i["peer_keys"][0].reshape(2 * HEADS, KEYS, P).transpose(2, 0, 1)
    o["peer_u"], o["peer_v"] = i["peer_u"][0], i["peer_v"][0]
    return {k: np.ascontiguousarray(v) for k, v in o.items()}


def kernel(**inputs):
    from concourse import bacc
    from concourse.bass_utils import run_bass_kernel_spmd

    nc = bacc.Bacc("TRN2", target_bir_lowering=False, num_devices=1)
    arrays = {**layout({k: np.asarray(v) for k, v in inputs.items()}), **masks()}
    t = {k: nc.dram_tensor(f"in_{k}", v.shape, F32, kind="ExternalInput").ap() for k, v in arrays.items()}
    for k, shape in OUTPUTS.items():
        t[k] = nc.dram_tensor(f"out_{k}", shape, F32, kind="ExternalOutput").ap()
    build(nc, t)
    r = run_bass_kernel_spmd(nc, [{f"in_{k}": v for k, v in arrays.items()}], core_ids=[0]).results[0]
    r = {k: r[f"out_{k}"] for k in OUTPUTS}
    y = r["y"]
    shift = r["new_shift"].transpose(3, 1, 0, 2).reshape(NSEQ, 3 * PAIRS * P)
    shift = np.concatenate([shift, r["new_shift_wg"].transpose(2, 0, 1).reshape(NSEQ, 2 * P)], 1)
    return (y[:SEQ].reshape(1, SEQ, D), y[SEQ:].reshape(NB, NT, D),
            r["new_gla_p"].reshape(1, 1, GH, P, GV),
            r["new_rw_p"].transpose(0, 1, 3, 2).reshape(1, 1, 2 * PAIRS, RH, RH),
            shift[0].reshape(1, 1, -1),
            r["new_gla_s"].transpose(2, 0, 1, 3).reshape(1, NB, GH, P, GV),
            r["new_rw_s"].transpose(3, 0, 1, 4, 2).reshape(1, NB, 2 * PAIRS, RH, RH),
            shift[1:].reshape(1, NB, -1))
```

```python
from contextlib import ExitStack

import numpy as np

import concourse.bass as bass
from concourse import mybir

F32 = mybir.dt.float32
U32 = mybir.dt.uint32
F32R = mybir.dt.float32r
ALU = mybir.AluOpType
ACT = mybir.ActivationFunctionType
AX = mybir.AxisListType

P = 128
D = 1024
KD = D // P
SEQ = 1024
NB, NT = 8, 4
NS = NB * NT
M = SEQ + NS
NSEQ = 1 + NB
G3 = M // 3
TILES = SEQ // P
NORM_EPS = 1e-6


S1, A1, G1, S2, A2, G2 = range(6)
HIGH_BITS = 0xFFFFF000


def split(eng, hi, lo, x, masked, link):
    link(eng.tensor_scalar(masked.bitcast(U32), x.bitcast(U32), HIGH_BITS, None, ALU.bitwise_and))
    eng.tensor_copy(hi, masked)
    link(eng.tensor_tensor(lo, x, masked, ALU.subtract))


def matmul3(pe, out, w, x, start, stop):
    pe.matmul(out, w[1], x[0], start=start, stop=False)
    pe.matmul(out, w[0], x[1], start=False, stop=False)
    return pe.matmul(out, w[0], x[0], start=False, stop=stop)


class Stage:

    def __init__(self, nc, ctx, name):
        self.nc, self.ctx, self.name = nc, ctx, name

    def sb(self, name, shape, dtype=F32):
        return self.ctx.enter_context(self.nc.sbuf_tensor(f"{self.name}_{name}", shape, dtype))

    def ps(self, name, shape=(P, 512)):
        return self.ctx.enter_context(self.nc.psum_tensor(f"{self.name}_{name}", list(shape), F32))

    def sem(self, name):
        return self.nc.alloc_semaphore(name=f"{self.name}_{name}")


class Chain:

    def __init__(self, eng, sem):
        self.eng, self.sem, self.base, self.n = eng, sem, 0, 0

    def link(self, ins):
        self.n += 1
        ins.then_inc(self.sem, 1)
        self.eng.wait_ge(self.sem, self.base + self.n)

    def enter(self, i, per):
        self.before, self.per = self.n, per
        self.base, self.n = self.n + i * per, 0

    def leave(self, count):
        assert self.n == self.per, (self.n, self.per)
        self.base, self.n = 0, self.before + count * self.per


def modulation(nc, t):
    CG = 12
    with ExitStack() as ctx:
        s = Stage(nc, ctx, "mod")
        cT = s.sb("cT", [P, KD * NSEQ])
        sg = s.sb("sg", [P, KD * NSEQ])
        w = s.sb("w", [P, 3, KD * 512])
        bias = s.sb("bias", [1, 6 * D])
        ones = s.sb("ones", [1, NSEQ])
        gains = s.sb("gains", [NSEQ, 4, D])
        out = s.sb("out", [NSEQ, 6, D])
        acc = s.ps("acc", [P, 4, 512])
        small_in = s.sem("small_in")
        w_in = [s.sem(f"w_in{n}") for n in range(3)]
        ready = s.sem("silu_ready")
        expd = s.sem("exp_done")
        summed = s.sem("summed")
        copied = s.sem("copied")
        done = s.sem("combined")
        stored = s.sem("stored")
        own = s.sem("vector_chain")
        with nc.Block() as block:
            @block.sync
            def _(sp):
                sp.dma_start(cT[:, :], t["cT"]).then_inc(small_in, 16)
                sp.dma_start(bias[:, :], t["b_ada"]).then_inc(small_in, 16)
                for n in range(4):
                    sp.dma_start(gains[:, n, :], t["gains"][n:n + 1, :].broadcast_to([NSEQ, D])).then_inc(small_in, 16)
                for g in range(CG):
                    if g >= 3:
                        sp.wait_ge(summed, g - 2)
                    sp.dma_start(w[:, g % 3, :], t["w_ada"][g]).then_inc(w_in[g % 3], 16)
                sp.wait_ge(done, 1)
                sp.dma_start(t["mod"], out[:, :, :]).then_inc(stored, 16)
                sp.wait_ge(stored, 16)

            @block.scalar
            def _(act):
                act.wait_ge(small_in, 96)
                act.activation(sg[:, :], cT[:, :], ACT.Exp, scale=-1.0).then_inc(expd, 1)
                for g in range(CG):
                    act.wait_ge(summed, g + 1)
                    act.copy(out[:, g // 2, (g % 2) * 512:(g % 2) * 512 + 512],
                             acc[0:NSEQ, g % 4, :]).then_inc(copied, 1)

            @block.vector
            def _(dve):
                ch = Chain(dve, own)
                ch.link(dve.memset(ones[:, :], 1.0))
                dve.wait_ge(expd, 1)
                ch.link(dve.tensor_scalar_add(sg[:, :], sg[:, :], 1.0))
                ch.link(dve.reciprocal(sg[:, :], sg[:, :]))
                dve.tensor_tensor(sg[:, :], sg[:, :], cT[:, :], ALU.mult).then_inc(ready, 1)
                dve.wait_ge(copied, CG)
                for n, row in ((0, 1), (2, 4)):
                    ch.link(dve.scalar_tensor_tensor(out=out[:, row, :], in0=out[:, row, :], scalar=1.0,
                                                     in1=gains[:, n, :], op0=ALU.add, op1=ALU.mult))
                ch.link(dve.tensor_tensor(out[:, 2, :], out[:, 2, :], gains[:, 1, :], ALU.mult))
                dve.tensor_tensor(out[:, 5, :], out[:, 5, :], gains[:, 3, :], ALU.mult).then_inc(done, 1)

            @block.tensor
            def _(pe):
                pe.wait_ge(ready, 1)
                for g in range(CG):
                    pe.wait_ge(w_in[g % 3], 16 * (g // 3 + 1))
                    if g >= 4:
                        pe.wait_ge(copied, g - 3)
                    for k in range(KD):
                        pe.matmul(acc[0:NSEQ, g % 4, :], sg[:, k * NSEQ:(k + 1) * NSEQ],
                                  w[:, g % 3, k * 512:(k + 1) * 512], start=(k == 0), stop=False)
                    pe.matmul(acc[0:NSEQ, g % 4, :], ones[0:1, :], bias[0:1, g * 512:(g + 1) * 512],
                              start=False, stop=True).then_inc(summed, 1)


def load_mod(eng, t, dst, row, samples, sem):
    if not samples:
        eng.dma_start(dst[:, :], t["mod"][0:1, row, :].broadcast_to([P, D])).then_inc(sem, 16)
        return
    for b in range(NB):
        eng.dma_start(dst[b * NT:(b + 1) * NT, :],
                      t["mod"][1 + b:2 + b, row, :].broadcast_to([NT, D])).then_inc(sem, 16)


def projection(nc, t):
    PT = t["w_in"].shape[0]
    W = 2
    ITER = PT // W
    assert ITER * W == PT
    with ExitStack() as ctx:
        s = Stage(nc, ctx, "proj")
        x = s.sb("x", [P, TILES, D])
        xs = s.sb("xs", [NS, D])
        h = s.sb("h", [P, 2, D])
        A, S = s.sb("A", [P, D]), s.sb("S", [P, D])
        As, Ss = s.sb("As", [NS, D]), s.sb("Ss", [NS, D])
        ident = s.sb("ident", [P, P])
        ssq = s.sb("ssq", [P, TILES + 1])
        eps = s.sb("eps", [P, 1])
        hT = [s.sb(f"hT_{part}", [P, KD, M], F32R) for part in ("high", "low")]
        w = s.sb("w", [P, W, KD, P])
        w2 = [s.sb(f"w_{part}", [P, W, KD, P], F32R) for part in ("high", "low")]
        wg = s.sb("wg", [P, KD, 16])
        wg2 = [s.sb(f"wg_{part}", [P, KD, 16], F32R) for part in ("high", "low")]
        masked = s.sb("masked", [P, KD, P])
        o = s.sb("o", [P, W, M])
        og = s.sb("og", [16, M])
        acc = [s.ps(f"acc{n}", [P, 3, 512]) for n in range(W)]
        consts_in, x_in, wg_in = s.sem("consts_in"), s.sem("x_in"), s.sem("wg_in")
        w_in = [s.sem(f"w_in{n}") for n in range(W)]
        cleared = s.sem("cleared")
        squared = s.sem("squared")
        h_ready = s.sem("h_ready")
        turned = s.sem("turned")
        hT_ready, w_split = s.sem("hT_ready"), s.sem("w_split")
        tile_done = s.sem("tile_done")
        first_out = s.sem("first_out")
        rest_out = s.sem("rest_out")
        stored = [s.sem(f"stored{n}") for n in range(W)]
        own, own_act = s.sem("vector_chain"), s.sem("scalar_chain")

        with nc.Block() as block:
            @block.sync
            def _(sp):
                sp.dma_start(x[:, :, :], t["x"][0:SEQ, :].rearrange("(i p) d -> p i d", p=P)).then_inc(x_in, 16)
                sp.dma_start(xs[:, :], t["x"][SEQ:M, :]).then_inc(x_in, 16)
                sp.dma_start(ident[:, :], t["ident"]).then_inc(consts_in, 16)
                load_mod(sp, t, A, A1, False, consts_in)
                load_mod(sp, t, S, S1, False, consts_in)
                load_mod(sp, t, As, A1, True, consts_in)
                load_mod(sp, t, Ss, S1, True, consts_in)
                sp.dma_start(wg[:, :, :], t["w_ga"]).then_inc(wg_in, 16)
                for n in range(W):
                    sp.dma_start(w[:, n, :, :], t["w_in"][n]).then_inc(w_in[n], 16)
                with sp.Fori(0, ITER - 1) as i:
                    for n in range(W):
                        sp.wait_ge(w_split, i * W + n + 1)
                        sp.dma_start(w[:, n, :, :], t["w_in"][i * W + (W + n)]).then_inc(w_in[n], 16)
                        sp.wait_ge(first_out, i * W + n + 1)
                        sp.wait_ge(rest_out, i * W + n + 1)
                        sp.dma_start(t["pT"][i * W + n], o[:, n, :]).then_inc(stored[n], 16)
                for n in range(W):
                    sp.wait_ge(first_out, (ITER - 1) * W + n + 1)
                    sp.wait_ge(rest_out, (ITER - 1) * W + n + 1)
                    sp.dma_start(t["pT"][PT - W + n], o[:, n, :]).then_inc(stored[n], 16)
                sp.wait_ge(first_out, PT + 1)
                sp.wait_ge(rest_out, PT + 1)
                sp.dma_start(t["gaT"], og[:, :]).then_inc(stored[0], 16)
                for n in range(W):
                    sp.wait_ge(stored[n], 16 * (ITER + (n == 0)))

            @block.scalar
            def _(act):
                ch = Chain(act, own_act)
                act.wait_ge(x_in, 32)
                act.wait_ge(cleared, 2)
                for i in range(TILES):
                    ch.link(act.activation(h[:, 0, :], x[:, i, :], ACT.Square, accum_out=ssq[:, i:i + 1]))
                ch.link(act.activation(h[0:NS, 0, :], xs[:, :], ACT.Square, accum_out=ssq[0:NS, TILES:TILES + 1]))
                ch.link(act.activation(ssq[:, :], ssq[:, :], ACT.Ln, bias=eps[:, :], scale=1.0 / D))
                act.activation(ssq[:, :], ssq[:, :], ACT.Exp, scale=-0.5).then_inc(squared, 1)

                def evacuate(i, first):
                    for n in range(W):
                        act.wait_ge(tile_done, i * W + n + 1)
                        if not first:
                            act.wait_ge(stored[n], i * 16)
                        act.copy(o[:, n, 0:G3], acc[n][:, 0, 0:G3]).then_inc(first_out, 1)

                evacuate(0, True)
                with act.Fori(1, ITER) as i:
                    evacuate(i, False)
                act.wait_ge(tile_done, PT + 1)
                act.copy(og[:, 0:G3], acc[0][0:16, 0, 0:G3]).then_inc(first_out, 1)

            @block.vector
            def _(dve):
                ch = Chain(dve, own)
                dve.memset(eps[:, :], NORM_EPS).then_inc(cleared, 1)
                dve.memset(ssq[:, :], 1.0).then_inc(cleared, 1)
                dve.wait_ge(consts_in, 16 * (3 + 2 * NB))
                dve.wait_ge(squared, 1)

                for n in range(W):
                    dve.wait_ge(w_in[n], 16)
                    split(dve, w2[0][:, n, :, :], w2[1][:, n, :, :], w[:, n, :, :], masked[:, :, :], ch.link)
                    dve.sem_inc(w_split, 1)
                dve.wait_ge(wg_in, 16)
                split(dve, wg2[0][:, :, :], wg2[1][:, :, :], wg[:, :, :], masked[:, :, 0:16], ch.link)

                def hidden(xi, r, Ai, Si, rows, n):
                    ch.link(dve.scalar_tensor_tensor(out=h[0:rows, n, :], in0=xi, scalar=r, in1=Ai,
                                                     op0=ALU.mult, op1=ALU.mult))
                    dve.tensor_tensor(h[0:rows, n, :], h[0:rows, n, :], Si, ALU.add).then_inc(h_ready, 1)

                def copy_hT(cols, n, rows):
                    for c in range(2):
                        split(dve, *(part[:, 4 * c:4 * c + 4, cols] for part in hT),
                              acc[n][:, c, 0:4 * rows].rearrange("p (k c) -> p k c", k=4), masked[:, 0:4, 0:rows], ch.link)
                    dve.sem_inc(hT_ready, 1)

                for n in range(2):
                    hidden(x[:, n, :], ssq[:, n:n + 1], A[:, :], S[:, :], P, n)
                with dve.Fori(0, TILES // 2 - 1) as i:
                    ch.enter(i, 10)
                    for n in range(2):
                        dve.wait_ge(turned, i * 2 + n + 1)
                        hidden(x[:, i * 2 + (2 + n), :], ssq[:, bass.ds(i * 2 + (2 + n), 1)], A[:, :], S[:, :], P, n)
                        copy_hT(bass.ts(i * 2 + n, P), n, P)
                    ch.leave(TILES // 2 - 1)
                dve.wait_ge(turned, TILES - 1)
                hidden(xs[:, :], ssq[0:NS, TILES:TILES + 1], As[:, :], Ss[:, :], NS, 0)
                copy_hT(slice(SEQ - 2 * P, SEQ - P), 0, P)
                dve.wait_ge(turned, TILES)
                copy_hT(slice(SEQ - P, SEQ), 1, P)
                dve.wait_ge(turned, TILES + 1)
                copy_hT(slice(SEQ, M), 0, NS)

                def split_w(i, n):
                    dve.wait_ge(w_in[n], i * 16 + 16)
                    split(dve, w2[0][:, n, :, :], w2[1][:, n, :, :], w[:, n, :, :], masked[:, :, :], ch.link)
                    dve.sem_inc(w_split, 1)

                def evacuate(i, first, more):
                    for n in range(W):
                        dve.wait_ge(tile_done, i * W + n + 1)
                        if more:
                            split_w(i + 1, n)
                        if not first:
                            dve.wait_ge(stored[n], i * 16)
                        dve.tensor_copy(o[:, n, G3:M].rearrange("p (g c) -> p g c", g=2),
                                        acc[n][:, 1:3, 0:G3]).then_inc(rest_out, 1)

                evacuate(0, True, True)
                with dve.Fori(1, ITER - 1) as i:
                    ch.enter(i - 1, 2 * W)
                    evacuate(i, False, True)
                    ch.leave(ITER - 2)
                evacuate(ITER - 1, False, False)
                dve.wait_ge(tile_done, PT + 1)
                dve.tensor_copy(og[:, G3:M].rearrange("p (g c) -> p g c", g=2),
                                acc[0][0:16, 1:3, 0:G3]).then_inc(rest_out, 1)

            @block.tensor
            def _(pe):
                def turn(n, rows):
                    for k in range(KD):
                        last = pe.transpose(acc[n][:, k // 4, (k % 4) * rows:(k % 4 + 1) * rows],
                                            h[0:rows, n, k * P:(k + 1) * P], ident[0:rows, 0:rows])
                    last.then_inc(turned, 1)

                for n in range(2):
                    pe.wait_ge(h_ready, n + 1)
                    turn(n, P)
                with pe.Fori(0, TILES // 2 - 1) as i:
                    for n in range(2):
                        pe.wait_ge(h_ready, i * 2 + (3 + n))
                        pe.wait_ge(hT_ready, i * 2 + (n + 1))
                        turn(n, P)
                pe.wait_ge(h_ready, TILES + 1)
                pe.wait_ge(hT_ready, TILES - 1)
                turn(0, NS)
                pe.wait_ge(hT_ready, TILES + 1)

                def project(n, wn, m):
                    for g in range(3):
                        for k in range(KD):
                            last = matmul3(pe, acc[n][0:m, g, 0:G3], [part[:, k, :] for part in wn],
                                           [part[:, k, g * G3:(g + 1) * G3] for part in hT],
                                           start=(k == 0), stop=(k == KD - 1))
                    last.then_inc(tile_done, 1)

                def tiles(i, first):
                    for n in range(W):
                        pe.wait_ge(w_split, i * W + n + 1)
                        if not first:
                            pe.wait_ge(first_out, (i - 1) * W + (n + 1))
                            pe.wait_ge(rest_out, (i - 1) * W + (n + 1))
                        project(n, [part[:, n, :, :] for part in w2], P)

                tiles(0, True)
                with pe.Fori(1, ITER) as i:
                    tiles(i, False)
                pe.wait_ge(first_out, PT - W + 1)
                pe.wait_ge(rest_out, PT - W + 1)
                project(0, wg2, 16)


GH, GV, GC = 4, 256, 64


def gla(nc, t):
    with ExitStack() as ctx:
        s = Stage(nc, ctx, "gla")
        ident = s.sb("ident", [P, P])
        mask = s.sb("mask", [P, P])
        mask_s = s.sb("mask_s", [NS, NS])
        seq_rows = s.sb("seq_rows", [NS, NB])
        starts = s.sb("starts", [P, M])
        gaT = s.sb("gaT", [16, M])
        wz = s.sb("wz", [16, P])
        cst = s.sb("cst", [P, 3])
        qkv = s.sb("qkv", [P, 4, M])
        gate = s.sb("gate", [P, 2, M])
        S_in = s.sb("S_in", [P, NB, GV])
        S_out = s.sb("S_out", [P, NB, GV])
        z = s.sb("z", [P, M])
        sp_ = s.sb("softplus", [P, M])
        B = s.sb("B", [P, M])
        up, dn, rest = s.sb("exp_up", [P, M]), s.sb("exp_down", [P, M]), s.sb("exp_rest", [P, M])
        ends = s.sb("ends", [P, SEQ // GC + NB])
        qe, ke, k2 = s.sb("qe", [P, M]), s.sb("ke", [P, M]), s.sb("k2", [P, M])
        S = s.sb("S", [P, 4, GV])
        kv = s.sb("kv", [P, 2, 3 * P])
        k2s = s.sb("k2s", [NS, NB, P])
        at = s.sb("at", [P, 2, P])
        o = s.sb("o", [P, 2, M])
        ones = s.sb("ones", [P, P])
        eps = s.sb("eps", [P, 1])
        zero = s.sb("zero", [P, 2 * M])
        zb = s.ps("zb", [P, 3, 512])
        at_b = s.ps("at_b")
        turn_b = s.ps("turn_b")
        o_b = s.ps("o_b")
        s_b = [s.ps(f"s_b{n}") for n in range(2)]
        N = TILES + 1
        CH = SEQ // GC
        consts_in, head_in = s.sem("consts_in"), s.sem("head_in")
        cleared = s.sem("cleared")
        z_summed, z_ready, softplus_ready = s.sem("z_summed"), s.sem("z_ready"), s.sem("softplus_ready")
        B_ready, exps_ready, scaled = s.sem("B_ready"), s.sem("exps_ready"), s.sem("scaled")
        turned, kv_ready = s.sem("turned"), s.sem("kv_ready")
        at_summed, at_ready = s.sem("at_summed"), s.sem("at_ready")
        k2s_ready = s.sem("k2s_ready")
        s_summed, S_ready = s.sem("s_summed"), s.sem("S_ready")
        o_summed, o_ready = s.sem("o_summed"), s.sem("o_ready")
        squares_ready, ms_summed, rstd_ready = s.sem("squares_ready"), s.sem("ms_summed"), s.sem("rstd_ready")
        og_ready, stored = s.sem("og_ready"), s.sem("stored")
        own, own_act = s.sem("vector_chain"), s.sem("scalar_chain")
        LOADS = 10
        STORES = 3
        US = CH + NB

        with nc.Block() as block:
            @block.sync
            def _(sp):
                for dst, name in ((ident, "ident"), (mask, "gla_mask"), (mask_s, "gla_mask_s"),
                                  (seq_rows, "seq_rows"), (starts, "starts"), (gaT, "gaT")):
                    src = t[name]
                    if name == "starts":
                        src = src[:, 0:M].broadcast_to([P, M])
                    sp.dma_start(dst[:, :], src).then_inc(consts_in, 16)

                def load(h):
                    sp.dma_start(wz[:, :], t["w_gate"][h]).then_inc(head_in, 16)
                    sp.dma_start(cst[:, :], t["gla_cst"][h]).then_inc(head_in, 16)
                    sp.dma_start(qkv[:, 0, :], t["pT"][h]).then_inc(head_in, 16)
                    sp.dma_start(qkv[:, 1, :], t["pT"][h + GH]).then_inc(head_in, 16)
                    for n in range(2):
                        sp.dma_start(qkv[:, 2 + n, :], t["pT"][h * 2 + (2 * GH + n)]).then_inc(head_in, 16)
                        sp.dma_start(gate[:, n, :], t["pT"][h * 2 + (4 * GH + n)]).then_inc(head_in, 16)
                    sp.dma_start(S_in[:, 0:4, :], t["state_gla"][h][:, 0:4, :]).then_inc(head_in, 16)
                    sp.dma_start(S_in[:, 4:8, :], t["state_gla"][h][:, 4:8, :]).then_inc(head_in, 16)

                def store(h):
                    sp.wait_ge(S_ready, (h + 1) * (US + 1))
                    sp.dma_start(t["new_gla_p"][h], S[:, CH % 4, :]).then_inc(stored, 16)
                    sp.dma_start(t["new_gla_s"][h], S_out[:, :, :]).then_inc(stored, 16)
                    sp.wait_ge(og_ready, h + 1)
                    sp.dma_start(t["ogT"][h], o[:, :, :]).then_inc(stored, 16)

                load(0)
                store(0)
                with sp.Fori(1, GH) as h:
                    load(h)
                    store(h)
                sp.wait_ge(stored, 16 * STORES * GH)

            @block.scalar
            def _(act):
                ch = Chain(act, own_act)
                act.wait_ge(cleared, 4)

                def head(h):
                    act.wait_ge(z_ready, h + 1)
                    ch.link(act.activation(sp_[:, :], z[:, :], ACT.Abs))
                    ch.link(act.activation(sp_[:, :], sp_[:, :], ACT.Exp, scale=-1.0))
                    act.activation(sp_[:, :], sp_[:, :], ACT.Ln, bias=1.0).then_inc(softplus_ready, 1)
                    act.wait_ge(B_ready, h + 1)
                    act.activation(up[:, :], B[:, :], ACT.Exp, scale=1.0 / 16)
                    act.activation(dn[:, :], B[:, :], ACT.Exp, scale=-1.0 / 16)
                    act.activation(rest[:, :], rest[:, :], ACT.Exp, scale=1.0 / 16)
                    act.activation(ends[:, 0:CH], B[:, 0:SEQ].rearrange("p (j c) -> p j c", c=GC)[:, :, GC - 1],
                                   ACT.Exp, scale=1.0 / 16)
                    act.activation(ends[:, CH:CH + NB], B[:, SEQ:M].rearrange("p (j c) -> p j c", c=NT)[:, :, NT - 1],
                                   ACT.Exp, scale=1.0 / 16).then_inc(exps_ready, 1)
                    for i in range(N):
                        act.wait_ge(turned, h * N + i + 1)
                        if i >= 2:
                            act.wait_ge(o_summed, h * N + i - 1)
                            act.wait_ge(s_summed, h * US + 2 * (i - 1))
                        rows = P if i < TILES else NS
                        act.copy(kv[0:rows, i % 2, :], turn_b[0:rows, 0:3 * P]).then_inc(kv_ready, 1)
                        if i:
                            copy_o(h, i - 1)
                    copy_o(h, N - 1)
                    act.wait_ge(o_ready, h * N + N)
                    act.activation(zero[:, :], o[:, :, :].rearrange("p a m -> p (a m)"), ACT.Square).then_inc(squares_ready, 1)
                    act.wait_ge(ms_summed, h + 1)
                    ch.link(act.activation(z[:, :].rearrange("p (g c) -> p g c", g=3), zb[:, :, 0:G3], ACT.Ln, bias=eps[:, :]))
                    act.activation(z[:, :], z[:, :], ACT.Exp, scale=-0.5)
                    act.activation(zero[:, :], gate[:, :, :].rearrange("p a m -> p (a m)"), ACT.Sigmoid).then_inc(rstd_ready, 1)

                def copy_o(h, i):
                    act.wait_ge(o_summed, h * N + i + 1)
                    rows = P if i < TILES else NS
                    act.copy(o[:, :, i * P:i * P + rows],
                             o_b[:, 0:2 * rows].rearrange("p (a c) -> p a c", a=2)).then_inc(o_ready, 1)

                ch.enter(0, 3)
                head(0)
                ch.leave(1)
                with act.Fori(1, GH) as h:
                    ch.enter(h - 1, 3)
                    act.wait_ge(stored, h * 16 * STORES)
                    head(h)
                    ch.leave(GH - 1)

            @block.vector
            def _(dve):
                ch = Chain(dve, own)
                dve.memset(ones[:, :], 1.0 / GV).then_inc(cleared, 1)
                dve.memset(eps[:, :], 1e-5).then_inc(cleared, 1)
                dve.memset(kv[:, :, :], 0.0).then_inc(cleared, 1)
                dve.memset(zero[:, :], 0.0).then_inc(cleared, 1)
                dve.wait_ge(consts_in, 16 * 6)
                PER = 6

                def head(h):
                    dve.wait_ge(head_in, (h + 1) * 16 * LOADS)
                    dve.wait_ge(z_summed, h + 1)
                    zv = z[:, :].rearrange("p (g c) -> p g c", g=3)
                    ch.link(dve.tensor_scalar(zv, zb[:, :, 0:G3], cst[:, 0:1], None, ALU.add))
                    dve.sem_inc(z_ready, 1)
                    dve.wait_ge(softplus_ready, h + 1)
                    ch.link(dve.scalar_tensor_tensor(out=sp_[:, :], in0=z[:, :], scalar=0.0, in1=sp_[:, :],
                                                     op0=ALU.min, op1=ALU.subtract))
                    ch.link(dve.tensor_tensor_scan(B[:, :], starts[:, :], sp_[:, :], 0.0, ALU.mult, ALU.add))
                    for c0, c1, c in ((0, SEQ, GC), (SEQ, M, NT)):
                        Bc = B[:, c0:c1].rearrange("p (j c) -> p j c", c=c)
                        last = dve.tensor_tensor(rest[:, c0:c1].rearrange("p (j c) -> p j c", c=c),
                                                 Bc[:, :, c - 1:c].broadcast_to([P, (c1 - c0) // c, c]), Bc, ALU.subtract)
                    ch.link(last)
                    dve.sem_inc(B_ready, 1)
                    dve.wait_ge(exps_ready, h + 1)
                    dve.scalar_tensor_tensor(out=qe[:, :], in0=qkv[:, 0, :], scalar=float(P) ** -0.5, in1=up[:, :],
                                             op0=ALU.mult, op1=ALU.mult).then_inc(scaled, 1)
                    dve.tensor_tensor(ke[:, :], qkv[:, 1, :], dn[:, :], ALU.mult).then_inc(scaled, 1)
                    dve.tensor_tensor(k2[:, :], qkv[:, 1, :], rest[:, :], ALU.mult).then_inc(scaled, 1)
                    dve.memset(S[:, 0, :], 0.0).then_inc(S_ready, 1)
                    for i in range(TILES):
                        dve.wait_ge(at_summed, h * N + i + 1)
                        if i >= 2:
                            dve.wait_ge(o_summed, h * N + i - 1)
                        dve.tensor_tensor(at[:, i % 2, :], at_b[:, 0:P], mask[:, :], ALU.mult).then_inc(at_ready, 1)
                        for j in (2 * i, 2 * i + 1):
                            dve.wait_ge(s_summed, h * US + j + 1)
                            dve.wait_ge(S_ready, h * (US + 1) + j + 1)
                            if j >= 4:
                                dve.wait_ge(o_summed, h * N + (j - 4) // 2 + 1)
                            dve.scalar_tensor_tensor(out=S[:, (j + 1) % 4, :], in0=S[:, j % 4, :],
                                                     scalar=ends[:, j:j + 1], in1=s_b[j % 2][:, 0:GV],
                                                     op0=ALU.mult, op1=ALU.add).then_inc(S_ready, 1)
                    dve.wait_ge(at_summed, h * N + N)
                    dve.tensor_tensor(at[0:NS, 0, 0:NS], at_b[0:NS, 0:NS], mask_s[:, :], ALU.mult).then_inc(at_ready, 1)
                    dve.wait_ge(kv_ready, h * N + N)
                    dve.tensor_tensor(k2s[:, :, :], kv[0:NS, 0, 0:P].unsqueeze(1).broadcast_to([NS, NB, P]),
                                      seq_rows[:, :].unsqueeze(2).broadcast_to([NS, NB, P]),
                                      ALU.mult).then_inc(k2s_ready, 1)
                    for b in range(NB):
                        dve.wait_ge(s_summed, h * US + CH + b + 1)
                        dve.scalar_tensor_tensor(out=S_out[:, b, :], in0=S_in[:, b, :], scalar=ends[:, CH + b:CH + b + 1],
                                                 in1=s_b[b % 2][:, 0:GV], op0=ALU.mult, op1=ALU.add).then_inc(S_ready, 1)
                    dve.wait_ge(rstd_ready, h + 1)
                    for n in range(2):
                        last = dve.scalar_tensor_tensor(out=gate[:, n, :], in0=gate[:, n, :], scalar=cst[:, 1 + n:2 + n],
                                                        in1=z[:, :], op0=ALU.mult, op1=ALU.mult)
                    ch.link(last)
                    gv = gate[:, :, :].rearrange("p a m -> p (a m)")
                    ov = o[:, :, :].rearrange("p a m -> p (a m)")
                    ch.link(dve.tensor_tensor(ov, ov, gv, ALU.mult))
                    dve.tensor_tensor(ov, ov, zero[:, :], ALU.mult).then_inc(og_ready, 1)

                ch.enter(0, PER)
                head(0)
                ch.leave(1)
                with dve.Fori(1, GH) as h:
                    dve.wait_ge(stored, h * 16 * STORES)
                    ch.enter(h - 1, PER)
                    head(h)
                    ch.leave(GH - 1)

            @block.tensor
            def _(pe):
                pe.wait_ge(consts_in, 16 * 6)
                pe.wait_ge(cleared, 4)

                def head(h, first):
                    pe.wait_ge(head_in, (h + 1) * 16 * LOADS)
                    if not first:
                        pe.wait_ge(rstd_ready, h)
                    for g in range(3):
                        last = pe.matmul(zb[:, g, 0:G3], wz[:, :], gaT[:, g * G3:(g + 1) * G3], start=True, stop=True)
                    last.then_inc(z_summed, 1)
                    pe.wait_ge(scaled, h * 3 + 3)

                    def start(i):
                        c0, rows = i * P, P if i < TILES else NS
                        if not first or i:
                            pe.wait_ge(kv_ready, h * N + i)
                            pe.wait_ge(at_ready, h * N + i)
                        for n, src in enumerate((k2[:, c0:c0 + rows], qkv[:, 2, c0:c0 + rows], qkv[:, 3, c0:c0 + rows])):
                            last = pe.transpose(turn_b[0:rows, n * P:(n + 1) * P], src, ident[:, :])
                        last.then_inc(turned, 1)
                        pe.matmul(at_b[0:rows, 0:rows], ke[:, c0:c0 + rows], qe[:, c0:c0 + rows],
                                  start=True, stop=True).then_inc(at_summed, 1)

                    def state(j, lhsT, rhs, k):
                        if not first or k >= 2:
                            done = h * (US + 1) + k if k >= 2 else h * (US + 1) - 2 + k + 1
                            pe.wait_ge(S_ready, done)
                        pe.matmul(s_b[k % 2][:, 0:GV], lhsT, rhs, start=True, stop=True).then_inc(s_summed, 1)

                    def finish(i):
                        pe.wait_ge(kv_ready, h * N + i + 1)
                        a = kv[:, i % 2, :]
                        if i < TILES:
                            for n in range(2):
                                state(n, a[64 * n:64 * n + 64, 0:P], a[64 * n:64 * n + 64, P:3 * P], 2 * i + n)
                        pe.wait_ge(at_ready, h * N + i + 1)
                        if not first or i:
                            pe.wait_ge(o_ready, h * N + i)
                        rows, c0 = (P, i * P) if i < TILES else (NS, SEQ)
                        for n in range(2):
                            pe.matmul(o_b[:, n * rows:(n + 1) * rows], a[0:rows, (1 + n) * P:(2 + n) * P],
                                      at[0:rows, i % 2, 0:rows], start=(n == 0), stop=False, skip_group_check=True)
                        if i < TILES:
                            for j in (2 * i, 2 * i + 1):
                                pe.wait_ge(S_ready, h * (US + 1) + j + 1)
                                for n in range(2):
                                    c = (j % 2) * GC
                                    last = pe.matmul(o_b[:, n * rows + c:n * rows + c + GC], S[:, j % 4, n * P:(n + 1) * P],
                                                     qe[:, j * GC:(j + 1) * GC], start=False, stop=True,
                                                     skip_group_check=True)
                        else:
                            for b in range(NB):
                                for n in range(2):
                                    last = pe.matmul(o_b[:, n * rows + b * NT:n * rows + (b + 1) * NT],
                                                     S_in[:, b, n * P:(n + 1) * P], qe[:, c0 + b * NT:c0 + (b + 1) * NT],
                                                     start=False, stop=True, skip_group_check=True)
                        last.then_inc(o_summed, 1)
                        if i == TILES:
                            pe.wait_ge(k2s_ready, h + 1)
                            for b in range(NB):
                                state(b, k2s[:, b, :], a[0:NS, P:3 * P], CH + b)

                    start(0)
                    for i in range(N):
                        if i + 1 < N:
                            start(i + 1)
                        finish(i)
                    pe.wait_ge(squares_ready, h + 1)
                    for g in range(3):
                        for n in range(2):
                            last = pe.matmul(zb[:, g, 0:G3], ones[:, :], zero[:, n * M + g * G3:n * M + (g + 1) * G3],
                                             start=(n == 0), stop=(n == 1))
                    last.then_inc(ms_summed, 1)

                head(0, True)
                with pe.Fori(1, GH) as h:
                    head(h, False)


RC, RH = 64, 64
PAIRS = 8
RW0 = 24
CHUNKS = SEQ // RC + 1
MW = CHUNKS * RC
QUADS = ((0, 4), (4, 4), (8, 4), (12, 4), (16, 1))
LEVELS = 5
DECAY = -float(np.exp(-0.5))


def rw_levels(q):
    return LEVELS if q < 4 else 1


def rw_duos(q):
    return 2 if q < 4 else 1


def rw_schedule(more):
    prep = {0: ["w", "lerp0"], 1: ["lerp1", "lerp2", "a", "kk", "scan"], 2: ["g", "km", "exps"],
            3: ["norm", "kkn"], 4: ["bonus"]}

    def free(q):
        yield ("gen", q, 0)
        for r in range(3):
            yield ("turn", q, r)
        if q == 0:
            yield ("keep", 0, 0)
        for l in range(rw_levels(q)):
            for kind in "PT":
                for d in range(rw_duos(q)):
                    yield (kind, q, (l, d))
        if more:
            for name in prep[q]:
                yield (name, q, 0)

    def sequential(q):
        c0, n = QUADS[q]
        for c in range(c0, c0 + n):
            for kind in "XUS":
                yield (kind, q, c)

    steps = list(free(0))
    for q in range(len(QUADS)):
        a, b = list(sequential(q)), list(free(q + 1)) if q + 1 < len(QUADS) else []
        order = [((n + 0.5) / len(a), 1, x) for n, x in enumerate(a)] + [((n + 0.5) / len(b), 0, x) for n, x in enumerate(b)]
        steps += [x for _, _, x in sorted(order, key=lambda o: o[:2])]
    return steps


def rwkv(nc, t):
    with ExitStack() as ctx:
        s = Stage(nc, ctx, "rw")
        ident = s.sb("ident", [P, P])
        strict = s.sb("strict", [P, 2, P])
        incl = s.sb("incl", [P, 2, RC])
        first_l = s.sb("first_l", [P, P])
        first_u = s.sb("first_u", [P, P])
        join = s.sb("join", [P, LEVELS, P])
        seq_cols = s.sb("seq_cols", [P, NB, P])
        seq_rows = s.sb("seq_rows", [P, NB])
        starts = s.sb("starts", [P, MW])
        heads = s.sb("heads", [P, P])
        mean = s.sb("mean", [P, P])
        cst_all = s.sb("cst_all", [P, PAIRS, 10])
        cst, norm_cst = s.sb("cst", [P, 11]), s.sb("norm_cst", [P, 2])
        mu_wg, sh_wg = s.sb("mu_wg", [P, 2]), s.sb("sh_wg", [P, 2, NB])
        raw = s.sb("raw", [P, 3, M])
        sh = s.sb("sh", [P, 3, NB])
        sho = s.sb("sho", [P, 3, NSEQ])
        wa = s.sb("wa", [P, M])
        gl = s.sb("gl", [P, M])
        w2a2, g2 = s.sb("w2a2", [P, P]), s.sb("g2", [P, P])
        rkv = s.sb("rkv", [P, 3, MW])
        d = s.sb("d", [P, M])
        sg, gt = s.sb("sg", [P, MW]), s.sb("gt", [P, M])
        av_all = s.sb("av", [P, MW])
        av = av_all[:, 0:M]
        gt_next = s.sb("gt_next", [P, M])
        Ls, Lp = s.sb("Ls", [P, MW]), sg
        Ei, Ed = s.sb("Ei", [P, MW]), s.sb("Ed", [P, MW])
        ends = s.sb("ends", [P, SEQ // RC + NB])
        kk, rn = s.sb("kk", [P, MW]), s.sb("rn", [P, M])
        km = s.sb("km", [P, M])
        bv = s.sb("bv", [P, M])
        ar = s.sb("ar", [P, 2, MW])
        aB, bB, kB, vB = (s.sb(n, [P, CHUNKS, P]) for n in ("aB", "bB", "kB", "vB"))
        abT = s.sb("abT", [P, 4, P])
        akT = s.sb("akT", [P, 2, 4, P])
        rbT, rkT = s.sb("rbT", [P, 2, 4, RC]), s.sb("rkT", [P, 2, 4, RC])
        nat = s.sb("nat", [P, 2, 3, 4, P])
        Tf = s.sb("Tf", [P, 2, 4, P])
        T = s.sb("T", [P, 2, 2, 2, P])
        Pm = s.sb("Pm", [P, 4, P])
        An = s.sb("An", [P, LEVELS, 4, P])
        Xs, Us = s.sb("Xs", [P, P]), s.sb("Us", [P, P])
        S, Su = s.sb("S", [P, 2, P]), s.sb("Su", [P, P])
        S_in, S_out = s.sb("S_in", [P, NB, P]), s.sb("S_out", [P, NB, P])
        a_seq = s.sb("a_seq", [P, NB, P])
        bk_seq = An[:, 1:LEVELS, :, :].rearrange("p l i s -> p (l i s)").rearrange("p (n b s) -> p n b s", n=2, b=NB)
        oT = s.sb("oT", [P, MW])
        eps = s.sb("eps", [P, 2])
        zb = s.ps("zb", [P, 3, 512])
        p_hi, turn_b, xu_b, s_b, o_b = (s.ps(n) for n in ("p_hi", "turn_b", "xu_b", "s_b", "o_b"))
        p_b = (zb[:, 0, :], p_hi[:, :])
        t_b = (zb[:, 1, :], zb[:, 2, :])
        x_b, u_b = xu_b[:, 0:P], xu_b[:, P:2 * P]

        NAMES = ("consts_in pair_in states_in cleared sho_ready lerped sg_ready av_ready gt_ready exps_ready "
                 "squares rn_ready vB_ready aB_ready kk_ready L_ready ss_ready km_ready scaled ar_ready bv_ready "
                 "cst_ready ends_ready kept d_squared out_stored w_summed gen_summed gen_ready abT_ready joins_ready turned nat_ready p_summed p_ready t_summed "
                 "T_ready x_summed x_ready u_summed u_ready s_summed S_ready o_summed o_ready a_seq_ready "
                 "bk_seq_ready d_ready rstd_ready out_ready shift_stored stored own own_act own_pool wa_ready "
                 "norm_summed").split()
        sem = {n: s.sem(n) for n in NAMES}
        (consts_in, pair_in, states_in, cleared, sho_ready, lerped, sg_ready, av_ready, gt_ready, exps_ready,
         squares, rn_ready, vB_ready, aB_ready, kk_ready, L_ready, ss_ready, km_ready, scaled, ar_ready, bv_ready,
         cst_ready, ends_ready, kept, d_squared, out_stored, w_summed, gen_summed, gen_ready, abT_ready, joins_ready, turned, nat_ready, p_summed, p_ready, t_summed,
         T_ready, x_summed, x_ready, u_summed, u_ready, s_summed, S_ready, o_summed, o_ready, a_seq_ready,
         bk_seq_ready, d_ready, rstd_ready, out_ready, shift_stored, stored, own, own_act, own_pool, wa_ready,
         norm_summed) = (sem[n] for n in NAMES)

        NQ, C = len(QUADS), CHUNKS
        NP = sum(rw_levels(q) * rw_duos(q) for q in range(NQ))
        NJ = sum(rw_levels(q) for q in range(NQ))
        NTR = NP + NQ
        NSS = (C - 1) + 2
        NSR = 1 + NSS
        ZS = 5
        CONSTS = 15
        PREP = ("w", "lerp0", "lerp1", "lerp2", "a", "kk", "scan", "g", "km", "exps", "norm", "kkn", "bonus")

        def p_at(q, l, d):
            return 10 * q + 2 * l + d + 1

        def T_at(q, l, d):
            return 11 * q + 1 + (2 * l + d + 1 if l >= 0 else 0)

        def last_at(at, q):
            return at(q, rw_levels(q) - 1, rw_duos(q) - 1)

        with nc.Block() as block:
            @block.sync
            def _(sp):
                for dst, name in ((ident, "ident"), (strict, "rw_strict"), (incl, "rw_incl"), (first_l, "rw_first_l"),
                                  (first_u, "rw_first_u"), (join, "rw_join"), (seq_cols, "rw_seq_cols"),
                                  (seq_rows, "rw_seq_rows"), (starts, "starts"), (heads, "rw_heads"), (mean, "rw_mean"),
                                  (cst_all, "rw_cst"), (mu_wg, "rw_mu_wg"), (sh_wg, "rw_sh_wg")):
                    src = t[name]
                    if name == "starts":
                        src = src.broadcast_to([P, MW])
                    if len(src.shape) == 3:
                        sp.dma_start(dst[:, :, :], src).then_inc(consts_in, 16)
                    else:
                        sp.dma_start(dst[:, :], src).then_inc(consts_in, 16)
                sp.dma_start(raw[:, 0:2, :], t["pT"][RW0 + 24:RW0 + 26].rearrange("n p m -> p n m")).then_inc(consts_in, 16)
                sp.wait_ge(sho_ready, 1)
                sp.dma_start(t["new_shift_wg"].rearrange("n p b -> p n b"), sho[:, 0:2, :]).then_inc(shift_stored, 16)
                sp.wait_ge(wa_ready, 1)
                sp.wait_ge(cleared, 13)

                def load(j):
                    for n in range(3):
                        sp.dma_start(raw[:, n, :], t["pT"][j + (RW0 + 8 * n)]).then_inc(pair_in, 16)
                    sp.dma_start(sh[:, :, :], t["rw_sh"][j]).then_inc(pair_in, 16)
                    sp.dma_start(w2a2[:, :], t["w2a2"][j]).then_inc(pair_in, 16)
                    sp.dma_start(g2[:, :], t["g2"][j]).then_inc(pair_in, 16)

                def load_states(j):
                    for n in range(2):
                        sp.dma_start(S_in[64 * n:64 * n + 64, :, 64 * n:64 * n + 64],
                                     t["state_rwkv"][j][n]).then_inc(states_in, 16)

                def middle(j):
                    sp.wait_ge(sho_ready, j + 2)
                    sp.dma_start(t["new_shift"][j].rearrange("n p b -> p n b"), sho[:, :, :]).then_inc(shift_stored, 16)

                def store(j):
                    sp.wait_ge(S_ready, (j + 1) * NSR)
                    for n in range(2):
                        a, b = 64 * n, 64 * n + 64
                        sp.dma_start(t["new_rw_p"][j][n], S[a:b, 0, a:b]).then_inc(stored, 16)
                        sp.dma_start(t["new_rw_s"][j][n], S_out[a:b, :, a:b]).then_inc(stored, 16)

                def store_out(j):
                    sp.wait_ge(out_ready, j + 1)
                    sp.dma_start(t["orT"][j], d[:, :]).then_inc(out_stored, 16)

                load(0)
                load_states(0)
                middle(0)
                sp.wait_ge(gt_ready, 1)
                sp.wait_ge(lerped, 3)
                load(1)
                def next_pair(j, more):
                    middle(j + 1)
                    if more:
                        sp.wait_ge(gt_ready, j + 2)
                        sp.wait_ge(lerped, j * 3 + 6)
                        load(j + 2)
                    store(j)
                    load_states(j + 1)
                    store_out(j)

                with sp.Fori(0, PAIRS - 2) as j:
                    next_pair(j, True)
                next_pair(PAIRS - 2, False)
                store(PAIRS - 1)
                store_out(PAIRS - 1)
                sp.wait_ge(shift_stored, 16 * (PAIRS + 1))
                sp.wait_ge(stored, 16 * 4 * PAIRS)
                sp.wait_ge(out_stored, 16 * PAIRS)

            def samples(ap):
                return ap[:, SEQ:M].rearrange("p (b c) -> p b c", c=NT)

            @block.scalar
            def _(act):
                ch = Chain(act, own_act)
                act.wait_ge(consts_in, 16 * CONSTS)
                act.copy(sho[:, 0:2, :], raw[:, 0:2, SEQ - 1:M:NT]).then_inc(sho_ready, 1)
                act.wait_ge(wa_ready, 1)
                act.activation(wa[0:64, :], wa[0:64, :], ACT.Tanh).then_inc(own_act, 1)
                act.activation(gl[:, :], gl[:, :], ACT.Sigmoid).then_inc(own_act, 1)

                def prep(name, j, first=False):
                    if name == "lerp0":
                        act.wait_ge(pair_in, (j + 1) * 16 * 6)
                        act.wait_ge(shift_stored, (j + 1) * 16)
                        act.copy(sho[:, :, :], raw[:, :, SEQ - 1:M:NT]).then_inc(sho_ready, 1)
                    elif name == "w":
                        act.wait_ge(w_summed, j * ZS + 1)
                        act.wait_ge(cst_ready, j + 1)
                        act.activation(sg[:, 0:M].rearrange("p (g c) -> p g c", g=3), zb[:, :, 0:G3], ACT.Sigmoid,
                                       bias=cst[:, 3:4]).then_inc(sg_ready, 1)
                    elif name == "a":
                        act.wait_ge(w_summed, j * ZS + 2)
                        act.activation(av[:, :].rearrange("p (g c) -> p g c", g=3), zb[:, :, 0:G3], ACT.Sigmoid,
                                       bias=cst[:, 4:5]).then_inc(av_ready, 1)
                    elif name == "g":
                        act.wait_ge(w_summed, j * ZS + 3)
                        if not first:
                            act.wait_ge(kept, j * 2)
                        act.copy(gt_next[:, :].rearrange("p (g c) -> p g c", g=3), zb[:, :, 0:G3]).then_inc(gt_ready, 1)
                    elif name == "kk":
                        act.wait_ge(kk_ready, j + 1)
                        act.activation(rn[:, :], kk[:, 0:M], ACT.Square).then_inc(squares, 1)
                    elif name == "exps":
                        act.wait_ge(L_ready, j + 1)
                        if not first:
                            act.wait_ge(ends_ready, j)
                        act.activation(Ei[:, :], Ls[:, :], ACT.Exp, scale=DECAY)
                        act.activation(Ed[:, :], Ls[:, :], ACT.Exp, scale=-DECAY)
                        act.activation(Lp[:, :], Lp[:, :], ACT.Exp, scale=DECAY).then_inc(exps_ready, 1)
                    elif name == "norm":
                        act.wait_ge(ss_ready, j + 1)
                        ch.link(act.activation(rn[:, :], rn[:, :], ACT.Ln, scale=2.0 ** 32))
                        act.activation(rn[:, :], rn[:, :], ACT.Exp, scale=-0.5, bias=eps[:, 1:2]).then_inc(rn_ready, 1)

                def expand(j):
                    act.wait_ge(exps_ready, j + 1)
                    act.copy(ends[:, 0:C - 1], Ei[:, RC - 1:SEQ:RC])
                    act.copy(ends[:, C - 1:C - 1 + NB], Ei[:, SEQ + NT - 1:M:NT]).then_inc(ends_ready, 1)
                    act.wait_ge(lerped, (j + 1) * 3)
                    for n in range(2):
                        a = 64 * n
                        act.copy(vB[a:a + 64, :, a:a + 64],
                                 rkv[a:a + 64, 2, :].rearrange("p (c s) -> p c s", s=RC)).then_inc(vB_ready, 1)
                    act.wait_ge(ar_ready, j + 1)
                    for n in range(2):
                        a = 64 * n
                        act.copy(aB[a:a + 64, :, a:a + 64],
                                 ar[a:a + 64, 0, :].rearrange("p (c s) -> p c s", s=RC)).then_inc(aB_ready, 1)

                def pair(j, first, more):
                    for kind, q, c in rw_schedule(more):
                        n = QUADS[q][1]
                        if kind == "turn":
                            act.wait_ge(turned, j * 3 * NQ + 3 * q + c + 1)
                            if q >= 2 and c == 0:
                                act.wait_ge(o_summed, j * C + 4 * (q - 1))
                            act.copy(nat[:, q % 2, c, 0:n, :],
                                     turn_b[:, 0:n * P].rearrange("p (i s) -> p i s", i=n)).then_inc(nat_ready, 1)
                        elif kind == "P":
                            (l, duo), m = c, min(n, 2)
                            act.wait_ge(p_summed, j * NP + p_at(q, l, duo))
                            act.copy(Pm[:, 2 * duo:2 * duo + m, :],
                                     p_b[duo][:, 0:m * P].rearrange("p (i s) -> p i s", i=m)).then_inc(p_ready, 1)
                        elif kind == "X":
                            act.wait_ge(x_summed, j * C + c + 1)
                            act.copy(Xs[:, :], x_b[:, 0:P]).then_inc(x_ready, 1)
                        elif kind == "S" and (c % 8 == 7 or c == C - 1):
                            act.wait_ge(o_summed, j * C + c + 1)
                            c0 = c // 8 * 8
                            act.copy(oT[:, c0 * RC:(c + 1) * RC], o_b[:, 0:(c + 1 - c0) * RC]).then_inc(o_ready, 1)
                        elif kind == "keep":
                            act.wait_ge(bv_ready, j + 1)
                            act.wait_ge(gt_ready, j + 1)
                            if not first:
                                act.wait_ge(out_ready, j)
                            act.copy(gt[:, :], gt_next[:, :]).then_inc(kept, 1)
                            act.copy(bv[:, :], km[:, :]).then_inc(kept, 1)
                        else:
                            prep(kind, j + 1)
                    act.wait_ge(d_ready, j + 1)
                    if more:
                        act.wait_ge(rn_ready, j + 2)
                    act.activation(rn[:, :], d[:, :], ACT.Square).then_inc(d_squared, 1)
                    if more:
                        expand(j + 1)
                    act.wait_ge(norm_summed, 2 * j + 2)
                    ch.link(act.activation(rn[:, :].rearrange("p (g c) -> p g c", g=3), zb[:, :, 0:G3], ACT.Ln,
                                           bias=eps[:, 0:1]))
                    act.activation(rn[:, :], rn[:, :], ACT.Exp, scale=-0.5).then_inc(rstd_ready, 1)

                ch.n = 2
                for name in PREP:
                    prep(name, 0, True)
                expand(0)
                ch.enter(0, 2)
                pair(0, True, True)
                ch.leave(1)
                with act.Fori(1, PAIRS - 1) as j:
                    ch.enter(j - 1, 2)
                    pair(j, False, True)
                    ch.leave(PAIRS - 2)
                pair(PAIRS - 1, False, False)

            @block.vector
            def _(dve):
                ch = Chain(dve, own)
                for buf in (aB, bB, kB, vB, S_in):
                    dve.memset(buf[:, :, :], 0.0).then_inc(cleared, 1)
                for buf in (rkv[:, 0, M:MW], rkv[:, 1, M:MW], rkv[:, 2, M:MW], sg[:, M:MW], kk[:, M:MW], av_all[:, M:MW]):
                    dve.memset(buf, 0.0).then_inc(cleared, 1)
                dve.memset(eps[:, 0:1], 64e-5).then_inc(cleared, 1)
                dve.memset(eps[:, 1:2], 16.0 * float(np.log(2.0))).then_inc(cleared, 1)
                dve.wait_ge(consts_in, 16 * CONSTS)
                dve.wait_ge(cleared, 13)

                def lerp(out, x, shift, mu):
                    dve.tensor_tensor(d[:, 1:SEQ], x[:, 0:SEQ - 1], x[:, 1:SEQ], ALU.subtract)
                    dve.tensor_scalar(d[:, 0:1], x[:, 0:1], -1.0, None, ALU.mult)
                    xs, ds = samples(x), samples(d)
                    dve.tensor_tensor(ds[:, :, 1:NT], xs[:, :, 0:NT - 1], xs[:, :, 1:NT], ALU.subtract)
                    ch.link(dve.tensor_tensor(ds[:, :, 0], shift, xs[:, :, 0], ALU.subtract))
                    return dve.scalar_tensor_tensor(out=out, in0=d[:, :], scalar=mu, in1=x, op0=ALU.mult, op1=ALU.add)

                ch.link(lerp(wa[:, :], raw[:, 0, :], sh_wg[:, 0, :], mu_wg[:, 0:1]))
                ch.link(lerp(gl[:, :], raw[:, 1, :], sh_wg[:, 1, :], mu_wg[:, 1:2]))
                dve.wait_ge(sho_ready, 1)
                dve.sem_inc(wa_ready, 1)

                def halves(out, x, y):
                    for n in range(2):
                        a = 64 * n
                        last = dve.tensor_tensor(out[a:a + 64, :, a:a + 64],
                                                 x[a:a + 64, :].rearrange("p (c s) -> p c s", s=RC),
                                                 y[a:a + 64, :].rearrange("p (c s) -> p c s", s=RC), ALU.mult)
                    return last

                g3 = lambda x: x.rearrange("p (g c) -> p g c", g=3)
                R, K, V = rkv[:, 0, :], rkv[:, 1, :], rkv[:, 2, :]

                def prep(name, j, first=False):
                    if name == "w":
                        ch.link(dve.tensor_copy(cst[:, 0:10], cst_all[:, 0, :] if first else
                                                cst_all[:, bass.ds(j, 1), :].rearrange("p o c -> p (o c)")))
                        ch.link(dve.tensor_scalar(cst[:, 10:11], cst[:, 6:7], -1.0, 1.0, ALU.mult, ALU.add))
                        dve.sem_inc(cst_ready, 1)
                    elif name[:4] == "lerp":
                        n = int(name[4])
                        if n == 0:
                            dve.wait_ge(pair_in, (j + 1) * 16 * 6)
                            if not first:
                                dve.wait_ge(scaled, j * 3)
                                dve.wait_ge(ar_ready, j)
                                dve.wait_ge(vB_ready, j * 2)
                        ch.link(lerp(rkv[:, n, 0:M], raw[:, n, :], sh[:, n, :], cst[:, n:n + 1]))
                        dve.sem_inc(lerped, 1)
                    elif name == "kk":
                        dve.tensor_scalar(kk[:, 0:M], K[:, 0:M], cst[:, 5:6], None, ALU.mult).then_inc(kk_ready, 1)
                    elif name == "scan":
                        dve.wait_ge(sg_ready, j + 1)
                        ch.link(dve.tensor_tensor_scan(Ls[:, :], starts[:, :], sg[:, :], 0.0, ALU.mult, ALU.add))
                        dve.tensor_tensor(Lp[:, :], Ls[:, :], sg[:, :], ALU.subtract).then_inc(L_ready, 1)
                    elif name == "km":
                        dve.wait_ge(av_ready, j + 1)
                        if not first:
                            dve.wait_ge(kept, j * 2)
                        ch.link(dve.tensor_scalar(km[:, :], av[:, :], cst[:, 6:7], cst[:, 10:11], ALU.mult, ALU.add))
                        ch.link(dve.tensor_tensor(K[:, 0:M], K[:, 0:M], km[:, :], ALU.mult))
                        dve.scalar_tensor_tensor(out=km[:, :], in0=R[:, 0:M], scalar=cst[:, 7:8], in1=K[:, 0:M],
                                                 op0=ALU.mult, op1=ALU.mult).then_inc(km_ready, 1)
                    elif name == "norm":
                        dve.wait_ge(w_summed, j * ZS + 4)
                        dve.tensor_scalar(g3(rn[:, :]), zb[:, :, 0:G3], 1e-24, None, ALU.max).then_inc(ss_ready, 1)
                    elif name == "kkn":
                        dve.wait_ge(rn_ready, j + 1)
                        ch.link(dve.tensor_tensor(kk[:, 0:M], kk[:, 0:M], rn[:, :], ALU.mult))
                        ch.link(dve.tensor_tensor(av[:, :], kk[:, 0:M], av[:, :], ALU.mult))
                    elif name == "bonus":
                        dve.wait_ge(w_summed, j * ZS + 5)
                        dve.tensor_tensor(g3(km[:, :]), g3(V[:, 0:M]), zb[:, :, 0:G3], ALU.mult).then_inc(bv_ready, 1)

                def expand(j):
                    dve.wait_ge(exps_ready, j + 1)
                    dve.scalar_tensor_tensor(out=ar[:, 0, :], in0=kk[:, :], scalar=-1.0, in1=Lp[:, :],
                                             op0=ALU.mult, op1=ALU.mult).then_inc(ar_ready, 1)
                    dve.tensor_tensor(ar[:, 1, :], R, Ei[:, :], ALU.mult).then_inc(scaled, 1)
                    halves(kB, K, Ed).then_inc(scaled, 1)
                    halves(bB, av_all, Ed).then_inc(scaled, 1)

                def pair(j, first, more):
                    if not first:
                        dve.wait_ge(stored, j * 16 * 4)
                    ch.link(dve.memset(S[:, 0, :], 0.0))
                    dve.sem_inc(S_ready, 1)
                    ch.link(dve.tensor_copy(norm_cst[:, :], cst[:, 8:10]))
                    dve.wait_ge(ends_ready, j + 1)
                    for kind, q, c in rw_schedule(more):
                        n = QUADS[q][1]
                        smp = q == NQ - 1
                        b4 = lambda ap: ap.rearrange("p (i s) -> p i s", i=n)
                        if kind == "gen":
                            dve.wait_ge(gen_summed, j * NQ + q + 1)
                            if q >= 2:
                                dve.wait_ge(o_summed, j * C + 4 * (q - 1))
                            if q or not first:
                                dve.wait_ge(joins_ready, j * NJ + LEVELS * q)
                            for bank, big, small in ((0, abT[:, 0:n, :], rbT), (1, akT[:, q % 2, 0:n, :], rkT)):
                                src = zb[:, bank, 0:n * P].rearrange("p (i a s) -> p i a s", i=n, a=2)
                                if n > 1:
                                    for h2 in range(2):
                                        last = dve.tensor_tensor(big[:, :, h2 * RC:(h2 + 1) * RC], src[:, :, 0, :],
                                                                 strict[:, 0, h2 * RC:(h2 + 1) * RC].unsqueeze(1).broadcast_to([P, n, RC]),
                                                                 ALU.mult)
                                    last2 = dve.tensor_tensor(small[:, q % 2, 0:n, :], src[:, :, 1, :],
                                                              incl[:, 0, :].unsqueeze(1).broadcast_to([P, n, RC]), ALU.mult)
                                else:
                                    for h2 in range(2):
                                        last = dve.tensor_tensor(big[:, 0, h2 * RC:(h2 + 1) * RC], src[:, 0, 0, :],
                                                                 strict[:, 1, h2 * RC:(h2 + 1) * RC], ALU.mult)
                                    last2 = dve.tensor_tensor(small[:, q % 2, 0, :], src[:, 0, 1, :], incl[:, 1, :], ALU.mult)
                                if bank == 0:
                                    ch.link(last)
                                    dve.sem_inc(abT_ready, 1)
                            if n > 1:
                                form = lambda ap: ap.rearrange("p (d c) s -> p d c s", c=2)
                                Tv, TTv = T[:, :, 0, :, :], T[:, :, 1, :, :]
                            else:
                                form = lambda ap: ap
                                Tv, TTv = T[:, 0, 0, 0:1, :], T[:, 0, 1, 0:1, :]
                            each = lambda ap: form(ap.unsqueeze(1).broadcast_to([P, n, P]))
                            dve.tensor_tensor(Tv, form(b4(zb[:, 2, 0:n * P])), each(first_l[:, :]), ALU.mult)
                            ch.link(dve.tensor_tensor(TTv, form(abT[:, 0:n, :]), each(first_u[:, :]), ALU.mult))
                            dve.sem_inc(gen_ready, 1)
                            dve.tensor_tensor(Tv, Tv, each(ident[:, :]), ALU.add)
                            dve.tensor_tensor(TTv, TTv, each(ident[:, :]), ALU.add).then_inc(T_ready, 1)
                        elif kind == "T":
                            (l, duo), m = c, min(n, 2)
                            dve.wait_ge(t_summed, j * NP + p_at(q, l, duo))
                            if l + 1 < rw_levels(q):
                                Td = T[:, duo, :, :, :].rearrange("p a c s -> p (a c s)")
                                dve.tensor_tensor(Td, Td, t_b[duo], ALU.add).then_inc(T_ready, 1)
                            else:
                                dve.tensor_tensor(Tf[:, q % 2, 2 * duo:2 * duo + m, :], T[:, duo, 1, 0:m, :],
                                                  t_b[duo][:, 2 * P:(2 + m) * P].rearrange("p (i s) -> p i s", i=m),
                                                  ALU.add).then_inc(T_ready, 1)
                        elif kind == "U":
                            dve.wait_ge(u_summed, j * C + c + 1)
                            dve.tensor_copy(Us[:, :], u_b[:, 0:P]).then_inc(u_ready, 1)
                        elif kind == "X" and not smp:
                            dve.wait_ge(S_ready, j * NSR + c + 1)
                            ch.link(dve.tensor_scalar(Su[:, :], S[:, c % 2, :], ends[:, c:c + 1], None, ALU.mult))
                        elif kind == "S" and not smp:
                            dve.wait_ge(s_summed, j * NSS + c + 1)
                            dve.scalar_tensor_tensor(out=S[:, (c + 1) % 2, :], in0=s_b[:, 0:P], scalar=ends[:, c:c + 1],
                                                     in1=Su[:, :], op0=ALU.mult, op1=ALU.add).then_inc(S_ready, 1)
                        elif kind == "S":
                            for h in range(2):
                                dve.wait_ge(s_summed, j * NSS + c + h + 1)
                                four = slice(4 * h, 4 * h + 4)
                                ch.link(dve.tensor_tensor(S_out[:, four, :], S_in[:, four, :],
                                                          (s_b, xu_b)[h][:, :].rearrange("p (b s) -> p b s", b=4), ALU.add))
                                dve.tensor_tensor(S_out[:, four, :], S_out[:, four, :],
                                                  ends[:, C - 1 + 4 * h:C + 3 + 4 * h].unsqueeze(2).broadcast_to([P, 4, P]),
                                                  ALU.mult).then_inc(S_ready, 1)
                        elif kind[:4] not in ("turn", "keep", "P", "X"):
                            if kind == "lerp0" and not first:
                                dve.wait_ge(out_stored, j * 16)
                            prep(kind, j + 1)
                    dve.wait_ge(norm_summed, 2 * j + 1)
                    if not more:
                        dve.wait_ge(out_stored, j * 16)
                    dve.tensor_tensor(g3(d[:, :]), g3(oT[:, 0:M]), zb[:, :, 0:G3], ALU.subtract).then_inc(d_ready, 1)
                    if more:
                        expand(j + 1)
                    dve.wait_ge(rstd_ready, j + 1)
                    ch.link(dve.tensor_tensor(d[:, :], d[:, :], rn[:, :], ALU.mult))
                    ch.link(dve.tensor_scalar(d[:, :], d[:, :], norm_cst[:, 0:1], norm_cst[:, 1:2], ALU.mult, ALU.add))
                    ch.link(dve.tensor_tensor(d[:, :], d[:, :], bv[:, :], ALU.add))
                    dve.tensor_tensor(d[:, :], d[:, :], gt[:, :], ALU.mult).then_inc(out_ready, 1)

                for name in PREP:
                    prep(name, 0, True)
                expand(0)
                PER = 46
                ch.enter(0, PER)
                pair(0, True, True)
                ch.leave(1)
                with dve.Fori(1, PAIRS - 1) as j:
                    ch.enter(j - 1, PER)
                    pair(j, False, True)
                    ch.leave(PAIRS - 2)
                pair(PAIRS - 1, False, False)

            @block.gpsimd
            def _(pool):
                pool.wait_ge(consts_in, 16 * CONSTS)

                def pair(j, first):
                    for kind, q, c in rw_schedule(False):
                        n = QUADS[q][1]
                        if kind == "gen":
                            pool.wait_ge(abT_ready, j * NQ + q + 1)
                            if q or not first:
                                pool.wait_ge(p_summed, j * NP + 10 * q)
                            if not first and q == 0:
                                pool.wait_ge(s_summed, j * NSS)
                            for l in range(rw_levels(q)):
                                pool.tensor_tensor(An[:, l, 0:n, :], abT[:, 0:n, :],
                                                   join[:, l, :].unsqueeze(1).broadcast_to([P, n, P]),
                                                   ALU.mult).then_inc(joins_ready, 1)
                    pool.wait_ge(aB_ready, 2 * (j + 1))
                    if not first:
                        pool.wait_ge(s_summed, j * NSS)
                    pool.tensor_tensor(a_seq[:, :, :], aB[:, C - 1, :].unsqueeze(1).broadcast_to([P, NB, P]),
                                       seq_cols[:, :, :], ALU.mult).then_inc(a_seq_ready, 1)
                    pool.wait_ge(nat_ready, (j + 1) * 3 * NQ)
                    for n in range(2):
                        last = pool.tensor_tensor(bk_seq[:, n, :, :],
                                                  nat[:, (NQ - 1) % 2, n, 0, :].unsqueeze(1).broadcast_to([P, NB, P]),
                                                  seq_rows[:, :].unsqueeze(2).broadcast_to([P, NB, P]), ALU.mult)
                    last.then_inc(bk_seq_ready, 1)

                pair(0, True)
                with pool.Fori(1, PAIRS) as j:
                    pair(j, False)

            @block.tensor
            def _(pe):
                pe.wait_ge(consts_in, 16 * CONSTS)
                pe.wait_ge(cleared, 13)
                pe.wait_ge(own_act, 2)

                def sum3(lhsT, rhs, sem):
                    for g in range(3):
                        last = pe.matmul(zb[:, g, 0:G3], lhsT, rhs[:, g * G3:(g + 1) * G3], start=True, stop=True)
                    last.then_inc(sem, 1)

                def prep(name, j):
                    if name == "w":
                        pe.wait_ge(pair_in, (j + 1) * 16 * 6)
                        sum3(w2a2[0:64, :], wa[0:64, :], w_summed)
                    elif name == "a":
                        pe.wait_ge(sg_ready, j + 1)
                        sum3(w2a2[64:128, :], wa[64:128, :], w_summed)
                    elif name == "g":
                        pe.wait_ge(av_ready, j + 1)
                        sum3(g2[:, :], gl[:, :], w_summed)
                    elif name == "norm":
                        pe.wait_ge(gt_ready, j + 1)
                        pe.wait_ge(squares, j + 1)
                        sum3(heads[:, :], rn[:, :], w_summed)
                    elif name == "bonus":
                        pe.wait_ge(ss_ready, j + 1)
                        pe.wait_ge(km_ready, j + 1)
                        sum3(heads[:, :], km[:, :], w_summed)

                def pair(j, first, more):
                    pe.wait_ge(bv_ready, j + 1)
                    if not first:
                        pe.wait_ge(rstd_ready, j)
                    pe.wait_ge(scaled, 3 * (j + 1))
                    pe.wait_ge(aB_ready, 2 * (j + 1))
                    pe.wait_ge(vB_ready, 2 * (j + 1))
                    for kind, q, c in rw_schedule(more):
                        c0, n = QUADS[q]
                        if kind in ("w", "a", "g", "norm", "bonus"):
                            pe.wait_ge(p_ready, j * NP + last_at(p_at, q))
                            pe.wait_ge(T_ready, j * NTR + last_at(T_at, q))
                            prep(kind, j + 1)
                        if kind == "gen":
                            if q:
                                pe.wait_ge(p_ready, j * NP + last_at(p_at, q - 1))
                                pe.wait_ge(T_ready, j * NTR + last_at(T_at, q - 1))
                                if more:
                                    pe.wait_ge((sg_ready, av_ready, gt_ready, ss_ready)[q - 1], j + 2)
                            for i in range(n):
                                cols = slice((c0 + i) * RC, (c0 + i + 1) * RC)
                                dst = slice(i * P, (i + 1) * P)
                                pe.matmul(zb[:, 0, dst], bB[:, c0 + i, :], ar[:, :, cols], start=True, stop=True)
                                pe.matmul(zb[:, 1, dst], kB[:, c0 + i, :], ar[:, :, cols], start=True, stop=True)
                                last = pe.matmul(zb[:, 2, dst], aB[:, c0 + i, :], bB[:, c0 + i, :], start=True, stop=True)
                            last.then_inc(gen_summed, 1)
                        elif kind == "turn":
                            if q or c or not first:
                                pe.wait_ge(nat_ready, j * 3 * NQ + 3 * q + c)
                            for i in range(n):
                                last = pe.transpose(turn_b[:, i * P:(i + 1) * P], (bB, kB, vB)[c][:, c0 + i, :], ident[:, :])
                            last.then_inc(turned, 1)
                        elif kind == "P":
                            pe.wait_ge(gen_ready, j * NQ + q + 1)
                            pe.wait_ge(joins_ready, j * NJ + LEVELS * q + c[0] + 1)
                            l, duo = c
                            pe.wait_ge(T_ready, j * NTR + T_at(q, l - 1, duo))
                            for i in range(min(n, 2)):
                                last = pe.matmul(p_b[duo][:, i * P:(i + 1) * P], An[:, l, 2 * duo + i, :], T[:, duo, 0, i, :],
                                                 start=True, stop=True)
                            last.then_inc(p_summed, 1)
                        elif kind == "T":
                            l, duo = c
                            pe.wait_ge(p_ready, j * NP + p_at(q, l, duo))
                            for i in range(min(n, 2)):
                                if l + 1 < rw_levels(q):
                                    pe.matmul(t_b[duo][:, i * P:(i + 1) * P], T[:, duo, 1, i, :], Pm[:, 2 * duo + i, :],
                                              start=True, stop=True)
                                last = pe.matmul(t_b[duo][:, (2 + i) * P:(3 + i) * P], Pm[:, 2 * duo + i, :], T[:, duo, 1, i, :],
                                                 start=True, stop=True)
                            last.then_inc(t_summed, 1)
                        elif kind == "X":
                            i, b2 = c - c0, q % 2
                            pe.wait_ge(T_ready, j * NTR + T_at(q, rw_levels(q) - 1, i // 2))
                            pe.wait_ge(nat_ready, j * 3 * NQ + 3 * q + 3)
                            if c or not first:
                                pe.wait_ge(x_ready, j * C + c)
                            if c < C - 1:
                                pe.wait_ge(S_ready, j * NSR + c + 1)
                                pe.matmul(x_b[:, 0:P], aB[:, c, :], S[:, c % 2, :], start=True, stop=False)
                            else:
                                pe.wait_ge(states_in, (j + 1) * 32)
                                pe.wait_ge(a_seq_ready, j + 1)
                                for b in range(NB):
                                    pe.matmul(x_b[:, 0:P], a_seq[:, b, :], S_in[:, b, :], start=(b == 0), stop=False)
                            pe.matmul(x_b[:, 0:P], akT[:, b2, i, :], nat[:, b2, 2, i, :], start=False,
                                      stop=True).then_inc(x_summed, 1)
                        elif kind == "U":
                            pe.wait_ge(x_ready, j * C + c + 1)
                            if c or not first:
                                pe.wait_ge(u_ready, j * C + c)
                            pe.matmul(u_b[:, 0:P], Tf[:, q % 2, c - c0, :], Xs[:, :], start=True, stop=True).then_inc(u_summed, 1)
                        elif kind == "S":
                            i, b2, o0 = c - c0, q % 2, (c % 8) * RC
                            pe.wait_ge(u_ready, j * C + c + 1)
                            if c < C - 1:
                                pe.matmul(s_b[:, 0:P], nat[:, b2, 0, i, :], Us[:, :], start=True, stop=False)
                                pe.matmul(s_b[:, 0:P], nat[:, b2, 1, i, :], nat[:, b2, 2, i, :], start=False,
                                          stop=True).then_inc(s_summed, 1)
                            if c % 8 == 0 and (c or not first):
                                pe.wait_ge(o_ready, 3 * j + c // 8)
                            cols = slice(c * RC, (c + 1) * RC)
                            pe.matmul(o_b[:, o0:o0 + RC], Us[:, :], rbT[:, b2, i, :], start=True, stop=False)
                            if c < C - 1:
                                pe.matmul(o_b[:, o0:o0 + RC], S[:, c % 2, :], ar[:, 1, cols], start=False, stop=False)
                            else:
                                for b in range(NB):
                                    pe.matmul(o_b[:, b * NT:(b + 1) * NT], S_in[:, b, :],
                                              ar[:, 1, SEQ + b * NT:SEQ + (b + 1) * NT], start=False, stop=False,
                                              skip_group_check=True)
                            pe.matmul(o_b[:, o0:o0 + RC], nat[:, b2, 2, i, :], rkT[:, b2, i, :], start=False,
                                      stop=True).then_inc(o_summed, 1)
                            if c == C - 1:
                                pe.wait_ge(bk_seq_ready, j + 1)
                                pe.wait_ge(S_ready, j * NSR + c + 1)
                                for b in range(NB):
                                    dst = (s_b, xu_b)[b // 4][:, (b % 4) * P:(b % 4 + 1) * P]
                                    pe.matmul(dst, bk_seq[:, 0, b, :], Us[:, :], start=True, stop=False)
                                    last = pe.matmul(dst, bk_seq[:, 1, b, :], nat[:, b2, 2, i, :], start=False, stop=True)
                                    if b % 4 == 3:
                                        last.then_inc(s_summed, 1)
                    pe.wait_ge(o_ready, 3 * (j + 1))
                    pe.wait_ge(T_ready, (j + 1) * NTR)
                    pe.wait_ge(p_ready, (j + 1) * NP)
                    if more:
                        pe.wait_ge(bv_ready, j + 2)
                    sum3(mean[:, :], oT[:, 0:M], norm_summed)
                    pe.wait_ge(d_squared, j + 1)
                    sum3(mean[:, :], rn[:, :], norm_summed)

                for name in PREP:
                    prep(name, 0)
                pair(0, True, True)
                with pe.Fori(1, PAIRS - 1) as j:
                    pair(j, False, True)
                pair(PAIRS - 1, False, False)


MP = (TILES + 1) * P


def merge(nc, t):
    with ExitStack() as ctx:
        s = Stage(nc, ctx, "mg")
        br = s.sb("br", [P, 2, KD, M])
        mT = s.sb("mT", [P, KD, M])
        w = s.sb("w", [P, 2, 2, KD, P])
        gt = s.sb("gt", [P, 2, M])
        tmp = s.sb("tmp", [P, 2, M])
        MW_ = [s.ps(f"acc{n}", [P, 3, 512]) for n in range(2)]
        acc = MW_
        consts_in, g_in = s.sem("consts_in"), s.sem("g_in")
        w_in = [s.sem(f"w_in{n}") for n in range(2)]
        gates_ready, gated, merged = s.sem("gates_ready"), s.sem("gated"), s.sem("merged")
        summed = [s.sem(f"summed{n}") for n in range(2)]
        own, own_act = s.sem("vector_chain"), s.sem("scalar_chain")
        with nc.Block() as block:
            @block.sync
            def _(sp):
                sp.dma_start(br[:, 0, :, :].rearrange("p (h a) m -> p h a m", a=2),
                             t["ogT"].rearrange("h p a m -> p h a m")).then_inc(consts_in, 16)
                sp.dma_start(br[:, 1, :, :], t["orT"].rearrange("j p m -> p j m")).then_inc(consts_in, 16)
                for n in range(2):
                    sp.dma_start(w[:, n, :, :, :], t["w_br"][n]).then_inc(w_in[n], 16)

                def gates(j):
                    for b in range(2):
                        sp.dma_start(gt[:, b, :], t["pT"][j + (50 + KD * b)]).then_inc(g_in, 16)

                gates(0)
                with sp.Fori(0, KD // 2 - 1) as i:
                    for n in range(2):
                        sp.wait_ge(merged, i * 2 + n + 1)
                        gates(i * 2 + (n + 1))
                        sp.dma_start(w[:, n, :, :, :], t["w_br"][i * 2 + (n + 2)]).then_inc(w_in[n], 16)
                sp.wait_ge(merged, KD - 1)
                gates(KD - 1)

            @block.scalar
            def _(act):
                with act.Fori(0, KD) as i:
                    act.wait_ge(g_in, i * 32 + 32)
                    act.activation(gt[:, :, :], gt[:, :, :], ACT.Sigmoid).then_inc(gates_ready, 1)

            @block.vector
            def _(dve):
                g3 = lambda x: x.rearrange("p (g c) -> p g c", g=3)
                with dve.Fori(0, KD) as i:
                    dve.wait_ge(gates_ready, i + 1)
                    for b in range(2):
                        dve.wait_ge(summed[b], i + 1)
                        dve.tensor_tensor(g3(tmp[:, b, :]), acc[b][:, :, 0:G3], g3(gt[:, b, :]), ALU.mult).then_inc(gated, 1)
                    dve.wait_ge(gated, i * 2 + 2)
                    dve.tensor_tensor(mT[:, i, :], tmp[:, 0, :], tmp[:, 1, :], ALU.add).then_inc(merged, 1)
                    dve.wait_ge(merged, i + 1)

            @block.tensor
            def _(pe):
                pe.wait_ge(consts_in, 32)

                def tiles(i, first):
                    for n in range(2):
                        pe.wait_ge(w_in[n], i * 16 + 16)
                        for b in range(2):
                            if not first or n:
                                pe.wait_ge(gated, i * 4 + (2 * n - 1 + b))
                            for g in range(3):
                                for k in range(KD):
                                    last = pe.matmul(acc[b][:, g, 0:G3], w[:, n, b, k, :],
                                                     br[:, b, k, g * G3:(g + 1) * G3], start=(k == 0), stop=(k == KD - 1))
                            last.then_inc(summed[b], 1)

                tiles(0, True)
                with pe.Fori(1, KD // 2) as i:
                    tiles(i, False)

        with ExitStack() as ctx2:
            s = Stage(nc, ctx2, "out")
            w_out = w[:, :, :, :, :].rearrange("p a b k c -> p (a b k c)")[:, 0:4 * D]
            w_hi = s.sb("w_hi", [P, 4, D])
            rhs = lambda k, c: (w_out[:, k * D + c:k * D + c + 512] if k < 4 else w_hi[:, k - 4, c:c + 512])
            mod = s.sb("mod", [P, 3, D])
            free = br[:, :, :, :].rearrange("p a k m -> p (a k m)")
            mod_s = free[0:NS, 0:3 * D].rearrange("p (r c) -> p r c", r=3)
            x = free[:, 3 * D:5 * D].rearrange("p (n c) -> p n c", n=2)
            mt = free[:, 5 * D:7 * D].rearrange("p (n k c) -> p n k c", n=2, k=KD)
            x2 = free[:, 7 * D:9 * D].rearrange("p (n c) -> p n c", n=2)
            h2 = free[:, 9 * D:11 * D].rearrange("p (n c) -> p n c", n=2)
            sq = free[:, 11 * D:12 * D]
            ss = s.sb("ss", [P, 2])
            eps = s.sb("eps", [P, 1])
            (c_in, cleared, turned, y_summed, rstd1, rstd2, x2_ready, h2_ready, y_read, oc, oa) = (
                s.sem(n) for n in ("consts_in", "cleared", "mt_ready", "y_summed", "rstd1", "rstd2", "x2_ready",
                                   "h2_ready", "y_read", "vector_chain", "scalar_chain"))
            x_in = [s.sem(f"x_in{n}") for n in range(2)]
            stored = [s.sem(f"stored{n}") for n in range(2)]
            with nc.Block() as block:
                @block.sync
                def _(sp):
                    sp.dma_start(w_out, t["w_out"][0]).then_inc(c_in, 16)
                    sp.dma_start(w_hi[:, :, :], t["w_out"][1].rearrange("p (k c) -> p k c", k=4)).then_inc(c_in, 16)
                    for n, row in enumerate((G1, A2, S2)):
                        load_mod(sp, t, mod[:, n, :], row, False, c_in)
                        load_mod(sp, t, mod_s[:, n, :], row, True, c_in)
                    for n in range(2):
                        sp.dma_start(x[:, n, :], t["x"][n * P:(n + 1) * P, :]).then_inc(x_in[n], 16)

                    def out(row0, rows, n):
                        sp.dma_start(t["x2"][bass.ds(row0, rows), :], x2[0:rows, n, :]).then_inc(stored[n], 16)
                        sp.dma_start(t["h2"][bass.ds(row0, rows), :], h2[0:rows, n, :]).then_inc(stored[n], 16)

                    with sp.Fori(0, TILES // 2 - 1) as i:
                        for n in range(2):
                            sp.wait_ge(h2_ready, i * 2 + n + 1)
                            out(i * (2 * P) + n * P, P, n)
                            sp.dma_start(x[:, n, :], t["x"][bass.ds(i * (2 * P) + (n + 2) * P, P), :]).then_inc(x_in[n], 16)
                    for n in range(2):
                        sp.wait_ge(h2_ready, TILES - 1 + n)
                        out(SEQ - (2 - n) * P, P, n)
                        if n == 0:
                            sp.dma_start(x[0:NS, 0, :], t["x"][SEQ:M, :]).then_inc(x_in[0], 16)
                    sp.wait_ge(h2_ready, TILES + 1)
                    out(SEQ, NS, 0)
                    for g in range(1, P // NS):
                        sp.dma_start(t["h2"][SEQ + g * NS:SEQ + (g + 1) * NS, :], h2[0:NS, 0, :]).then_inc(stored[0], 16)
                    sp.wait_ge(stored[0], 32 * (TILES // 2 + 1) + 16 * (P // NS - 1))
                    sp.wait_ge(stored[1], 32 * (TILES // 2))

                @block.scalar
                def _(act):
                    ch = Chain(act, oa)
                    act.wait_ge(cleared, 1)
                    act.copy(mt[:, 0, :, :], mT[:, :, 0:P]).then_inc(turned, 1)

                    def tile(i, n, rows, nxt):
                        if nxt is not None:
                            c0, r = nxt
                            if n is not None:
                                act.wait_ge(y_summed, i) if not (isinstance(i, int) and i == 0) else None
                            act.copy(mt[:, 1 - n, :, 0:r], mT[:, :, bass.ds(c0, r)]).then_inc(turned, 1)
                        act.wait_ge(y_summed, i + 1)
                        ch.link(act.activation(sq[0:rows, :].rearrange("p (g c) -> p g c", g=2), acc[n][0:rows, 0:2, :],
                                               ACT.Square, accum_out=ss[0:rows, 0:1]))
                        ch.link(act.activation(ss[0:rows, 0:1], ss[0:rows, 0:1], ACT.Ln, bias=eps[0:rows, :], scale=1.0 / D))
                        act.activation(ss[0:rows, 0:1], ss[0:rows, 0:1], ACT.Exp, scale=-0.5).then_inc(rstd1, 1)
                        act.wait_ge(x2_ready, i + 1)
                        ch.link(act.activation(sq[0:rows, :], x2[0:rows, n, :], ACT.Square, accum_out=ss[0:rows, 1:2]))
                        ch.link(act.activation(ss[0:rows, 1:2], ss[0:rows, 1:2], ACT.Ln, bias=eps[0:rows, :], scale=1.0 / D))
                        act.activation(ss[0:rows, 1:2], ss[0:rows, 1:2], ACT.Exp, scale=-0.5).then_inc(rstd2, 1)

                    tile(0, 0, P, (P, P))
                    ch.enter(0, 8) if False else None
                    base = ch.n
                    with act.Fori(0, TILES // 2 - 1) as i:
                        ch.enter(i, 8)
                        for n in (1, 0):
                            j = i * 2 + (1 if n else 2)
                            tile(j, n, P, (j * P + P, P))
                        ch.leave(TILES // 2 - 1)
                    tile(TILES - 1, 1, P, (SEQ, NS))
                    tile(TILES, 0, NS, None)

                @block.vector
                def _(dve):
                    ch = Chain(dve, oc)
                    dve.memset(eps[:, :], NORM_EPS).then_inc(cleared, 1)
                    dve.wait_ge(c_in, 16 * (2 + 3 * (1 + NB)))

                    def tile(i, n, rows, m, first=False):
                        xr, x2r, h2r = x[0:rows, n, :], x2[0:rows, n, :], h2[0:rows, n, :]
                        dve.wait_ge(rstd1, i + 1)
                        if not first:
                            dve.wait_ge(stored[n], (i // 2) * 32 if isinstance(i, int) else first_stored[0])
                        g2 = lambda v: v.rearrange("p (g c) -> p g c", g=2)
                        ch.link(dve.scalar_tensor_tensor(out=g2(x2r), in0=acc[n][0:rows, 0:2, :], scalar=ss[0:rows, 0:1],
                                                         in1=g2(m[:, 0, :]), op0=ALU.mult, op1=ALU.mult))
                        dve.sem_inc(y_read, 1)
                        dve.wait_ge(x_in[n], 16 * (i // 2 + 1) if isinstance(i, int) else first_stored[1])
                        dve.tensor_tensor(x2r, x2r, xr, ALU.add).then_inc(x2_ready, 1)
                        dve.wait_ge(rstd2, i + 1)
                        ch.link(dve.scalar_tensor_tensor(out=h2r, in0=x2r, scalar=ss[0:rows, 1:2], in1=m[:, 1, :],
                                                         op0=ALU.mult, op1=ALU.mult))
                        dve.tensor_tensor(h2r, h2r, m[:, 2, :], ALU.add).then_inc(h2_ready, 1)

                    first_stored = [0, 0]
                    for n in range(2):
                        tile(n, n, P, mod[:, :, :], True)
                    with dve.Fori(1, TILES // 2) as i:
                        ch.enter(i - 1, 4)
                        for n in range(2):
                            first_stored = [i * 32, i * 16 + 16]
                            tile(i * 2 + n, n, P, mod[:, :, :])
                        ch.leave(TILES // 2 - 1)
                    tile(TILES, 0, NS, mod_s)

                @block.tensor
                def _(pe):
                    pe.wait_ge(c_in, 16 * (2 + 3 * (1 + NB)))

                    def tile(i, n, rows, first=False):
                        pe.wait_ge(turned, i + 1)
                        if not first:
                            pe.wait_ge(y_read, i - 1)
                        for c in range(2):
                            for k in range(KD):
                                last = pe.matmul(acc[n][0:rows, c, :], mt[:, n, k, 0:rows], rhs(k, c * 512),
                                                 start=(k == 0), stop=(k == KD - 1))
                        last.then_inc(y_summed, 1)

                    tile(0, 0, P, True)
                    tile(1, 1, P, True)
                    with pe.Fori(1, TILES // 2) as i:
                        for n in range(2):
                            tile(i * 2 + n, n, P)
                    tile(TILES, 0, NS)


HEADS, KEYS, TOP = 8, 128, 16
RING = TOP
GROUPS = P // NS
UNITS = TILES * HEADS
S_UNITS = HEADS // GROUPS
HALF = TOP // 2
LOWEST = -3.0e38


def peer(nc, t):
    with ExitStack() as ctx:
        s = Stage(nc, ctx, "peer")
        ident = s.sb("ident", [P, P])
        fold = s.sb("fold", [P, NS])
        iota = s.sb("iota", [P, TOP])
        zeros = s.sb("zeros", [1, 512])
        wq = s.sb("wq", [P, KD, 2 * HEADS * P])
        keys = s.sb("keys", [P, 2 * HEADS, KEYS])
        G2p, G2s = s.sb("G2p", [P, D]), s.sb("G2s", [NS, D])
        ring = s.sb("ring", [P, RING, D])
        h_next, h_now, hT = s.sb("h_next", [P, D]), s.sb("h_now", [P, D]), s.sb("hT", [P, KD, P])
        hT_smp = s.sb("hT_smp", [P, KD, P])
        x2 = s.sb("x2", [P, D])
        acc = s.sb("acc", [P, 2, D])
        y, sq = s.sb("y", [P, D]), s.sb("sq", [P, D])
        idx_all, w_all = s.sb("idx_all", [P, HEADS * TOP], U32), s.sb("w_all", [P, HEADS * TOP])
        idx_smp, w_smp = s.sb("idx_smp", [P, S_UNITS * TOP], U32), s.sb("w_smp", [P, S_UNITS * TOP])
        idx = [s.sb(f"idx{n}", [P, TOP], U32) for n in range(2)]
        w = [s.sb(f"w{n}", [P, TOP]) for n in range(2)]
        dots, act_d, coef = s.sb("dots", [P, TOP]), s.sb("act_d", [P, TOP]), s.sb("coef", [P, TOP])
        diag = s.sb("diag", [P, HALF, P])
        q, qT, sc = s.sb("q", [P, 2 * P]), s.sb("qT", [P, 2 * P]), s.sb("sc", [P, 2, KEYS])
        top, pos = s.sb("top", [P, 2, TOP]), s.sb("pos", [P, 2, TOP], U32)
        posf = s.sb("posf", [P, 2, TOP])
        cand = s.sb("cand", [P, TOP, TOP])
        best, j16, j2 = s.sb("best", [P, TOP]), s.sb("j16", [P, TOP], U32), s.sb("j2", [P, 2, TOP], U32)
        jf = s.sb("jf", [P, 2, TOP])
        hot = s.sb("hot", [P, 2, TOP, TOP])
        sel = s.sb("sel", [P, 2, TOP])
        ex, z = s.sb("ex", [P, TOP]), s.sb("z", [P, 2])
        ss, eps = s.sb("ss", [P, 1]), s.sb("eps", [P, 1])
        q_b, qT_b, s_b = s.ps("q_b"), s.ps("qT_b"), s.ps("s_b")
        h_b = [s.ps(f"h_b{n}") for n in range(2)]
        v_b = s.ps("v_b", [P, 2, 512])
        (consts_in, wq_in, cleared, h_in, x2_in, h_turned, hT_ready, h_moved, u_used, v_used, pe_used, dots_ready,
         gelu_ready, coef_ready, diag_ready, q_summed, q_ready, q_turned, qT_ready, s_summed, s_ready, best_ready,
         ex_ready, smp_ready, dealt, idx_ready, issued, v_summed, v_read, total_ready, folded, acc_ready, ms_ready, y_ready,
         y_stored, y_free, passed, passed_pe, own, own_act) = (s.sem(n) for n in (
             "consts_in wq_in cleared h_in x2_in h_turned hT_ready h_moved u_used v_used pe_used dots_ready "
             "gelu_ready coef_ready diag_ready q_summed q_ready q_turned qT_ready s_summed s_ready best_ready "
             "ex_ready smp_ready dealt idx_ready issued v_summed v_read total_ready folded acc_ready ms_ready y_ready "
             "y_stored y_free passed passed_pe own own_act").split())
        landed = [s.sem(f"landed{n}") for n in range(RING)]
        CONSTS = 4 + NB
        LAST = UNITS - HEADS
        ROUTES = UNITS + HEADS

        with nc.Block() as block:
            @block.sync
            def _(sp):
                sp.dma_start(h_next[:, :], t["h2"][0:P, :]).then_inc(h_in, 16)
                sp.dma_start(ident[:, :], t["ident"]).then_inc(consts_in, 16)
                sp.dma_start(wq[:, :, :], t["peer_wq"]).then_inc(wq_in, 16)
                sp.dma_start(keys[:, :, :], t["peer_keys"]).then_inc(wq_in, 16)
                sp.dma_start(iota[:, :], t["iota"].broadcast_to([P, TOP])).then_inc(consts_in, 16)
                sp.dma_start(fold[:, :], t["fold"]).then_inc(consts_in, 16)
                load_mod(sp, t, G2p, G2, False, consts_in)
                load_mod(sp, t, G2s, G2, True, consts_in)
                sp.dma_start(x2[:, :], t["x2"][0:P, :]).then_inc(x2_in, 16)

                def load_h(i):
                    sp.wait_ge(h_moved, i)
                    sp.dma_start(h_next[:, :], t["h2"][bass.ds(i * P, P), :]).then_inc(h_in, 16)

                def tile(i, rows):
                    sp.wait_ge(y_ready, i + 1)
                    sp.dma_start(t["y"][bass.ds(i * P, rows), :], y[0:rows, :]).then_inc(y_stored, 16)

                sp.sem_inc(y_free, 1)
                load_h(1)
                with sp.Fori(0, TILES - 1) as i:
                    load_h(i + 2)
                    tile(i, P)
                    sp.dma_start(x2[:, :], t["x2"][bass.ds((i + 1) * P, P), :]).then_inc(x2_in, 16)
                    sp.wait_ge(y_stored, i * 16 + 16)
                    sp.sem_inc(y_free, 1)
                tile(TILES - 1, P)
                sp.dma_start(x2[0:NS, :], t["x2"][SEQ:M, :]).then_inc(x2_in, 16)
                sp.wait_ge(y_stored, 16 * TILES)
                sp.sem_inc(y_free, 1)
                tile(TILES, NS)
                sp.wait_ge(y_stored, 16 * (TILES + 1))

            @block.gpsimd
            def _(pool):
                def unit(U, par):
                    pool.wait_ge(idx_ready, U + 1)
                    for k in range(TOP):
                        pool.wait_ge(pe_used if k % 2 else v_used, U * HALF + (k // 2 + 1))
                        pool.sem_inc(issued, 1)
                        pool.indirect_dma_start(
                            out=ring[:, k, :], out_offset=None, in_=t["peer_u"],
                            in_offset=bass.IndirectOffsetOnAxis(ap=idx[par][:, k:k + 1], axis=0)).then_inc(landed[k], 16)
                    for k in range(TOP):
                        pool.wait_ge(u_used, U * TOP + (k + 1))
                        pool.sem_inc(issued, 1)
                        pool.indirect_dma_start(
                            out=ring[:, k, :], out_offset=None, in_=t["peer_v"],
                            in_offset=bass.IndirectOffsetOnAxis(ap=idx[par][:, k:k + 1], axis=0)).then_inc(landed[k], 16)

                with pool.Fori(0, (UNITS + S_UNITS) // 2) as m:
                    for n in range(2):
                        unit(m * 2 + n, n)

            @block.scalar
            def _(act):
                ch = Chain(act, own_act)
                act.sem_inc(diag_ready, HALF)
                act.wait_ge(cleared, 2)
                act.wait_ge(consts_in, 16 * CONSTS)

                def turn_h(i, dst=hT):
                    act.wait_ge(h_turned, i + 1)
                    for n in range(2):
                        act.copy(dst[:, 4 * n:4 * n + 4, :],
                                 h_b[n][:, :].rearrange("p (k c) -> p k c", k=4)).then_inc(hT_ready, 1)

                def scores(R):
                    act.wait_ge(q_summed, R + 1)
                    act.copy(q[:, :], q_b[:, 0:2 * P]).then_inc(q_ready, 1)
                    act.wait_ge(q_turned, R + 1)
                    act.copy(qT[:, :], qT_b[:, 0:2 * P]).then_inc(qT_ready, 1)
                    act.wait_ge(s_summed, R + 1)
                    act.copy(sc[:, :, :].rearrange("p a n -> p (a n)"), s_b[:, 0:2 * KEYS]).then_inc(s_ready, 1)

                def exps(R):
                    act.wait_ge(best_ready, R + 1)
                    act.activation(ex[:, :], best[:, :], ACT.Exp, bias=z[:, 1:2], accum_out=z[:, 0:1]).then_inc(ex_ready, 1)

                def weigh(U):
                    act.wait_ge(dots_ready, U + 1)
                    act.wait_ge(diag_ready, U * HALF + HALF)
                    act.activation(act_d[:, :], dots[:, :], ACT.Gelu).then_inc(gelu_ready, 1)
                    act.wait_ge(coef_ready, U + 1)
                    for j in range(HALF):
                        act.wait_ge(pe_used, U * HALF + (j + 1))
                        act.activation(diag[:, j, :], ident[:, :], ACT.Copy,
                                       scale=coef[:, 2 * j + 1:2 * j + 2]).then_inc(diag_ready, 1)

                def finish(i, rows):
                    act.wait_ge(acc_ready, i + 1)
                    ch.link(act.activation(sq[0:rows, :], acc[0:rows, 0, :], ACT.Square, accum_out=ss[0:rows, :]))
                    ch.link(act.activation(ss[0:rows, :], ss[0:rows, :], ACT.Ln, bias=eps[0:rows, :], scale=1.0 / D))
                    act.activation(ss[0:rows, :], ss[0:rows, :], ACT.Exp, scale=-0.5).then_inc(ms_ready, 1)

                turn_h(0)
                scores(0)
                exps(0)
                act.copy(h_now[:, :], h_next[:, :]).then_inc(h_moved, 1)
                with act.Fori(0, TILES - 1) as i:
                    ch.enter(i, 2)
                    with act.Fori(0, HEADS - 1) as h:
                        scores(i * HEADS + h + 1)
                        weigh(i * HEADS + h)
                        exps(i * HEADS + h + 1)
                    turn_h(i + 1)
                    scores(i * HEADS + HEADS)
                    weigh(i * HEADS + (HEADS - 1))
                    exps(i * HEADS + HEADS)
                    act.copy(h_now[:, :], h_next[:, :]).then_inc(h_moved, 1)
                    finish(i, P)
                    ch.leave(TILES - 1)
                turn_h(TILES, hT_smp)
                with act.Fori(0, HEADS - 1) as h:
                    scores(h * 2 + (LAST + 1))
                    weigh(h + LAST)
                    exps(h * 2 + (LAST + 1))
                    scores(h * 2 + (LAST + 2))
                    exps(h * 2 + (LAST + 2))
                scores(ROUTES - 1)
                weigh(UNITS - 1)
                exps(ROUTES - 1)
                act.copy(h_now[:, :], h_next[:, :]).then_inc(h_moved, 1)
                finish(TILES - 1, P)
                for n in range(S_UNITS):
                    weigh(UNITS + n)
                finish(TILES, NS)

            @block.vector
            def _(dve):
                ch = Chain(dve, own)
                dve.memset(eps[:, :], NORM_EPS).then_inc(cleared, 1)
                dve.memset(zeros[:, :], 0.0).then_inc(cleared, 1)
                dve.sem_inc(v_used, HALF)
                dve.wait_ge(consts_in, 16 * CONSTS)

                def alone(ins):
                    ch.link(ins)
                    dve.sem_inc(passed, 1)

                def top16(vals, val, place):
                    for n in range(2):
                        o8 = slice(8 * n, 8 * n + 8)
                        alone(dve.max(val[:, o8], vals))
                        last = dve.max_index(place[:, o8], val[:, o8], vals)
                        if n == 0:
                            alone(last)
                            alone(dve.match_replace(vals, val[:, o8], vals, LOWEST))
                    return last

                def route_keys(R):
                    dve.wait_ge(s_ready, R + 1)
                    dve.sem_inc(passed, 1)
                    for n in range(2):
                        last = top16(sc[:, n, :], top[:, n, :], pos[:, n, :])
                    ch.link(last)

                def route_pairs(R, idx_to, w_to, to_pool):
                    dve.tensor_copy(posf[:, :, :], pos[:, :, :])
                    alone(dve.tensor_tensor(cand[:, :, :], top[:, 0, :].unsqueeze(2).broadcast_to([P, TOP, TOP]),
                                            top[:, 1, :].unsqueeze(1).broadcast_to([P, TOP, TOP]), ALU.add))
                    ch.link(top16(cand[:, :, :].rearrange("p a b -> p (a b)"), best, j16))
                    dve.tensor_scalar(z[:, 1:2], best[:, 0:1], -1.0, None, ALU.mult).then_inc(best_ready, 1)
                    dve.tensor_scalar(j2[:, 0, :], j16[:, :], 4, None, ALU.logical_shift_right)
                    ch.link(dve.tensor_scalar(j2[:, 1, :], j16[:, :], TOP - 1, None, ALU.bitwise_and))
                    ch.link(dve.tensor_copy(jf[:, :, :], j2[:, :, :]))
                    for n in range(2):
                        last = dve.tensor_tensor(hot[:, n, :, :], jf[:, n, :].unsqueeze(2).broadcast_to([P, TOP, TOP]),
                                                 iota[:, :].unsqueeze(1).broadcast_to([P, TOP, TOP]), ALU.is_equal)
                    ch.link(last)
                    for n in range(2):
                        last = dve.tensor_tensor(hot[:, n, :, :], hot[:, n, :, :],
                                                 posf[:, n, :].unsqueeze(1).broadcast_to([P, TOP, TOP]), ALU.mult)
                    ch.link(last)
                    ch.link(dve.tensor_reduce(sel[:, :, :], hot[:, :, :, :], AX.X, ALU.add))
                    dve.scalar_tensor_tensor(out=idx_to, in0=sel[:, 0, :], scalar=float(KEYS),
                                             in1=sel[:, 1, :], op0=ALU.mult,
                                             op1=ALU.add).then_inc(idx_ready if to_pool else smp_ready, 1)
                    dve.wait_ge(ex_ready, R + 1)
                    ch.link(dve.reciprocal(z[:, 0:1], z[:, 0:1]))
                    ch.link(dve.tensor_scalar(w_to, ex[:, :], z[:, 0:1], None, ALU.mult))

                def unit(U, weights, R=None, par=None):
                    for k in range(TOP):
                        dve.wait_ge(landed[k], U * 32 + 16)
                        dve.tensor_tensor_reduce(ring[:, k, :], ring[:, k, :], h_now[:, :], 1.0, 0.0,
                                                 ALU.mult, ALU.add, dots[:, k:k + 1]).then_inc(u_used, 1)
                    dve.wait_ge(u_used, U * TOP + TOP)
                    dve.sem_inc(dots_ready, 1)
                    if R is not None:
                        route_keys(R)
                    dve.wait_ge(gelu_ready, U + 1)
                    dve.wait_ge(v_used, U * HALF + HALF)
                    dve.tensor_tensor(coef[:, :], act_d[:, :], weights, ALU.mult).then_inc(coef_ready, 1)
                    if par is not None:
                        route_pairs(R, idx[par][:, :], w[par][:, :], True)
                    elif R is not None:
                        route_pairs(R, *samples_head(HEADS - 1), False)

                def add_v(U):
                    dve.wait_ge(coef_ready, U + 1)
                    for j in range(HALF):
                        k = 2 * j
                        dve.wait_ge(landed[k], U * 32 + 32)
                        if j < 2:
                            dve.wait_ge(v_used, U * HALF + HALF)
                        else:
                            dve.wait_ge(v_used, U * HALF + (HALF + j - 1))
                        dve.scalar_tensor_tensor(out=acc[:, j % 2, :], in0=ring[:, k, :], scalar=coef[:, k:k + 1],
                                                 in1=acc[:, j % 2, :], op0=ALU.mult, op1=ALU.add).then_inc(v_used, 1)

                def clear():
                    dve.memset(acc[:, :, :], 0.0).then_inc(own, 1)
                    ch.n += 1
                    dve.wait_ge(own, ch.base + ch.n)
                    dve.sem_inc(passed, 1)

                def total(i, units):
                    dve.wait_ge(v_used, units * HALF + HALF)
                    ch.link(dve.tensor_tensor(acc[:, 0, :], acc[:, 0, :], acc[:, 1, :], ALU.add))
                    dve.wait_ge(v_summed, i + 1)
                    ch.link(dve.tensor_tensor(acc[:, 0, :].rearrange("p (g c) -> p g c", g=2),
                                              acc[:, 0, :].rearrange("p (g c) -> p g c", g=2), v_b[:, :, :], ALU.add))

                def finish(i, rows, gain):
                    dve.sem_inc(acc_ready, 1)
                    dve.wait_ge(ms_ready, i + 1)
                    dve.wait_ge(x2_in, i * 16 + 16)
                    dve.wait_ge(y_free, i + 1)
                    ch.link(dve.scalar_tensor_tensor(out=y[0:rows, :], in0=acc[0:rows, 0, :], scalar=ss[0:rows, 0:1],
                                                     in1=gain, op0=ALU.mult, op1=ALU.mult))
                    dve.tensor_tensor(y[0:rows, :], y[0:rows, :], x2[0:rows, :], ALU.add).then_inc(y_ready, 1)

                def samples_head(h):
                    cols = bass.ds(h * TOP, TOP)
                    return idx_all[:, cols], w_all[:, cols]

                ROUTE = 22
                route_keys(0)
                route_pairs(0, idx[0][:, :], w[0][:, :], True)
                assert ch.n == ROUTE, ch.n
                ch0 = ch.n
                PER = 1 + HEADS * ROUTE + 3

                def tile_end(i, link0):
                    ch.base, ch.n = link0, 0
                    total(i, i * HEADS + HEADS)
                    dve.sem_inc(v_read, 1)
                    finish(i, P, G2p[:, :])
                    assert ch.n == 3

                with dve.Fori(0, TILES - 1) as i:
                    dve.wait_ge(h_moved, i + 1)
                    ch.base, ch.n = ch0 + i * PER, 0
                    clear()
                    with dve.Fori(0, HEADS // 2) as m:
                        ch.base, ch.n = ch0 + i * PER + 1 + m * (2 * ROUTE), 0
                        for n in range(2):
                            U = i * HEADS + m * 2 + n
                            unit(U, w[n][:, :], U + 1, 1 - n)
                            add_v(U)
                        assert ch.n == 2 * ROUTE, ch.n
                    tile_end(i, ch0 + i * PER + 1 + HEADS * ROUTE)

                def deal():
                    dve.wait_ge(smp_ready, HEADS)
                    for g in range(GROUPS):
                        rows = slice(g * NS, (g + 1) * NS)
                        dve.tensor_copy(w_smp[rows, :], w_all[rows, g:HEADS * TOP:GROUPS]).then_inc(dealt, 1)
                        dve.tensor_copy(idx_smp[rows, :], idx_all[rows, g:HEADS * TOP:GROUPS]).then_inc(dealt, 1)
                    dve.wait_ge(dealt, 2 * GROUPS)
                    dve.tensor_copy(idx[0][:, :], idx_smp[:, 0:TOP]).then_inc(idx_ready, 1)

                last = TILES - 1
                dve.wait_ge(h_moved, TILES)
                ch.base, ch.n = ch0 + last * PER, 0
                clear()

                def last_unit(h, par):
                    R = h * 2 + (LAST + 1)
                    unit(h + LAST, w[par][:, :], R, 1 - par)
                    route_keys(R + 1)
                    route_pairs(R + 1, *samples_head(h), False)
                    add_v(h + LAST)

                with dve.Fori(0, HEADS // 2 - 1) as m:
                    ch.base, ch.n = ch0 + last * PER + 1 + m * (4 * ROUTE), 0
                    for n in range(2):
                        last_unit(m * 2 + n, n)
                    assert ch.n == 4 * ROUTE
                ch.base, ch.n = ch0 + last * PER + 1 + (HEADS - 2) * 2 * ROUTE, 0
                last_unit(HEADS - 2, 0)
                unit(UNITS - 1, w[1][:, :], ROUTES - 1)
                deal()
                add_v(UNITS - 1)
                tile_end(last, ch0 + last * PER + 1 + (2 * HEADS - 1) * ROUTE)

                dve.wait_ge(h_moved, TILES + 1)
                ch.base, ch.n = ch0 + TILES * PER + (HEADS - 1) * ROUTE, 0
                clear()
                for n in range(S_UNITS):
                    unit(UNITS + n, w_smp[:, n * TOP:(n + 1) * TOP])
                    if n + 1 < S_UNITS:
                        dve.tensor_copy(idx[1 - n][:, :], idx_smp[:, (n + 1) * TOP:(n + 2) * TOP]).then_inc(idx_ready, 1)
                    add_v(UNITS + n)
                total(TILES, UNITS + S_UNITS)
                dve.sem_inc(total_ready, 1)
                dve.wait_ge(folded, 1)
                ch.link(dve.tensor_copy(acc[0:NS, 0, :].rearrange("p (g c) -> p g c", g=2), v_b[0:NS, :, :]))
                finish(TILES, NS, G2s[:, :])

            @block.tensor
            def _(pe):
                pe.sem_inc(pe_used, HALF)
                pe.wait_ge(cleared, 2)
                pe.wait_ge(consts_in, 16 * CONSTS)

                def turn_h(i):
                    pe.wait_ge(h_in, i * 16 + 16)
                    for k in range(KD):
                        last = pe.transpose(h_b[k // 4][:, (k % 4) * P:(k % 4 + 1) * P], h_next[:, k * P:(k + 1) * P],
                                            ident[:, :])
                    last.then_inc(h_turned, 1)
                    pe.wait_ge(hT_ready, i * 2 + 2)
                    pe.sem_inc(passed_pe, 1)

                def route(R, h, hT=hT):
                    for k in range(KD):
                        last = pe.matmul(q_b[:, 0:2 * P], hT[:, k, :], wq[:, k, bass.ds(h * (2 * P), 2 * P)],
                                         start=(k == 0), stop=(k == KD - 1))
                    last.then_inc(q_summed, 1)
                    pe.wait_ge(q_ready, R + 1)
                    for n in range(2):
                        last = pe.transpose(qT_b[:, n * P:(n + 1) * P], q[:, n * P:(n + 1) * P], ident[:, :])
                    last.then_inc(q_turned, 1)
                    pe.wait_ge(qT_ready, R + 1)
                    for n in range(2):
                        last = pe.matmul(s_b[:, n * KEYS:(n + 1) * KEYS], qT[:, n * P:(n + 1) * P],
                                         keys[:, bass.ds(h * 2 + n, 1), :].rearrange("p o n -> p (o n)"), start=True, stop=True)
                    last.then_inc(s_summed, 1)
                    pe.wait_ge(s_ready, R + 1)

                def zero_banks(start):
                    for c in range(2):
                        last = pe.matmul(v_b[:, c, :], zeros[:, 0:P], zeros[:, :], start=start, stop=not start)
                    return last

                def add_v(U):
                    for j in range(HALF):
                        k = 2 * j + 1
                        pe.wait_ge(diag_ready, U * HALF + (HALF + j + 1))
                        pe.wait_ge(landed[k], U * 32 + 32)
                        for c in range(2):
                            last = pe.matmul(v_b[:, c, :], diag[:, j, :], ring[:, k, c * 512:(c + 1) * 512],
                                             start=False, stop=False)
                        last.then_inc(pe_used, 1)

                pe.wait_ge(wq_in, 32)
                turn_h(0)
                route(0, 0)
                zero_banks(True)

                def tile_end(i):
                    zero_banks(False).then_inc(v_summed, 1)
                    pe.wait_ge(v_read, i + 1)
                    zero_banks(True)

                with pe.Fori(0, TILES - 1) as i:
                    with pe.Fori(0, HEADS - 1) as h:
                        route(i * HEADS + h + 1, h + 1)
                        add_v(i * HEADS + h)
                    turn_h(i + 1)
                    route(i * HEADS + HEADS, 0)
                    add_v(i * HEADS + (HEADS - 1))
                    tile_end(i)
                turn_h(TILES)
                with pe.Fori(0, HEADS - 1) as h:
                    route(h * 2 + (LAST + 1), h + 1)
                    route(h * 2 + (LAST + 2), h, hT_smp)
                    add_v(h + LAST)
                route(ROUTES - 1, HEADS - 1, hT_smp)
                add_v(UNITS - 1)
                tile_end(TILES - 1)
                for n in range(S_UNITS):
                    add_v(UNITS + n)
                zero_banks(False).then_inc(v_summed, 1)
                pe.wait_ge(total_ready, 1)
                for c in range(2):
                    last = pe.matmul(v_b[0:NS, c, :], fold[:, :], acc[:, 0, c * 512:(c + 1) * 512], start=True, stop=True)
                last.then_inc(folded, 1)


def scratch(nc, t):
    for name, shape in {"mod": [NSEQ, 6, D], "pT": [66, P, M], "gaT": [16, M],
                        "ogT": [GH, P, 2, M], "orT": [PAIRS, P, M],
                        "x2": [M, D], "h2": [MP, D]}.items():
        t[name] = nc.dram_tensor(name, shape, F32, kind="Internal").ap()


def build(nc, t):
    scratch(nc, t)
    for stage in (modulation, projection, gla, rwkv, merge, peer):
        with nc.cleanup_on_exit():
            stage(nc, t)


OUTPUTS = {"y": [M, D], "new_gla_p": [GH, P, GV], "new_gla_s": [GH, P, NB, GV],
           "new_rw_p": [PAIRS, 2, RH, RH], "new_rw_s": [PAIRS, 2, RH, NB, RH],
           "new_shift": [PAIRS, 3, P, NSEQ], "new_shift_wg": [2, P, NSEQ]}


def masks():
    f = np.float32
    s, q = np.arange(P), np.arange(NS)
    same_chunk = s[:, None] // GC == s[None] // GC
    same_seq = q[:, None] // NT == q[None] // NT
    tok = np.arange(MW)
    head, pos = s // RH, s % RH
    same_head = head[:, None] == head[None]
    before = pos[:, None] < pos[None]
    seq_pos = (pos[:, None] // NT == pos[None] // NT) & (pos[:, None] < NS) & (pos[None] < NS)
    t = np.arange(RC)
    upto = pos[:, None] <= t[None]
    ones_joined = same_head & (pos[:, None] == pos[None] + 1) & (pos[None] % 2 == 0)
    joins = [same_head & (pos[:, None] // (2 * n) == pos[None] // (2 * n)) & (pos[:, None] // n % 2 == 0)
             & (pos[None] // n % 2 == 1) for n in (2 ** (l + 1) for l in range(LEVELS))]
    c = {
        "ident": s[:, None] == s[None],
        "iota": np.arange(TOP)[None],
        "fold": s[:, None] % NS == q[None],
        "starts": np.where(tok < SEQ, tok % GC != 0, tok % NT != 0)[None],
        "gla_mask": same_chunk & (s[:, None] <= s[None]),
        "gla_mask_s": same_seq & (q[:, None] <= q[None]),
        "seq_rows": q[:, None] // NT == np.arange(NB)[None],
        "rw_strict": np.stack([same_head & before, same_head & before & seq_pos], 1),
        "rw_incl": np.stack([upto, upto & (pos[:, None] // NT == t[None] // NT)], 1),
        "rw_first_l": ones_joined,
        "rw_first_u": ones_joined.T,
        "rw_join": np.stack(joins, 1),
        "rw_seq_cols": np.broadcast_to((pos[None] // NT == np.arange(NB)[:, None])[None], (P, NB, P)),
        "rw_seq_rows": pos[:, None] // NT == np.arange(NB)[None],
        "rw_heads": same_head,
    }
    c = {k: np.ascontiguousarray(v.astype(f)) for k, v in c.items()}
    c["rw_mean"] = c["rw_heads"] / f(RH)
    return c


def layout(i):
    o = {}
    o["x"] = np.concatenate([i["x_prompt"].reshape(SEQ, D), i["x_sample"].reshape(NS, D)])
    c = np.concatenate([i["c_prompt"], i["c_sample"]])
    o["cT"] = c.T.reshape(KD, P, NSEQ).transpose(1, 0, 2).reshape(P, KD * NSEQ)
    o["w_ada"] = i["w_ada"][0].reshape(KD, P, 12, 512).transpose(2, 1, 0, 3).reshape(12, P, KD * 512)
    o["b_ada"] = i["b_ada"]
    o["gains"] = np.concatenate([i["g_pre_mix"], i["g_post_mix"], i["g_pre_ffn"], i["g_post_ffn"]])
    w = i["w_in"][0]
    ga0 = 2 * GH * P + 2 * GH * GV
    rest = np.concatenate([w[:, :ga0], w[:, ga0 + 16:]], 1)
    o["w_in"] = rest.reshape(KD, P, 66, P).transpose(2, 1, 0, 3)
    o["w_ga"] = w[:, ga0:ga0 + 16].reshape(KD, P, 16).transpose(1, 0, 2)
    o["w_gate"] = i["w_gla_gate"][0].reshape(16, GH, P).transpose(1, 0, 2)
    o["gla_cst"] = np.concatenate([i["b_gla_gate"][0].reshape(GH, P, 1),
                                   i["g_gla_norm"][0].reshape(GH, 2, P).transpose(0, 2, 1)], 2)
    o["state_gla"] = i["state_gla"][0].transpose(1, 2, 0, 3)
    mu = i["mu_shift"][0].reshape(26, P)
    vec = [i[k][0].reshape(PAIRS, P) for k in ("rw_w0", "rw_a0", "rw_k_k", "rw_k_a", "rw_r_k", "rw_gn_w", "rw_gn_b")]
    o["rw_cst"] = np.stack([mu[0:8], mu[8:16], mu[16:24]] + vec).transpose(2, 1, 0)
    o["rw_mu_wg"] = mu[24:26].T
    sh = i["state_shift"][0].reshape(NB, 26, P)
    o["rw_sh_wg"] = sh[:, 24:26].transpose(2, 1, 0)
    o["rw_sh"] = sh[:, :24].reshape(NB, 3, PAIRS, P).transpose(2, 3, 1, 0)
    o["w2a2"] = np.concatenate([i["rw_w2"][0], i["rw_a2"][0]]).reshape(P, PAIRS, P).transpose(1, 0, 2)
    o["g2"] = i["rw_g2"][0].reshape(P, PAIRS, P).transpose(1, 0, 2)
    o["state_rwkv"] = i["state_rwkv"][0].reshape(NB, PAIRS, 2, RH, RH).transpose(1, 2, 4, 0, 3)
    wb = np.stack([i["w_b_gla"][0], i["w_b_rw"][0]])
    o["w_br"] = wb.reshape(2, KD, P, KD, P).transpose(3, 2, 0, 1, 4)
    o["w_out"] = i["w_out"][0].reshape(2, 4, P, D).transpose(0, 2, 1, 3).reshape(2, P, 4 * D)
    o["peer_wq"] = i["peer_wq"][0].reshape(KD, P, 2 * HEADS * P).transpose(1, 0, 2)
    o["peer_keys"] = i["peer_keys"][0].reshape(2 * HEADS, KEYS, P).transpose(2, 0, 1)
    o["peer_u"], o["peer_v"] = i["peer_u"][0], i["peer_v"][0]
    return {k: np.ascontiguousarray(v) for k, v in o.items()}


def kernel(**inputs):
    from concourse import bacc
    from concourse.bass_utils import run_bass_kernel_spmd

    nc = bacc.Bacc("TRN2", target_bir_lowering=False, num_devices=1)
    arrays = {**layout({k: np.asarray(v) for k, v in inputs.items()}), **masks()}
    t = {k: nc.dram_tensor(f"in_{k}", v.shape, F32, kind="ExternalInput").ap() for k, v in arrays.items()}
    for k, shape in OUTPUTS.items():
        t[k] = nc.dram_tensor(f"out_{k}", shape, F32, kind="ExternalOutput").ap()
    build(nc, t)
    r = run_bass_kernel_spmd(nc, [{f"in_{k}": v for k, v in arrays.items()}], core_ids=[0]).results[0]
    r = {k: r[f"out_{k}"] for k in OUTPUTS}
    y = r["y"]
    shift = r["new_shift"].transpose(3, 1, 0, 2).reshape(NSEQ, 3 * PAIRS * P)
    shift = np.concatenate([shift, r["new_shift_wg"].transpose(2, 0, 1).reshape(NSEQ, 2 * P)], 1)
    return (y[:SEQ].reshape(1, SEQ, D), y[SEQ:].reshape(NB, NT, D),
            r["new_gla_p"].reshape(1, 1, GH, P, GV),
            r["new_rw_p"].transpose(0, 1, 3, 2).reshape(1, 1, 2 * PAIRS, RH, RH),
            shift[0].reshape(1, 1, -1),
            r["new_gla_s"].transpose(2, 0, 1, 3).reshape(1, NB, GH, P, GV),
            r["new_rw_s"].transpose(3, 0, 1, 4, 2).reshape(1, NB, 2 * PAIRS, RH, RH),
            shift[1:].reshape(1, NB, -1))
```

```python
from contextlib import ExitStack

import numpy as np

import concourse.bass as bass
from concourse import mybir

F32 = mybir.dt.float32
U32 = mybir.dt.uint32
F32R = mybir.dt.float32r
ALU = mybir.AluOpType
ACT = mybir.ActivationFunctionType
AX = mybir.AxisListType

P = 128
D = 1024
KD = D // P
SEQ = 1024
NB, NT = 8, 4
NS = NB * NT
M = SEQ + NS
NSEQ = 1 + NB
G3 = M // 3
TILES = SEQ // P
NORM_EPS = 1e-6


S1, A1, G1, S2, A2, G2 = range(6)
HIGH_BITS = 0xFFFFF000


def split(eng, hi, lo, x, masked, link):
    link(eng.tensor_scalar(masked.bitcast(U32), x.bitcast(U32), HIGH_BITS, None, ALU.bitwise_and))
    eng.tensor_copy(hi, masked)
    link(eng.tensor_tensor(lo, x, masked, ALU.subtract))


def matmul3(pe, out, w, x, start, stop):
    pe.matmul(out, w[1], x[0], start=start, stop=False)
    pe.matmul(out, w[0], x[1], start=False, stop=False)
    return pe.matmul(out, w[0], x[0], start=False, stop=stop)


class Stage:

    def __init__(self, nc, ctx, name):
        self.nc, self.ctx, self.name = nc, ctx, name

    def sb(self, name, shape, dtype=F32):
        return self.ctx.enter_context(self.nc.sbuf_tensor(f"{self.name}_{name}", shape, dtype))

    def ps(self, name, shape=(P, 512)):
        return self.ctx.enter_context(self.nc.psum_tensor(f"{self.name}_{name}", list(shape), F32))

    def sem(self, name):
        return self.nc.alloc_semaphore(name=f"{self.name}_{name}")


class Chain:

    def __init__(self, eng, sem):
        self.eng, self.sem, self.base, self.n = eng, sem, 0, 0

    def link(self, ins):
        self.n += 1
        ins.then_inc(self.sem, 1)
        self.eng.wait_ge(self.sem, self.base + self.n)

    def enter(self, i, per):
        self.before, self.per = self.n, per
        self.base, self.n = self.n + i * per, 0

    def leave(self, count):
        assert self.n == self.per, (self.n, self.per)
        self.base, self.n = 0, self.before + count * self.per


def modulation(nc, t, xT, modT):
    CG = 12
    LAG = CG - (TILES + 1)
    with ExitStack() as ctx:
        s = Stage(nc, ctx, "mod")
        cT = s.sb("cT", [P, KD * NSEQ])
        sg = s.sb("sg", [P, KD * NSEQ])
        w = s.sb("w", [P, 3, KD * 512])
        bias = s.sb("bias", [1, 6 * D])
        ones = s.sb("ones", [1, NSEQ])
        gains = s.sb("gains", [NSEQ, 4, D])
        out = s.sb("out", [NSEQ, 6, D])
        ident = s.sb("ident", [P, P])
        x = s.sb("x", [P, TILES, D])
        xs = s.sb("xs", [NS, D])
        sq = s.sb("sq", [P, D])
        ssq = s.sb("ssq", [P, TILES + 1])
        eps = s.sb("eps", [P, 1])
        acc = s.ps("acc", [P, 4, 512])
        x_b = [s.ps(f"x_b{n}") for n in range(2)]
        m_b = s.ps("m_b")
        small_in, x_in = s.sem("small_in"), s.sem("x_in")
        w_in = [s.sem(f"w_in{n}") for n in range(3)]
        ready = s.sem("silu_ready")
        expd = s.sem("exp_done")
        cleared, x_ready, turned = s.sem("cleared"), s.sem("x_ready"), s.sem("x_turned")
        xT_lo, xT_hi = s.sem("xT_lo"), s.sem("xT_hi")
        summed = s.sem("summed")
        copied = s.sem("copied")
        done = s.sem("combined")
        m_turned, modT_ready = s.sem("mod_turned"), s.sem("modT_ready")
        stored = s.sem("stored")
        own, own_act = s.sem("vector_chain"), s.sem("scalar_chain")

        def cols(i):
            return slice(i * P, i * P + P) if i < TILES else slice(SEQ, M)

        with nc.Block() as block:
            @block.sync
            def _(sp):
                sp.dma_start(cT[:, :], t["cT"]).then_inc(small_in, 16)
                sp.dma_start(bias[:, :], t["b_ada"]).then_inc(small_in, 16)
                for n in range(4):
                    sp.dma_start(gains[:, n, :], t["gains"][n:n + 1, :].broadcast_to([NSEQ, D])).then_inc(small_in, 16)
                for g in range(CG):
                    if g >= 3:
                        sp.wait_ge(summed, g - 2)
                    sp.dma_start(w[:, g % 3, :], t["w_ada"][g]).then_inc(w_in[g % 3], 16)
                    if g == 0:
                        sp.dma_start(x[:, :, :], t["x"][0:SEQ, :].rearrange("(i p) d -> p i d", p=P)).then_inc(x_in, 16)
                        sp.dma_start(xs[:, :], t["x"][SEQ:M, :]).then_inc(x_in, 16)
                        sp.dma_start(ident[:, :], t["ident"]).then_inc(x_in, 16)
                sp.wait_ge(done, 2)
                sp.dma_start(t["mod"], out[:, :, :]).then_inc(stored, 16)
                sp.wait_ge(stored, 16)

            @block.scalar
            def _(act):
                ch = Chain(act, own_act)
                act.wait_ge(small_in, 96)
                act.activation(sg[:, :], cT[:, :], ACT.Exp, scale=-1.0).then_inc(expd, 1)
                act.wait_ge(x_in, 48)
                act.wait_ge(cleared, 2)
                for i in range(TILES):
                    ch.link(act.activation(sq[:, :], x[:, i, :], ACT.Square, accum_out=ssq[:, i:i + 1]))
                ch.link(act.activation(sq[0:NS, :], xs[:, :], ACT.Square, accum_out=ssq[0:NS, TILES:TILES + 1]))
                ch.link(act.activation(ssq[:, :], ssq[:, :], ACT.Ln, bias=eps[:, :], scale=1.0 / D))
                ch.link(act.activation(ssq[:, :], ssq[:, :], ACT.Exp, scale=-0.5))
                for g in range(CG):
                    i = g - LAG
                    if i + 1 >= 0 and i + 1 <= TILES:
                        v, r = (x[:, i + 1, :], ssq[:, i + 1:i + 2]) if i + 1 < TILES else (xs[:, :], ssq[0:NS, TILES:TILES + 1])
                        act.activation(v, v, ACT.Copy, scale=r).then_inc(x_ready, 1)
                    act.wait_ge(summed, g + 1)
                    act.copy(out[:, g // 2, (g % 2) * 512:(g % 2) * 512 + 512],
                             acc[0:NSEQ, g % 4, :]).then_inc(copied, 1)
                    if i >= 0:
                        act.wait_ge(turned, i + 1)
                        n = cols(i).stop - cols(i).start
                        act.copy(xT[:, 0:4, cols(i)], x_b[0][:, 0:4 * n].rearrange("p (k c) -> p k c", k=4)).then_inc(xT_lo, 1)
                act.wait_ge(m_turned, 1)
                act.copy(modT[:, :, :, :].rearrange("p r k b -> p (r k b)"),
                         m_b[:, 0:2 * KD * NSEQ]).then_inc(modT_ready, 1)

            @block.vector
            def _(dve):
                ch = Chain(dve, own)
                dve.memset(eps[:, :], NORM_EPS).then_inc(cleared, 1)
                dve.memset(ssq[:, :], 1.0).then_inc(cleared, 1)
                ch.link(dve.memset(ones[:, :], 1.0))
                dve.wait_ge(expd, 1)
                ch.link(dve.tensor_scalar_add(sg[:, :], sg[:, :], 1.0))
                ch.link(dve.reciprocal(sg[:, :], sg[:, :]))
                dve.tensor_tensor(sg[:, :], sg[:, :], cT[:, :], ALU.mult).then_inc(ready, 1)

                def combine(row, n):
                    if row % 3 == 1:
                        return dve.scalar_tensor_tensor(out=out[:, row, :], in0=out[:, row, :], scalar=1.0,
                                                        in1=gains[:, n, :], op0=ALU.add, op1=ALU.mult)
                    return dve.tensor_tensor(out[:, row, :], out[:, row, :], gains[:, n, :], ALU.mult)

                for i in range(TILES + 1):
                    dve.wait_ge(turned, i + 1)
                    n = cols(i).stop - cols(i).start
                    dve.tensor_copy(xT[:, 4:8, cols(i)], x_b[1][:, 0:4 * n].rearrange("p (k c) -> p k c", k=4)).then_inc(xT_hi, 1)
                    if i == 2:
                        dve.wait_ge(copied, 4)
                        combine(1, 0).then_inc(done, 1)
                dve.wait_ge(copied, CG)
                ch.link(combine(4, 2))
                ch.link(combine(2, 1))
                combine(5, 3).then_inc(done, 1)

            @block.tensor
            def _(pe):
                pe.wait_ge(ready, 1)
                for g in range(CG):
                    pe.wait_ge(w_in[g % 3], 16 * (g // 3 + 1))
                    if g >= 4:
                        pe.wait_ge(copied, g - 3)
                    for k in range(KD):
                        pe.matmul(acc[0:NSEQ, g % 4, :], sg[:, k * NSEQ:(k + 1) * NSEQ],
                                  w[:, g % 3, k * 512:(k + 1) * 512], start=(k == 0), stop=False)
                    pe.matmul(acc[0:NSEQ, g % 4, :], ones[0:1, :], bias[0:1, g * 512:(g + 1) * 512],
                              start=False, stop=True).then_inc(summed, 1)
                    i = g - LAG
                    if i >= 0:
                        pe.wait_ge(x_ready, i + 1)
                        if i:
                            pe.wait_ge(xT_lo, i)
                            pe.wait_ge(xT_hi, i)
                        n = cols(i).stop - cols(i).start
                        v = x[:, i, :] if i < TILES else xs[:, :]
                        for k in range(KD):
                            last = pe.transpose(x_b[k // 4][:, (k % 4) * n:(k % 4 + 1) * n], v[:, k * P:(k + 1) * P],
                                                ident[0:n, 0:n])
                        last.then_inc(turned, 1)
                    if g == CG - 2:
                        pe.wait_ge(done, 1)
                        for r, row in enumerate((A1, S1)):
                            for k in range(KD):
                                last = pe.transpose(m_b[:, (r * KD + k) * NSEQ:(r * KD + k + 1) * NSEQ],
                                                    out[:, row, k * P:(k + 1) * P], ident[0:NSEQ, 0:NSEQ])
                        last.then_inc(m_turned, 1)


def load_mod(eng, t, dst, row, samples, sem):
    if not samples:
        eng.dma_start(dst[:, :], t["mod"][0:1, row, :].broadcast_to([P, D])).then_inc(sem, 16)
        return
    for b in range(NB):
        eng.dma_start(dst[b * NT:(b + 1) * NT, :],
                      t["mod"][1 + b:2 + b, row, :].broadcast_to([NT, D])).then_inc(sem, 16)


def projection(nc, t, xT, modT):
    PT = t["w_in"].shape[0]
    W = 2
    ITER = PT // W
    assert ITER * W == PT
    with ExitStack() as ctx:
        s = Stage(nc, ctx, "proj")
        hT = [s.sb(f"hT_{part}", [P, KD, M], F32R) for part in ("high", "low")]
        w = s.sb("w", [P, W, KD, P])
        w2 = [s.sb(f"w_{part}", [P, W, KD, P], F32R) for part in ("high", "low")]
        wg = s.sb("wg", [P, KD, 16])
        wg2 = [s.sb(f"wg_{part}", [P, KD, 16], F32R) for part in ("high", "low")]
        masked = s.sb("masked", [P, KD, G3])
        o = s.sb("o", [P, W, M])
        og = s.sb("og", [16, M])
        acc = [s.ps(f"acc{n}", [P, 3, 512]) for n in range(W)]
        wg_in = s.sem("wg_in")
        w_in = [s.sem(f"w_in{n}") for n in range(W)]
        shifted = s.sem("shifted")
        hT_ready, w_split = s.sem("hT_ready"), s.sem("w_split")
        tile_done = s.sem("tile_done")
        first_out = s.sem("first_out")
        rest_out = s.sem("rest_out")
        stored = [s.sem(f"stored{n}") for n in range(W)]
        own = s.sem("vector_chain")

        with nc.Block() as block:
            @block.sync
            def _(sp):
                sp.dma_start(wg[:, :, :], t["w_ga"]).then_inc(wg_in, 16)
                for n in range(W):
                    sp.dma_start(w[:, n, :, :], t["w_in"][n]).then_inc(w_in[n], 16)
                with sp.Fori(0, ITER - 1) as i:
                    for n in range(W):
                        sp.wait_ge(w_split, i * W + n + 1)
                        sp.dma_start(w[:, n, :, :], t["w_in"][i * W + (W + n)]).then_inc(w_in[n], 16)
                        sp.wait_ge(first_out, i * W + n + 1)
                        sp.wait_ge(rest_out, i * W + n + 1)
                        sp.dma_start(t["pT"][i * W + n], o[:, n, :]).then_inc(stored[n], 16)
                for n in range(W):
                    sp.wait_ge(first_out, (ITER - 1) * W + n + 1)
                    sp.wait_ge(rest_out, (ITER - 1) * W + n + 1)
                    sp.dma_start(t["pT"][PT - W + n], o[:, n, :]).then_inc(stored[n], 16)
                sp.wait_ge(first_out, PT + 1)
                sp.wait_ge(rest_out, PT + 1)
                sp.dma_start(t["gaT"], og[:, :]).then_inc(stored[0], 16)
                for n in range(W):
                    sp.wait_ge(stored[n], 16 * (ITER + (n == 0)))

            @block.scalar
            def _(act):
                for g in range(3):
                    c0, c1 = g * G3, min((g + 1) * G3, SEQ)
                    for k in range(KD):
                        last = act.activation(xT[:, k, c0:c1], xT[:, k, c0:c1], ACT.Identity,
                                              scale=modT[:, 0, k, 0:1], bias=modT[:, 1, k, 0:1])
                    last.then_inc(shifted, 1)

                def evacuate(i, first):
                    for n in range(W):
                        act.wait_ge(tile_done, i * W + n + 1)
                        if not first:
                            act.wait_ge(stored[n], i * 16)
                        act.copy(o[:, n, 0:G3], acc[n][:, 0, 0:G3]).then_inc(first_out, 1)

                evacuate(0, True)
                with act.Fori(1, ITER) as i:
                    evacuate(i, False)
                act.wait_ge(tile_done, PT + 1)
                act.copy(og[:, 0:G3], acc[0][0:16, 0, 0:G3]).then_inc(first_out, 1)

            @block.vector
            def _(dve):
                ch = Chain(dve, own)
                xv = xT[:, :, SEQ:M].rearrange("p k (b c) -> p k b c", c=NT)
                mv = [modT[:, r, :, 1:NSEQ].unsqueeze(3).broadcast_to([P, KD, NB, NT]) for r in range(2)]
                ch.link(dve.tensor_tensor(xv, xv, mv[0], ALU.mult))
                ch.link(dve.tensor_tensor(xv, xv, mv[1], ALU.add))
                def split_w(i, n):
                    dve.wait_ge(w_in[n], i * 16 + 16)
                    split(dve, w2[0][:, n, :, :], w2[1][:, n, :, :], w[:, n, :, :], masked[:, :, 0:P], ch.link)
                    dve.sem_inc(w_split, 1)

                split_w(0, 0)
                for g in range(3):
                    dve.wait_ge(shifted, g + 1)
                    tokens = slice(g * G3, (g + 1) * G3)
                    split(dve, *(part[:, :, tokens] for part in hT), xT[:, :, tokens], masked[:, :, :], ch.link)
                    dve.sem_inc(hT_ready, 1)
                split_w(0, 1)
                dve.wait_ge(wg_in, 16)
                split(dve, wg2[0][:, :, :], wg2[1][:, :, :], wg[:, :, :], masked[:, :, 0:16], ch.link)

                def evacuate(i, first, more):
                    for n in range(W):
                        dve.wait_ge(tile_done, i * W + n + 1)
                        if more:
                            split_w(i + 1, n)
                        if not first:
                            dve.wait_ge(stored[n], i * 16)
                        dve.tensor_copy(o[:, n, G3:M].rearrange("p (g c) -> p g c", g=2),
                                        acc[n][:, 1:3, 0:G3]).then_inc(rest_out, 1)

                evacuate(0, True, True)
                with dve.Fori(1, ITER - 1) as i:
                    ch.enter(i - 1, 2 * W)
                    evacuate(i, False, True)
                    ch.leave(ITER - 2)
                evacuate(ITER - 1, False, False)
                dve.wait_ge(tile_done, PT + 1)
                dve.tensor_copy(og[:, G3:M].rearrange("p (g c) -> p g c", g=2),
                                acc[0][0:16, 1:3, 0:G3]).then_inc(rest_out, 1)

            @block.tensor
            def _(pe):
                def project(n, wn, m, first=False):
                    for g in range(3):
                        if first:
                            pe.wait_ge(hT_ready, g + 1)
                        for k in range(KD):
                            last = matmul3(pe, acc[n][0:m, g, 0:G3], [part[:, k, :] for part in wn],
                                           [part[:, k, g * G3:(g + 1) * G3] for part in hT],
                                           start=(k == 0), stop=(k == KD - 1))
                    last.then_inc(tile_done, 1)

                def tiles(i, first):
                    for n in range(W):
                        pe.wait_ge(w_split, i * W + n + 1)
                        if not first:
                            pe.wait_ge(first_out, (i - 1) * W + (n + 1))
                            pe.wait_ge(rest_out, (i - 1) * W + (n + 1))
                        project(n, [part[:, n, :, :] for part in w2], P, first and n == 0)

                tiles(0, True)
                with pe.Fori(1, ITER) as i:
                    tiles(i, False)
                pe.wait_ge(first_out, PT - W + 1)
                pe.wait_ge(rest_out, PT - W + 1)
                project(0, wg2, 16)


def front(nc, t):
    with ExitStack() as ctx:
        s = Stage(nc, ctx, "front")
        xT = s.sb("xT", [P, KD, M])
        modT = s.sb("modT", [P, 2, KD, NSEQ])
        with nc.cleanup_on_exit():
            modulation(nc, t, xT, modT)
        projection(nc, t, xT, modT)


GH, GV, GC = 4, 256, 64


def gla(nc, t):
    with ExitStack() as ctx:
        s = Stage(nc, ctx, "gla")
        ident = s.sb("ident", [P, P])
        mask = s.sb("mask", [P, P])
        mask_s = s.sb("mask_s", [NS, NS])
        seq_rows = s.sb("seq_rows", [NS, NB])
        starts = s.sb("starts", [P, M])
        gaT = s.sb("gaT", [16, M])
        wz = s.sb("wz", [16, P])
        cst = s.sb("cst", [P, 3])
        gain = s.sb("gain", [P, 2])
        qk = s.sb("qk", [P, 2, M])
        vg_next = s.sb("vg_next", [P, 4, M])
        v, gate = s.sb("v", [P, 2, M]), s.sb("gate", [P, 2, M])
        S_in = s.sb("S_in", [P, NB, GV])
        S_out = s.sb("S_out", [P, NB, GV])
        z = s.sb("z", [P, M])
        sp_ = s.sb("softplus", [P, M])
        B = s.sb("B", [P, M])
        up, dn, rest = s.sb("exp_up", [P, M]), s.sb("exp_down", [P, M]), s.sb("exp_rest", [P, M])
        ends = s.sb("ends", [P, SEQ // GC + NB])
        qe, ke, k2 = s.sb("qe", [P, M]), s.sb("ke", [P, M]), s.sb("k2", [P, M])
        S = s.sb("S", [P, 4, GV])
        kv = s.sb("kv", [P, 2, 3 * P])
        k2s = s.sb("k2s", [NS, NB, P])
        at = s.sb("at", [P, 2, P])
        o, og = s.sb("o", [P, 2, M]), s.sb("og", [P, 2, M])
        ones = s.sb("ones", [P, P])
        eps = s.sb("eps", [P, 1])
        sq = s.sb("sq", [P, 2 * M])
        zb = s.ps("zb", [P, 3, 512])
        at_b = s.ps("at_b")
        turn_b = s.ps("turn_b")
        o_b = s.ps("o_b")
        s_b = [s.ps(f"s_b{n}") for n in range(2)]
        N = TILES + 1
        CH = SEQ // GC
        consts_in, qk_in, vg_in, states_in = (s.sem(n) for n in ("consts_in", "qk_in", "vg_in", "states_in"))
        v_kept, gate_kept, ends_ready, gain_kept = (s.sem(n) for n in ("v_kept", "gate_kept", "ends_ready", "gain_kept"))
        cleared = s.sem("cleared")
        z_summed, z_ready, softplus_ready = s.sem("z_summed"), s.sem("z_ready"), s.sem("softplus_ready")
        B_ready, exps_ready, scaled = s.sem("B_ready"), s.sem("exps_ready"), s.sem("scaled")
        turned, kv_ready = s.sem("turned"), s.sem("kv_ready")
        at_summed, at_ready = s.sem("at_summed"), s.sem("at_ready")
        k2s_ready = s.sem("k2s_ready")
        s_summed, S_ready = s.sem("s_summed"), s.sem("S_ready")
        o_summed, o_ready = s.sem("o_summed"), s.sem("o_ready")
        squares_ready, ms_summed, rstd_ready = s.sem("squares_ready"), s.sem("ms_summed"), s.sem("rstd_ready")
        og_ready, stored, og_stored = s.sem("og_ready"), s.sem("states_stored"), s.sem("og_stored")
        own, own_act, passed = s.sem("vector_chain"), s.sem("scalar_chain"), s.sem("passed")
        US = CH + NB
        PREP = {3: "softplus", 5: "exps"}

        with nc.Block() as block:
            @block.sync
            def _(sp):
                for dst, name in ((ident, "ident"), (mask, "gla_mask"), (mask_s, "gla_mask_s"),
                                  (seq_rows, "seq_rows"), (starts, "starts"), (gaT, "gaT")):
                    src = t[name]
                    if name == "starts":
                        src = src[:, 0:M].broadcast_to([P, M])
                    sp.dma_start(dst[:, :], src).then_inc(consts_in, 16)

                def load_qk(h):
                    sp.dma_start(wz[:, :], t["w_gate"][h]).then_inc(qk_in, 16)
                    sp.dma_start(cst[:, :], t["gla_cst"][h]).then_inc(qk_in, 16)
                    sp.dma_start(qk[:, 0, :], t["pT"][h]).then_inc(qk_in, 16)
                    sp.dma_start(qk[:, 1, :], t["pT"][h + GH]).then_inc(qk_in, 16)

                def load_vg(h):
                    for n in range(2):
                        sp.dma_start(vg_next[:, n, :], t["pT"][h * 2 + (2 * GH + n)]).then_inc(vg_in, 16)
                        sp.dma_start(vg_next[:, 2 + n, :], t["pT"][h * 2 + (4 * GH + n)]).then_inc(vg_in, 16)

                def load_states(h):
                    for n in range(2):
                        sp.dma_start(S_in[:, 4 * n:4 * n + 4, :],
                                     t["state_gla"][h][:, 4 * n:4 * n + 4, :]).then_inc(states_in, 16)

                def wait(sem, value):
                    sp.wait_ge(sem, value)
                    sp.sem_inc(passed, 1)

                def head(h, more):
                    if more:
                        wait(scaled, h * 3 + 3)
                        wait(gain_kept, h + 1)
                        load_qk(h + 1)
                        wait(v_kept, h + 1)
                        wait(gate_kept, h + 1)
                        load_vg(h + 1)
                    wait(S_ready, h * (US + 1) + CH + 1)
                    sp.dma_start(t["new_gla_p"][h], S[:, CH % 4, :]).then_inc(stored, 16)
                    wait(S_ready, (h + 1) * (US + 1))
                    sp.dma_start(t["new_gla_s"][h], S_out[:, :, :]).then_inc(stored, 16)
                    if more:
                        load_states(h + 1)
                    wait(og_ready, h + 1)
                    sp.dma_start(t["ogT"][h], og[:, :, :]).then_inc(og_stored, 16)

                load_qk(0)
                load_vg(0)
                load_states(0)
                with sp.Fori(0, GH - 1) as h:
                    head(h, True)
                head(GH - 1, False)
                sp.wait_ge(stored, 16 * 2 * GH)
                sp.wait_ge(og_stored, 16 * GH)

            @block.scalar
            def _(act):
                ch = Chain(act, own_act)
                act.wait_ge(cleared, 3)

                def prep(step, h):
                    if step == "softplus":
                        act.wait_ge(z_ready, h + 1)
                        ch.link(act.activation(sp_[:, :], z[:, :], ACT.Abs))
                        ch.link(act.activation(sp_[:, :], sp_[:, :], ACT.Exp, scale=-1.0))
                        act.activation(sp_[:, :], sp_[:, :], ACT.Ln, bias=1.0).then_inc(softplus_ready, 1)
                    elif step == "exps":
                        act.wait_ge(B_ready, h + 1)
                        act.activation(up[:, :], B[:, :], ACT.Exp, scale=1.0 / 16)
                        act.activation(dn[:, :], B[:, :], ACT.Exp, scale=-1.0 / 16)
                        act.activation(rest[:, :], rest[:, :], ACT.Exp, scale=1.0 / 16).then_inc(exps_ready, 1)

                def expand(h):
                    act.wait_ge(vg_in, (h + 1) * 16 * 4)
                    act.copy(v[:, :, :], vg_next[:, 0:2, :]).then_inc(v_kept, 1)
                    act.wait_ge(exps_ready, h + 1)
                    act.copy(ends[:, 0:CH], up[:, GC - 1:SEQ:GC])
                    act.copy(ends[:, CH:CH + NB], up[:, SEQ + NT - 1:M:NT]).then_inc(ends_ready, 1)

                def head(h, first, more):
                    for i in range(N):
                        act.wait_ge(turned, h * N + i + 1)
                        if i >= 2:
                            act.wait_ge(o_summed, h * N + i - 1)
                            act.wait_ge(s_summed, h * US + 2 * (i - 1))
                        rows = P if i < TILES else NS
                        act.copy(kv[0:rows, i % 2, :], turn_b[0:rows, 0:3 * P]).then_inc(kv_ready, 1)
                        if i:
                            copy_o(h, i - 1)
                        elif not first:
                            act.wait_ge(og_ready, h)
                        if i == 0:
                            act.copy(gate[:, :, :], vg_next[:, 2:4, :]).then_inc(gate_kept, 1)
                        if more and i in PREP:
                            prep(PREP[i], h + 1)
                    copy_o(h, N - 1)
                    act.wait_ge(o_ready, h * N + N)
                    act.activation(sq[:, :], o[:, :, :].rearrange("p a m -> p (a m)"), ACT.Square).then_inc(squares_ready, 1)
                    if more:
                        act.wait_ge(S_ready, (h + 1) * (US + 1))
                        expand(h + 1)
                    act.wait_ge(ms_summed, h + 1)
                    ch.link(act.activation(z[:, :].rearrange("p (g c) -> p g c", g=3), zb[:, :, 0:G3], ACT.Ln, bias=eps[:, :]))
                    act.activation(z[:, :], z[:, :], ACT.Exp, scale=-0.5)
                    act.wait_ge(gate_kept, h + 1)
                    act.activation(sq[:, :], gate[:, :, :].rearrange("p a m -> p (a m)"), ACT.Sigmoid).then_inc(rstd_ready, 1)

                def copy_o(h, i):
                    act.wait_ge(o_summed, h * N + i + 1)
                    rows = P if i < TILES else NS
                    act.copy(o[:, :, i * P:i * P + rows],
                             o_b[:, 0:2 * rows].rearrange("p (a c) -> p a c", a=2)).then_inc(o_ready, 1)

                prep("softplus", 0)
                prep("exps", 0)
                expand(0)
                ch.enter(0, 3)
                head(0, True, True)
                ch.leave(1)
                with act.Fori(1, GH - 1) as h:
                    ch.enter(h - 1, 3)
                    head(h, False, True)
                    ch.leave(GH - 2)
                head(GH - 1, False, False)

            @block.vector
            def _(dve):
                ch = Chain(dve, own)
                dve.memset(ones[:, :], 1.0 / GV).then_inc(cleared, 1)
                dve.memset(eps[:, :], 1e-5).then_inc(cleared, 1)
                dve.memset(kv[:, :, :], 0.0).then_inc(cleared, 1)
                dve.wait_ge(consts_in, 16 * 6)

                def prep(step, h):
                    if step == "z":
                        dve.wait_ge(qk_in, (h + 1) * 16 * 4)
                        dve.wait_ge(z_summed, h + 1)
                        zv = z[:, :].rearrange("p (g c) -> p g c", g=3)
                        ch.link(dve.tensor_scalar(zv, zb[:, :, 0:G3], cst[:, 0:1], None, ALU.add))
                        dve.sem_inc(z_ready, 1)
                    elif step == "sums":
                        dve.wait_ge(softplus_ready, h + 1)
                        ch.link(dve.scalar_tensor_tensor(out=sp_[:, :], in0=z[:, :], scalar=0.0, in1=sp_[:, :],
                                                         op0=ALU.min, op1=ALU.subtract))
                        ch.link(dve.tensor_tensor_scan(B[:, :], starts[:, :], sp_[:, :], 0.0, ALU.mult, ALU.add))
                        for c0, c1, c in ((0, SEQ, GC), (SEQ, M, NT)):
                            Bc = B[:, c0:c1].rearrange("p (j c) -> p j c", c=c)
                            last = dve.tensor_tensor(rest[:, c0:c1].rearrange("p (j c) -> p j c", c=c),
                                                     Bc[:, :, c - 1:c].broadcast_to([P, (c1 - c0) // c, c]), Bc, ALU.subtract)
                        ch.link(last)
                        dve.sem_inc(B_ready, 1)

                def expand(h):
                    dve.wait_ge(exps_ready, h + 1)
                    dve.scalar_tensor_tensor(out=qe[:, :], in0=qk[:, 0, :], scalar=float(P) ** -0.5, in1=up[:, :],
                                             op0=ALU.mult, op1=ALU.mult).then_inc(scaled, 1)
                    dve.tensor_tensor(ke[:, :], qk[:, 1, :], dn[:, :], ALU.mult).then_inc(scaled, 1)
                    dve.tensor_tensor(k2[:, :], qk[:, 1, :], rest[:, :], ALU.mult).then_inc(scaled, 1)

                def head(h, first, more):
                    ch.link(dve.tensor_copy(gain[:, :], cst[:, 1:3]))
                    dve.sem_inc(gain_kept, 1)
                    if not first:
                        dve.wait_ge(stored, h * 16 * 2)
                    dve.memset(S[:, 0, :], 0.0).then_inc(S_ready, 1)
                    dve.wait_ge(ends_ready, h + 1)
                    for i in range(TILES):
                        dve.wait_ge(at_summed, h * N + i + 1)
                        if i >= 2:
                            dve.wait_ge(o_summed, h * N + i - 1)
                        dve.tensor_tensor(at[:, i % 2, :], at_b[:, 0:P], mask[:, :], ALU.mult).then_inc(at_ready, 1)
                        for j in (2 * i, 2 * i + 1):
                            dve.wait_ge(s_summed, h * US + j + 1)
                            dve.wait_ge(S_ready, h * (US + 1) + j + 1)
                            if j >= 3:
                                dve.wait_ge(o_summed, h * N + (j - 3) // 2 + 1)
                            dve.scalar_tensor_tensor(out=S[:, (j + 1) % 4, :], in0=S[:, j % 4, :],
                                                     scalar=ends[:, j:j + 1], in1=s_b[j % 2][:, 0:GV],
                                                     op0=ALU.mult, op1=ALU.add).then_inc(S_ready, 1)
                        if more and i == 1:
                            prep("z", h + 1)
                        if more and i == 3:
                            prep("sums", h + 1)
                    dve.wait_ge(at_summed, h * N + N)
                    dve.tensor_tensor(at[0:NS, 0, 0:NS], at_b[0:NS, 0:NS], mask_s[:, :], ALU.mult).then_inc(at_ready, 1)
                    dve.wait_ge(kv_ready, h * N + N)
                    dve.tensor_tensor(k2s[:, :, :], kv[0:NS, 0, 0:P].unsqueeze(1).broadcast_to([NS, NB, P]),
                                      seq_rows[:, :].unsqueeze(2).broadcast_to([NS, NB, P]),
                                      ALU.mult).then_inc(k2s_ready, 1)
                    for b in range(NB):
                        dve.wait_ge(s_summed, h * US + CH + b + 1)
                        dve.scalar_tensor_tensor(out=S_out[:, b, :], in0=S_in[:, b, :], scalar=ends[:, CH + b:CH + b + 1],
                                                 in1=s_b[b % 2][:, 0:GV], op0=ALU.mult, op1=ALU.add).then_inc(S_ready, 1)
                    if more:
                        dve.wait_ge(o_summed, (h + 1) * N)
                        expand(h + 1)
                    dve.wait_ge(rstd_ready, h + 1)
                    for n in range(2):
                        last = dve.scalar_tensor_tensor(out=gate[:, n, :], in0=gate[:, n, :], scalar=gain[:, n:n + 1],
                                                        in1=z[:, :], op0=ALU.mult, op1=ALU.mult)
                    ch.link(last)
                    gv = gate[:, :, :].rearrange("p a m -> p (a m)")
                    ov = o[:, :, :].rearrange("p a m -> p (a m)")
                    ogv = og[:, :, :].rearrange("p a m -> p (a m)")
                    if not first:
                        dve.wait_ge(og_stored, h * 16)
                    ch.link(dve.tensor_tensor(ogv, ov, gv, ALU.mult))
                    dve.tensor_tensor(ogv, ogv, sq[:, :], ALU.mult).then_inc(og_ready, 1)

                prep("z", 0)
                prep("sums", 0)
                expand(0)
                PER = 7
                ch.enter(0, PER)
                head(0, True, True)
                ch.leave(1)
                with dve.Fori(1, GH - 1) as h:
                    ch.enter(h - 1, PER)
                    head(h, False, True)
                    ch.leave(GH - 2)
                head(GH - 1, False, False)

            @block.tensor
            def _(pe):
                pe.wait_ge(consts_in, 16 * 6)
                pe.wait_ge(cleared, 3)

                def z_sums(h):
                    pe.wait_ge(qk_in, (h + 1) * 16 * 4)
                    for g in range(3):
                        last = pe.matmul(zb[:, g, 0:G3], wz[:, :], gaT[:, g * G3:(g + 1) * G3], start=True, stop=True)
                    last.then_inc(z_summed, 1)

                def head(h, first, more):
                    pe.wait_ge(scaled, h * 3 + 3)
                    pe.wait_ge(v_kept, h + 1)

                    def start(i):
                        c0, rows = i * P, P if i < TILES else NS
                        if not first or i:
                            pe.wait_ge(kv_ready, h * N + i)
                            pe.wait_ge(at_ready, h * N + i)
                        for n, src in enumerate((k2[:, c0:c0 + rows], v[:, 0, c0:c0 + rows], v[:, 1, c0:c0 + rows])):
                            last = pe.transpose(turn_b[0:rows, n * P:(n + 1) * P], src, ident[:, :])
                        last.then_inc(turned, 1)
                        pe.matmul(at_b[0:rows, 0:rows], ke[:, c0:c0 + rows], qe[:, c0:c0 + rows],
                                  start=True, stop=True).then_inc(at_summed, 1)

                    def state(lhsT, rhs, k):
                        if not first or k >= 2:
                            done = h * (US + 1) + k if k >= 2 else h * (US + 1) - 2 + k + 1
                            pe.wait_ge(S_ready, done)
                        pe.matmul(s_b[k % 2][:, 0:GV], lhsT, rhs, start=True, stop=True).then_inc(s_summed, 1)

                    def states(i):
                        pe.wait_ge(kv_ready, h * N + i + 1)
                        a = kv[:, i % 2, :]
                        for n in range(2):
                            state(a[64 * n:64 * n + 64, 0:P], a[64 * n:64 * n + 64, P:3 * P], 2 * i + n)

                    def finish(i):
                        pe.wait_ge(kv_ready, h * N + i + 1)
                        a = kv[:, i % 2, :]
                        pe.wait_ge(at_ready, h * N + i + 1)
                        if not first or i:
                            pe.wait_ge(o_ready, h * N + i)
                        rows, c0 = (P, i * P) if i < TILES else (NS, SEQ)
                        for n in range(2):
                            pe.matmul(o_b[:, n * rows:(n + 1) * rows], a[0:rows, (1 + n) * P:(2 + n) * P],
                                      at[0:rows, i % 2, 0:rows], start=(n == 0), stop=False, skip_group_check=True)
                        if i + 1 < TILES:
                            states(i + 1)
                        if i < TILES:
                            for j in (2 * i, 2 * i + 1):
                                pe.wait_ge(S_ready, h * (US + 1) + j + 1)
                                for n in range(2):
                                    c = (j % 2) * GC
                                    last = pe.matmul(o_b[:, n * rows + c:n * rows + c + GC], S[:, j % 4, n * P:(n + 1) * P],
                                                     qe[:, j * GC:(j + 1) * GC], start=False, stop=True,
                                                     skip_group_check=True)
                        else:
                            pe.wait_ge(states_in, (h + 1) * 32)
                            for b in range(NB):
                                for n in range(2):
                                    last = pe.matmul(o_b[:, n * rows + b * NT:n * rows + (b + 1) * NT],
                                                     S_in[:, b, n * P:(n + 1) * P], qe[:, c0 + b * NT:c0 + (b + 1) * NT],
                                                     start=False, stop=True, skip_group_check=True)
                        last.then_inc(o_summed, 1)
                        if i == TILES:
                            pe.wait_ge(k2s_ready, h + 1)
                            for b in range(NB):
                                state(k2s[:, b, :], a[0:NS, P:3 * P], CH + b)

                    start(0)
                    states(0)
                    for i in range(N):
                        if i + 1 < N:
                            start(i + 1)
                        finish(i)
                        if more and i == 1:
                            if not first:
                                pe.wait_ge(rstd_ready, h)
                            z_sums(h + 1)
                    pe.wait_ge(squares_ready, h + 1)
                    if more:
                        pe.wait_ge(z_ready, h + 2)
                    for g in range(3):
                        for n in range(2):
                            last = pe.matmul(zb[:, g, 0:G3], ones[:, :], sq[:, n * M + g * G3:n * M + (g + 1) * G3],
                                             start=(n == 0), stop=(n == 1))
                    last.then_inc(ms_summed, 1)

                z_sums(0)
                head(0, True, True)
                with pe.Fori(1, GH - 1) as h:
                    head(h, False, True)
                head(GH - 1, False, False)


RC, RH = 64, 64
PAIRS = 8
RW0 = 24
CHUNKS = SEQ // RC + 1
MW = CHUNKS * RC
QUADS = ((0, 4), (4, 4), (8, 4), (12, 4), (16, 1))
LEVELS = 5
DECAY = -float(np.exp(-0.5))


def rw_levels(q):
    return LEVELS if q < 4 else 1


def rw_duos(q):
    return 2 if q < 4 else 1


def rw_schedule(more):
    prep = {0: ["w", "lerp0"], 1: ["lerp1", "lerp2", "a", "kk", "scan"], 2: ["g", "km", "exps"],
            3: ["norm", "kkn"], 4: ["bonus"]}

    def free(q):
        yield ("gen", q, 0)
        for r in range(3):
            yield ("turn", q, r)
        if q == 0:
            yield ("keep", 0, 0)
        for l in range(rw_levels(q)):
            for kind in "PT":
                for d in range(rw_duos(q)):
                    yield (kind, q, (l, d))
        if more:
            for name in prep[q]:
                yield (name, q, 0)

    def sequential(q):
        c0, n = QUADS[q]
        for c in range(c0, c0 + n):
            for kind in "XUS":
                yield (kind, q, c)

    steps = list(free(0))
    for q in range(len(QUADS)):
        a, b = list(sequential(q)), list(free(q + 1)) if q + 1 < len(QUADS) else []
        order = [((n + 0.5) / len(a), 1, x) for n, x in enumerate(a)] + [((n + 0.5) / len(b), 0, x) for n, x in enumerate(b)]
        steps += [x for _, _, x in sorted(order, key=lambda o: o[:2])]
    return steps


def rwkv(nc, t):
    with ExitStack() as ctx:
        s = Stage(nc, ctx, "rw")
        ident = s.sb("ident", [P, P])
        strict = s.sb("strict", [P, 2, P])
        incl = s.sb("incl", [P, 2, RC])
        first_l = s.sb("first_l", [P, P])
        first_u = s.sb("first_u", [P, P])
        join = s.sb("join", [P, LEVELS, P])
        seq_cols = s.sb("seq_cols", [P, NB, P])
        seq_rows = s.sb("seq_rows", [P, NB])
        starts = s.sb("starts", [P, MW])
        heads = s.sb("heads", [P, P])
        mean = s.sb("mean", [P, P])
        cst_all = s.sb("cst_all", [P, PAIRS, 10])
        cst, norm_cst = s.sb("cst", [P, 11]), s.sb("norm_cst", [P, 2])
        mu_wg, sh_wg = s.sb("mu_wg", [P, 2]), s.sb("sh_wg", [P, 2, NB])
        raw = s.sb("raw", [P, 3, M])
        sh = s.sb("sh", [P, 3, NB])
        sho = s.sb("sho", [P, 3, NSEQ])
        wa = s.sb("wa", [P, M])
        gl = s.sb("gl", [P, M])
        w2a2, g2 = s.sb("w2a2", [P, P]), s.sb("g2", [P, P])
        rkv = s.sb("rkv", [P, 3, MW])
        d = s.sb("d", [P, M])
        sg, gt = s.sb("sg", [P, MW]), s.sb("gt", [P, M])
        av_all = s.sb("av", [P, MW])
        av = av_all[:, 0:M]
        gt_next = s.sb("gt_next", [P, M])
        Ls, Lp = s.sb("Ls", [P, MW]), sg
        Ei, Ed = s.sb("Ei", [P, MW]), s.sb("Ed", [P, MW])
        ends = s.sb("ends", [P, SEQ // RC + NB])
        kk, rn = s.sb("kk", [P, MW]), s.sb("rn", [P, M])
        km = s.sb("km", [P, M])
        bv = s.sb("bv", [P, M])
        ar = s.sb("ar", [P, 2, MW])
        aB, bB, kB, vB = (s.sb(n, [P, CHUNKS, P]) for n in ("aB", "bB", "kB", "vB"))
        abT = s.sb("abT", [P, 4, P])
        akT = s.sb("akT", [P, 2, 4, P])
        rbT, rkT = s.sb("rbT", [P, 2, 4, RC]), s.sb("rkT", [P, 2, 4, RC])
        nat = s.sb("nat", [P, 2, 3, 4, P])
        Tf = s.sb("Tf", [P, 2, 4, P])
        T = s.sb("T", [P, 2, 2, 2, P])
        Pm = s.sb("Pm", [P, 4, P])
        An = s.sb("An", [P, LEVELS, 4, P])
        Xs, Us = s.sb("Xs", [P, P]), s.sb("Us", [P, P])
        S, Su = s.sb("S", [P, 2, P]), s.sb("Su", [P, P])
        S_in, S_out = s.sb("S_in", [P, NB, P]), s.sb("S_out", [P, NB, P])
        a_seq = s.sb("a_seq", [P, NB, P])
        bk_seq = An[:, 1:LEVELS, :, :].rearrange("p l i s -> p (l i s)").rearrange("p (n b s) -> p n b s", n=2, b=NB)
        oT = s.sb("oT", [P, MW])
        eps = s.sb("eps", [P, 2])
        zb = s.ps("zb", [P, 3, 512])
        p_hi, turn_b, xu_b, s_b, o_b = (s.ps(n) for n in ("p_hi", "turn_b", "xu_b", "s_b", "o_b"))
        p_b = (zb[:, 0, :], p_hi[:, :])
        t_b = (zb[:, 1, :], zb[:, 2, :])
        x_b, u_b = xu_b[:, 0:P], xu_b[:, P:2 * P]

        NAMES = ("consts_in pair_in states_in cleared sho_ready lerped sg_ready av_ready gt_ready exps_ready "
                 "squares rn_ready vB_ready aB_ready kk_ready L_ready ss_ready km_ready scaled ar_ready bv_ready "
                 "cst_ready ends_ready kept d_squared out_stored "
                 "w_summed gen_summed gen_ready abT_ready joins_ready turned nat_ready p_summed p_ready t_summed "
                 "T_ready x_summed x_ready u_summed u_ready s_summed S_ready o_summed o_ready a_seq_ready "
                 "bk_seq_ready d_ready rstd_ready out_ready shift_stored stored own own_act wa_ready "
                 "norm_summed").split()
        sem = {n: s.sem(n) for n in NAMES}
        (consts_in, pair_in, states_in, cleared, sho_ready, lerped, sg_ready, av_ready, gt_ready, exps_ready,
         squares, rn_ready, vB_ready, aB_ready, kk_ready, L_ready, ss_ready, km_ready, scaled, ar_ready, bv_ready,
         cst_ready, ends_ready, kept, d_squared, out_stored,
         w_summed, gen_summed, gen_ready, abT_ready, joins_ready, turned, nat_ready, p_summed, p_ready, t_summed,
         T_ready, x_summed, x_ready, u_summed, u_ready, s_summed, S_ready, o_summed, o_ready, a_seq_ready,
         bk_seq_ready, d_ready, rstd_ready, out_ready, shift_stored, stored, own, own_act, wa_ready,
         norm_summed) = (sem[n] for n in NAMES)

        NQ, C = len(QUADS), CHUNKS
        NP = sum(rw_levels(q) * rw_duos(q) for q in range(NQ))
        NJ = sum(rw_levels(q) for q in range(NQ))
        NTR = NP + NQ
        NSS = (C - 1) + 2
        NSR = 1 + NSS
        ZS = 5
        CONSTS = 15
        PREP = ("w", "lerp0", "lerp1", "lerp2", "a", "kk", "scan", "g", "km", "exps", "norm", "kkn", "bonus")

        def p_at(q, l, d):
            return 10 * q + 2 * l + d + 1

        def T_at(q, l, d):
            return 11 * q + 1 + (2 * l + d + 1 if l >= 0 else 0)

        def last_at(at, q):
            return at(q, rw_levels(q) - 1, rw_duos(q) - 1)

        with nc.Block() as block:
            @block.sync
            def _(sp):
                for dst, name in ((ident, "ident"), (strict, "rw_strict"), (incl, "rw_incl"), (first_l, "rw_first_l"),
                                  (first_u, "rw_first_u"), (join, "rw_join"), (seq_cols, "rw_seq_cols"),
                                  (seq_rows, "rw_seq_rows"), (starts, "starts"), (heads, "rw_heads"), (mean, "rw_mean"),
                                  (cst_all, "rw_cst"), (mu_wg, "rw_mu_wg"), (sh_wg, "rw_sh_wg")):
                    src = t[name]
                    if name == "starts":
                        src = src.broadcast_to([P, MW])
                    if len(src.shape) == 3:
                        sp.dma_start(dst[:, :, :], src).then_inc(consts_in, 16)
                    else:
                        sp.dma_start(dst[:, :], src).then_inc(consts_in, 16)
                sp.dma_start(raw[:, 0:2, :], t["pT"][RW0 + 24:RW0 + 26].rearrange("n p m -> p n m")).then_inc(consts_in, 16)
                sp.wait_ge(sho_ready, 1)
                sp.dma_start(t["new_shift_wg"].rearrange("n p b -> p n b"), sho[:, 0:2, :]).then_inc(shift_stored, 16)
                sp.wait_ge(wa_ready, 1)
                sp.wait_ge(cleared, 13)

                def load(j):
                    for n in range(3):
                        sp.dma_start(raw[:, n, :], t["pT"][j + (RW0 + 8 * n)]).then_inc(pair_in, 16)
                    sp.dma_start(sh[:, :, :], t["rw_sh"][j]).then_inc(pair_in, 16)
                    sp.dma_start(w2a2[:, :], t["w2a2"][j]).then_inc(pair_in, 16)
                    sp.dma_start(g2[:, :], t["g2"][j]).then_inc(pair_in, 16)

                def load_states(j):
                    for n in range(2):
                        sp.dma_start(S_in[64 * n:64 * n + 64, :, 64 * n:64 * n + 64],
                                     t["state_rwkv"][j][n]).then_inc(states_in, 16)

                def middle(j):
                    sp.wait_ge(sho_ready, j + 2)
                    sp.dma_start(t["new_shift"][j].rearrange("n p b -> p n b"), sho[:, :, :]).then_inc(shift_stored, 16)

                def store(j):
                    sp.wait_ge(S_ready, (j + 1) * NSR)
                    for n in range(2):
                        a, b = 64 * n, 64 * n + 64
                        sp.dma_start(t["new_rw_p"][j][n], S[a:b, 0, a:b]).then_inc(stored, 16)
                        sp.dma_start(t["new_rw_s"][j][n], S_out[a:b, :, a:b]).then_inc(stored, 16)

                def store_out(j):
                    sp.wait_ge(out_ready, j + 1)
                    sp.dma_start(t["orT"][j], d[:, :]).then_inc(out_stored, 16)

                load(0)
                load_states(0)
                middle(0)
                sp.wait_ge(gt_ready, 1)
                sp.wait_ge(lerped, 3)
                load(1)
                def next_pair(j, more):
                    middle(j + 1)
                    if more:
                        sp.wait_ge(gt_ready, j + 2)
                        sp.wait_ge(lerped, j * 3 + 6)
                        load(j + 2)
                    store(j)
                    load_states(j + 1)
                    store_out(j)

                with sp.Fori(0, PAIRS - 2) as j:
                    next_pair(j, True)
                next_pair(PAIRS - 2, False)
                store(PAIRS - 1)
                store_out(PAIRS - 1)
                sp.wait_ge(shift_stored, 16 * (PAIRS + 1))
                sp.wait_ge(stored, 16 * 4 * PAIRS)
                sp.wait_ge(out_stored, 16 * PAIRS)

            def samples(ap):
                return ap[:, SEQ:M].rearrange("p (b c) -> p b c", c=NT)

            @block.scalar
            def _(act):
                ch = Chain(act, own_act)
                act.wait_ge(consts_in, 16 * CONSTS)
                act.copy(sho[:, 0:2, :], raw[:, 0:2, SEQ - 1:M:NT]).then_inc(sho_ready, 1)
                act.wait_ge(wa_ready, 1)
                act.activation(wa[0:64, :], wa[0:64, :], ACT.Tanh).then_inc(own_act, 1)
                act.activation(gl[:, :], gl[:, :], ACT.Sigmoid).then_inc(own_act, 1)

                def prep(name, j, first=False):
                    if name == "lerp0":
                        act.wait_ge(pair_in, (j + 1) * 16 * 6)
                        act.wait_ge(shift_stored, (j + 1) * 16)
                        act.copy(sho[:, :, :], raw[:, :, SEQ - 1:M:NT]).then_inc(sho_ready, 1)
                    elif name == "w":
                        act.wait_ge(w_summed, j * ZS + 1)
                        act.wait_ge(cst_ready, j + 1)
                        act.activation(sg[:, 0:M].rearrange("p (g c) -> p g c", g=3), zb[:, :, 0:G3], ACT.Sigmoid,
                                       bias=cst[:, 3:4]).then_inc(sg_ready, 1)
                    elif name == "a":
                        act.wait_ge(w_summed, j * ZS + 2)
                        act.activation(av[:, :].rearrange("p (g c) -> p g c", g=3), zb[:, :, 0:G3], ACT.Sigmoid,
                                       bias=cst[:, 4:5]).then_inc(av_ready, 1)
                    elif name == "g":
                        act.wait_ge(w_summed, j * ZS + 3)
                        if not first:
                            act.wait_ge(kept, j * 2)
                        act.copy(gt_next[:, :].rearrange("p (g c) -> p g c", g=3), zb[:, :, 0:G3]).then_inc(gt_ready, 1)
                    elif name == "kk":
                        act.wait_ge(kk_ready, j + 1)
                        act.activation(rn[:, :], kk[:, 0:M], ACT.Square).then_inc(squares, 1)
                    elif name == "exps":
                        act.wait_ge(L_ready, j + 1)
                        if not first:
                            act.wait_ge(ends_ready, j)
                        act.activation(Ei[:, :], Ls[:, :], ACT.Exp, scale=DECAY)
                        act.activation(Ed[:, :], Ls[:, :], ACT.Exp, scale=-DECAY)
                        act.activation(Lp[:, :], Lp[:, :], ACT.Exp, scale=DECAY).then_inc(exps_ready, 1)
                    elif name == "norm":
                        act.wait_ge(ss_ready, j + 1)
                        ch.link(act.activation(rn[:, :], rn[:, :], ACT.Ln, scale=2.0 ** 32))
                        act.activation(rn[:, :], rn[:, :], ACT.Exp, scale=-0.5, bias=eps[:, 1:2]).then_inc(rn_ready, 1)

                def expand(j):
                    act.wait_ge(exps_ready, j + 1)
                    act.copy(ends[:, 0:C - 1], Ei[:, RC - 1:SEQ:RC])
                    act.copy(ends[:, C - 1:C - 1 + NB], Ei[:, SEQ + NT - 1:M:NT]).then_inc(ends_ready, 1)
                    act.wait_ge(lerped, (j + 1) * 3)
                    for n in range(2):
                        a = 64 * n
                        act.copy(vB[a:a + 64, :, a:a + 64],
                                 rkv[a:a + 64, 2, :].rearrange("p (c s) -> p c s", s=RC)).then_inc(vB_ready, 1)
                    act.wait_ge(ar_ready, j + 1)
                    for n in range(2):
                        a = 64 * n
                        act.copy(aB[a:a + 64, :, a:a + 64],
                                 ar[a:a + 64, 0, :].rearrange("p (c s) -> p c s", s=RC)).then_inc(aB_ready, 1)

                def pair(j, first, more):
                    for kind, q, c in rw_schedule(more):
                        n = QUADS[q][1]
                        if kind == "turn":
                            act.wait_ge(turned, j * 3 * NQ + 3 * q + c + 1)
                            if q >= 2 and c == 0:
                                act.wait_ge(o_summed, j * C + 4 * (q - 1))
                            act.copy(nat[:, q % 2, c, 0:n, :],
                                     turn_b[:, 0:n * P].rearrange("p (i s) -> p i s", i=n)).then_inc(nat_ready, 1)
                        elif kind == "P":
                            (l, duo), m = c, min(n, 2)
                            act.wait_ge(p_summed, j * NP + p_at(q, l, duo))
                            act.copy(Pm[:, 2 * duo:2 * duo + m, :],
                                     p_b[duo][:, 0:m * P].rearrange("p (i s) -> p i s", i=m)).then_inc(p_ready, 1)
                        elif kind == "X":
                            act.wait_ge(x_summed, j * C + c + 1)
                            act.copy(Xs[:, :], x_b[:, 0:P]).then_inc(x_ready, 1)
                        elif kind == "S" and (c % 8 == 7 or c == C - 1):
                            act.wait_ge(o_summed, j * C + c + 1)
                            c0 = c // 8 * 8
                            act.copy(oT[:, c0 * RC:(c + 1) * RC], o_b[:, 0:(c + 1 - c0) * RC]).then_inc(o_ready, 1)
                        elif kind == "keep":
                            act.wait_ge(bv_ready, j + 1)
                            act.wait_ge(gt_ready, j + 1)
                            if not first:
                                act.wait_ge(out_ready, j)
                            act.copy(gt[:, :], gt_next[:, :]).then_inc(kept, 1)
                            act.copy(bv[:, :], km[:, :]).then_inc(kept, 1)
                        else:
                            prep(kind, j + 1)
                    act.wait_ge(d_ready, j + 1)
                    if more:
                        act.wait_ge(rn_ready, j + 2)
                    act.activation(rn[:, :], d[:, :], ACT.Square).then_inc(d_squared, 1)
                    if more:
                        expand(j + 1)
                    act.wait_ge(norm_summed, 2 * j + 2)
                    ch.link(act.activation(rn[:, :].rearrange("p (g c) -> p g c", g=3), zb[:, :, 0:G3], ACT.Ln,
                                           bias=eps[:, 0:1]))
                    act.activation(rn[:, :], rn[:, :], ACT.Exp, scale=-0.5).then_inc(rstd_ready, 1)

                ch.n = 2
                for name in PREP:
                    prep(name, 0, True)
                expand(0)
                ch.enter(0, 2)
                pair(0, True, True)
                ch.leave(1)
                with act.Fori(1, PAIRS - 1) as j:
                    ch.enter(j - 1, 2)
                    pair(j, False, True)
                    ch.leave(PAIRS - 2)
                pair(PAIRS - 1, False, False)

            @block.vector
            def _(dve):
                ch = Chain(dve, own)
                for buf in (aB, bB, kB, vB, S_in):
                    dve.memset(buf[:, :, :], 0.0).then_inc(cleared, 1)
                for buf in (rkv[:, 0, M:MW], rkv[:, 1, M:MW], rkv[:, 2, M:MW], sg[:, M:MW], kk[:, M:MW], av_all[:, M:MW]):
                    dve.memset(buf, 0.0).then_inc(cleared, 1)
                dve.memset(eps[:, 0:1], 64e-5).then_inc(cleared, 1)
                dve.memset(eps[:, 1:2], 16.0 * float(np.log(2.0))).then_inc(cleared, 1)
                dve.wait_ge(consts_in, 16 * CONSTS)
                dve.wait_ge(cleared, 13)

                def lerp(out, x, shift, mu):
                    dve.tensor_tensor(d[:, 1:SEQ], x[:, 0:SEQ - 1], x[:, 1:SEQ], ALU.subtract)
                    dve.tensor_scalar(d[:, 0:1], x[:, 0:1], -1.0, None, ALU.mult)
                    xs, ds = samples(x), samples(d)
                    dve.tensor_tensor(ds[:, :, 1:NT], xs[:, :, 0:NT - 1], xs[:, :, 1:NT], ALU.subtract)
                    ch.link(dve.tensor_tensor(ds[:, :, 0], shift, xs[:, :, 0], ALU.subtract))
                    return dve.scalar_tensor_tensor(out=out, in0=d[:, :], scalar=mu, in1=x, op0=ALU.mult, op1=ALU.add)

                ch.link(lerp(wa[:, :], raw[:, 0, :], sh_wg[:, 0, :], mu_wg[:, 0:1]))
                ch.link(lerp(gl[:, :], raw[:, 1, :], sh_wg[:, 1, :], mu_wg[:, 1:2]))
                dve.wait_ge(sho_ready, 1)
                dve.sem_inc(wa_ready, 1)

                def halves(out, x, y):
                    for n in range(2):
                        a = 64 * n
                        last = dve.tensor_tensor(out[a:a + 64, :, a:a + 64],
                                                 x[a:a + 64, :].rearrange("p (c s) -> p c s", s=RC),
                                                 y[a:a + 64, :].rearrange("p (c s) -> p c s", s=RC), ALU.mult)
                    return last

                g3 = lambda x: x.rearrange("p (g c) -> p g c", g=3)
                R, K, V = rkv[:, 0, :], rkv[:, 1, :], rkv[:, 2, :]

                def prep(name, j, first=False):
                    if name == "w":
                        ch.link(dve.tensor_copy(cst[:, 0:10], cst_all[:, 0, :] if first else
                                                cst_all[:, bass.ds(j, 1), :].rearrange("p o c -> p (o c)")))
                        ch.link(dve.tensor_scalar(cst[:, 10:11], cst[:, 6:7], -1.0, 1.0, ALU.mult, ALU.add))
                        dve.sem_inc(cst_ready, 1)
                    elif name[:4] == "lerp":
                        n = int(name[4])
                        if n == 0:
                            dve.wait_ge(pair_in, (j + 1) * 16 * 6)
                            if not first:
                                dve.wait_ge(scaled, j * 3)
                                dve.wait_ge(ar_ready, j)
                                dve.wait_ge(vB_ready, j * 2)
                        ch.link(lerp(rkv[:, n, 0:M], raw[:, n, :], sh[:, n, :], cst[:, n:n + 1]))
                        dve.sem_inc(lerped, 1)
                    elif name == "kk":
                        dve.tensor_scalar(kk[:, 0:M], K[:, 0:M], cst[:, 5:6], None, ALU.mult).then_inc(kk_ready, 1)
                    elif name == "scan":
                        dve.wait_ge(sg_ready, j + 1)
                        ch.link(dve.tensor_tensor_scan(Ls[:, :], starts[:, :], sg[:, :], 0.0, ALU.mult, ALU.add))
                        dve.tensor_tensor(Lp[:, :], Ls[:, :], sg[:, :], ALU.subtract).then_inc(L_ready, 1)
                    elif name == "km":
                        dve.wait_ge(av_ready, j + 1)
                        if not first:
                            dve.wait_ge(kept, j * 2)
                        ch.link(dve.tensor_scalar(km[:, :], av[:, :], cst[:, 6:7], cst[:, 10:11], ALU.mult, ALU.add))
                        ch.link(dve.tensor_tensor(K[:, 0:M], K[:, 0:M], km[:, :], ALU.mult))
                        dve.scalar_tensor_tensor(out=km[:, :], in0=R[:, 0:M], scalar=cst[:, 7:8], in1=K[:, 0:M],
                                                 op0=ALU.mult, op1=ALU.mult).then_inc(km_ready, 1)
                    elif name == "norm":
                        dve.wait_ge(w_summed, j * ZS + 4)
                        dve.tensor_scalar(g3(rn[:, :]), zb[:, :, 0:G3], 1e-24, None, ALU.max).then_inc(ss_ready, 1)
                    elif name == "kkn":
                        dve.wait_ge(rn_ready, j + 1)
                        ch.link(dve.tensor_tensor(kk[:, 0:M], kk[:, 0:M], rn[:, :], ALU.mult))
                        ch.link(dve.tensor_tensor(av[:, :], kk[:, 0:M], av[:, :], ALU.mult))
                    elif name == "bonus":
                        dve.wait_ge(w_summed, j * ZS + 5)
                        dve.tensor_tensor(g3(km[:, :]), g3(V[:, 0:M]), zb[:, :, 0:G3], ALU.mult).then_inc(bv_ready, 1)

                def expand(j):
                    dve.wait_ge(exps_ready, j + 1)
                    dve.scalar_tensor_tensor(out=ar[:, 0, :], in0=kk[:, :], scalar=-1.0, in1=Lp[:, :],
                                             op0=ALU.mult, op1=ALU.mult).then_inc(ar_ready, 1)
                    dve.tensor_tensor(ar[:, 1, :], R, Ei[:, :], ALU.mult).then_inc(scaled, 1)
                    halves(kB, K, Ed).then_inc(scaled, 1)
                    halves(bB, av_all, Ed).then_inc(scaled, 1)

                def pair(j, first, more):
                    if not first:
                        dve.wait_ge(stored, j * 16 * 4)
                    ch.link(dve.memset(S[:, 0, :], 0.0))
                    dve.sem_inc(S_ready, 1)
                    ch.link(dve.tensor_copy(norm_cst[:, :], cst[:, 8:10]))
                    dve.wait_ge(ends_ready, j + 1)
                    for kind, q, c in rw_schedule(more):
                        n = QUADS[q][1]
                        smp = q == NQ - 1
                        b4 = lambda ap: ap.rearrange("p (i s) -> p i s", i=n)
                        if kind == "gen":
                            dve.wait_ge(gen_summed, j * NQ + q + 1)
                            if q >= 2:
                                dve.wait_ge(o_summed, j * C + 4 * (q - 1))
                            if q or not first:
                                dve.wait_ge(joins_ready, j * NJ + LEVELS * q)
                            for bank, big, small in ((0, abT[:, 0:n, :], rbT), (1, akT[:, q % 2, 0:n, :], rkT)):
                                src = zb[:, bank, 0:n * P].rearrange("p (i a s) -> p i a s", i=n, a=2)
                                if n > 1:
                                    for h2 in range(2):
                                        last = dve.tensor_tensor(big[:, :, h2 * RC:(h2 + 1) * RC], src[:, :, 0, :],
                                                                 strict[:, 0, h2 * RC:(h2 + 1) * RC].unsqueeze(1).broadcast_to([P, n, RC]),
                                                                 ALU.mult)
                                    dve.tensor_tensor(small[:, q % 2, 0:n, :], src[:, :, 1, :],
                                                      incl[:, 0, :].unsqueeze(1).broadcast_to([P, n, RC]), ALU.mult)
                                else:
                                    for h2 in range(2):
                                        last = dve.tensor_tensor(big[:, 0, h2 * RC:(h2 + 1) * RC], src[:, 0, 0, :],
                                                                 strict[:, 1, h2 * RC:(h2 + 1) * RC], ALU.mult)
                                    dve.tensor_tensor(small[:, q % 2, 0, :], src[:, 0, 1, :], incl[:, 1, :], ALU.mult)
                                if bank == 0:
                                    ch.link(last)
                                    dve.sem_inc(abT_ready, 1)
                            if n > 1:
                                form = lambda ap: ap.rearrange("p (d c) s -> p d c s", c=2)
                                Tv, TTv = T[:, :, 0, :, :], T[:, :, 1, :, :]
                            else:
                                form = lambda ap: ap
                                Tv, TTv = T[:, 0, 0, 0:1, :], T[:, 0, 1, 0:1, :]
                            each = lambda ap: form(ap.unsqueeze(1).broadcast_to([P, n, P]))
                            dve.tensor_tensor(Tv, form(b4(zb[:, 2, 0:n * P])), each(first_l[:, :]), ALU.mult)
                            ch.link(dve.tensor_tensor(TTv, form(abT[:, 0:n, :]), each(first_u[:, :]), ALU.mult))
                            dve.sem_inc(gen_ready, 1)
                            dve.tensor_tensor(Tv, Tv, each(ident[:, :]), ALU.add)
                            dve.tensor_tensor(TTv, TTv, each(ident[:, :]), ALU.add).then_inc(T_ready, 1)
                        elif kind == "T":
                            (l, duo), m = c, min(n, 2)
                            dve.wait_ge(t_summed, j * NP + p_at(q, l, duo))
                            if l + 1 < rw_levels(q):
                                Td = T[:, duo, :, :, :].rearrange("p a c s -> p (a c s)")
                                dve.tensor_tensor(Td, Td, t_b[duo], ALU.add).then_inc(T_ready, 1)
                            else:
                                dve.tensor_tensor(Tf[:, q % 2, 2 * duo:2 * duo + m, :], T[:, duo, 1, 0:m, :],
                                                  t_b[duo][:, 2 * P:(2 + m) * P].rearrange("p (i s) -> p i s", i=m),
                                                  ALU.add).then_inc(T_ready, 1)
                        elif kind == "U":
                            dve.wait_ge(u_summed, j * C + c + 1)
                            dve.tensor_copy(Us[:, :], u_b[:, 0:P]).then_inc(u_ready, 1)
                        elif kind == "X" and not smp:
                            dve.wait_ge(S_ready, j * NSR + c + 1)
                            ch.link(dve.tensor_scalar(Su[:, :], S[:, c % 2, :], ends[:, c:c + 1], None, ALU.mult))
                        elif kind == "S" and not smp:
                            dve.wait_ge(s_summed, j * NSS + c + 1)
                            dve.scalar_tensor_tensor(out=S[:, (c + 1) % 2, :], in0=s_b[:, 0:P], scalar=ends[:, c:c + 1],
                                                     in1=Su[:, :], op0=ALU.mult, op1=ALU.add).then_inc(S_ready, 1)
                        elif kind == "S":
                            for h in range(2):
                                dve.wait_ge(s_summed, j * NSS + c + h + 1)
                                four = slice(4 * h, 4 * h + 4)
                                ch.link(dve.tensor_tensor(S_out[:, four, :], S_in[:, four, :],
                                                          (s_b, xu_b)[h][:, :].rearrange("p (b s) -> p b s", b=4), ALU.add))
                                dve.tensor_tensor(S_out[:, four, :], S_out[:, four, :],
                                                  ends[:, C - 1 + 4 * h:C + 3 + 4 * h].unsqueeze(2).broadcast_to([P, 4, P]),
                                                  ALU.mult).then_inc(S_ready, 1)
                        elif kind[:4] not in ("turn", "keep", "P", "X"):
                            if kind == "lerp0" and not first:
                                dve.wait_ge(out_stored, j * 16)
                            prep(kind, j + 1)
                    dve.wait_ge(norm_summed, 2 * j + 1)
                    if not more:
                        dve.wait_ge(out_stored, j * 16)
                    dve.tensor_tensor(g3(d[:, :]), g3(oT[:, 0:M]), zb[:, :, 0:G3], ALU.subtract).then_inc(d_ready, 1)
                    if more:
                        expand(j + 1)
                    dve.wait_ge(rstd_ready, j + 1)
                    ch.link(dve.tensor_tensor(d[:, :], d[:, :], rn[:, :], ALU.mult))
                    ch.link(dve.tensor_scalar(d[:, :], d[:, :], norm_cst[:, 0:1], norm_cst[:, 1:2], ALU.mult, ALU.add))
                    ch.link(dve.tensor_tensor(d[:, :], d[:, :], bv[:, :], ALU.add))
                    dve.tensor_tensor(d[:, :], d[:, :], gt[:, :], ALU.mult).then_inc(out_ready, 1)

                for name in PREP:
                    prep(name, 0, True)
                expand(0)
                PER = 46
                ch.enter(0, PER)
                pair(0, True, True)
                ch.leave(1)
                with dve.Fori(1, PAIRS - 1) as j:
                    ch.enter(j - 1, PER)
                    pair(j, False, True)
                    ch.leave(PAIRS - 2)
                pair(PAIRS - 1, False, False)

            @block.gpsimd
            def _(pool):
                pool.wait_ge(consts_in, 16 * CONSTS)

                def pair(j, first):
                    for kind, q, c in rw_schedule(False):
                        n = QUADS[q][1]
                        if kind == "gen":
                            pool.wait_ge(abT_ready, j * NQ + q + 1)
                            if q or not first:
                                pool.wait_ge(p_summed, j * NP + 10 * q)
                            if not first and q == 0:
                                pool.wait_ge(s_summed, j * NSS)
                            for l in range(rw_levels(q)):
                                pool.tensor_tensor(An[:, l, 0:n, :], abT[:, 0:n, :],
                                                   join[:, l, :].unsqueeze(1).broadcast_to([P, n, P]),
                                                   ALU.mult).then_inc(joins_ready, 1)
                    pool.wait_ge(aB_ready, 2 * (j + 1))
                    if not first:
                        pool.wait_ge(s_summed, j * NSS)
                    pool.tensor_tensor(a_seq[:, :, :], aB[:, C - 1, :].unsqueeze(1).broadcast_to([P, NB, P]),
                                       seq_cols[:, :, :], ALU.mult).then_inc(a_seq_ready, 1)
                    pool.wait_ge(nat_ready, (j + 1) * 3 * NQ)
                    for n in range(2):
                        last = pool.tensor_tensor(bk_seq[:, n, :, :],
                                                  nat[:, (NQ - 1) % 2, n, 0, :].unsqueeze(1).broadcast_to([P, NB, P]),
                                                  seq_rows[:, :].unsqueeze(2).broadcast_to([P, NB, P]), ALU.mult)
                    last.then_inc(bk_seq_ready, 1)

                pair(0, True)
                with pool.Fori(1, PAIRS) as j:
                    pair(j, False)

            @block.tensor
            def _(pe):
                pe.wait_ge(consts_in, 16 * CONSTS)
                pe.wait_ge(cleared, 13)
                pe.wait_ge(own_act, 2)

                def sum3(lhsT, rhs, sem):
                    for g in range(3):
                        last = pe.matmul(zb[:, g, 0:G3], lhsT, rhs[:, g * G3:(g + 1) * G3], start=True, stop=True)
                    last.then_inc(sem, 1)

                def prep(name, j):
                    if name == "w":
                        pe.wait_ge(pair_in, (j + 1) * 16 * 6)
                        sum3(w2a2[0:64, :], wa[0:64, :], w_summed)
                    elif name == "a":
                        pe.wait_ge(sg_ready, j + 1)
                        sum3(w2a2[64:128, :], wa[64:128, :], w_summed)
                    elif name == "g":
                        pe.wait_ge(av_ready, j + 1)
                        sum3(g2[:, :], gl[:, :], w_summed)
                    elif name == "norm":
                        pe.wait_ge(gt_ready, j + 1)
                        pe.wait_ge(squares, j + 1)
                        sum3(heads[:, :], rn[:, :], w_summed)
                    elif name == "bonus":
                        pe.wait_ge(ss_ready, j + 1)
                        pe.wait_ge(km_ready, j + 1)
                        sum3(heads[:, :], km[:, :], w_summed)

                def pair(j, first, more):
                    pe.wait_ge(bv_ready, j + 1)
                    if not first:
                        pe.wait_ge(rstd_ready, j)
                    pe.wait_ge(scaled, 3 * (j + 1))
                    pe.wait_ge(aB_ready, 2 * (j + 1))
                    pe.wait_ge(vB_ready, 2 * (j + 1))
                    for kind, q, c in rw_schedule(more):
                        c0, n = QUADS[q]
                        if kind in ("w", "a", "g", "norm", "bonus"):
                            pe.wait_ge(p_ready, j * NP + last_at(p_at, q))
                            pe.wait_ge(T_ready, j * NTR + last_at(T_at, q))
                            prep(kind, j + 1)
                        if kind == "gen":
                            if q:
                                pe.wait_ge(p_ready, j * NP + last_at(p_at, q - 1))
                                pe.wait_ge(T_ready, j * NTR + last_at(T_at, q - 1))
                                if more:
                                    pe.wait_ge((sg_ready, av_ready, gt_ready, ss_ready)[q - 1], j + 2)
                            for i in range(n):
                                cols = slice((c0 + i) * RC, (c0 + i + 1) * RC)
                                dst = slice(i * P, (i + 1) * P)
                                pe.matmul(zb[:, 0, dst], bB[:, c0 + i, :], ar[:, :, cols], start=True, stop=True)
                                pe.matmul(zb[:, 1, dst], kB[:, c0 + i, :], ar[:, :, cols], start=True, stop=True)
                                last = pe.matmul(zb[:, 2, dst], aB[:, c0 + i, :], bB[:, c0 + i, :], start=True, stop=True)
                            last.then_inc(gen_summed, 1)
                        elif kind == "turn":
                            if q or c or not first:
                                pe.wait_ge(nat_ready, j * 3 * NQ + 3 * q + c)
                            for i in range(n):
                                last = pe.transpose(turn_b[:, i * P:(i + 1) * P], (bB, kB, vB)[c][:, c0 + i, :], ident[:, :])
                            last.then_inc(turned, 1)
                        elif kind == "P":
                            pe.wait_ge(gen_ready, j * NQ + q + 1)
                            pe.wait_ge(joins_ready, j * NJ + LEVELS * q + c[0] + 1)
                            l, duo = c
                            pe.wait_ge(T_ready, j * NTR + T_at(q, l - 1, duo))
                            for i in range(min(n, 2)):
                                last = pe.matmul(p_b[duo][:, i * P:(i + 1) * P], An[:, l, 2 * duo + i, :], T[:, duo, 0, i, :],
                                                 start=True, stop=True)
                            last.then_inc(p_summed, 1)
                        elif kind == "T":
                            l, duo = c
                            pe.wait_ge(p_ready, j * NP + p_at(q, l, duo))
                            for i in range(min(n, 2)):
                                if l + 1 < rw_levels(q):
                                    pe.matmul(t_b[duo][:, i * P:(i + 1) * P], T[:, duo, 1, i, :], Pm[:, 2 * duo + i, :],
                                              start=True, stop=True)
                                last = pe.matmul(t_b[duo][:, (2 + i) * P:(3 + i) * P], Pm[:, 2 * duo + i, :], T[:, duo, 1, i, :],
                                                 start=True, stop=True)
                            last.then_inc(t_summed, 1)
                        elif kind == "X":
                            i, b2 = c - c0, q % 2
                            pe.wait_ge(T_ready, j * NTR + T_at(q, rw_levels(q) - 1, i // 2))
                            pe.wait_ge(nat_ready, j * 3 * NQ + 3 * q + 3)
                            if c or not first:
                                pe.wait_ge(x_ready, j * C + c)
                            if c < C - 1:
                                pe.wait_ge(S_ready, j * NSR + c + 1)
                                pe.matmul(x_b[:, 0:P], aB[:, c, :], S[:, c % 2, :], start=True, stop=False)
                            else:
                                pe.wait_ge(states_in, (j + 1) * 32)
                                pe.wait_ge(a_seq_ready, j + 1)
                                for b in range(NB):
                                    pe.matmul(x_b[:, 0:P], a_seq[:, b, :], S_in[:, b, :], start=(b == 0), stop=False)
                            pe.matmul(x_b[:, 0:P], akT[:, b2, i, :], nat[:, b2, 2, i, :], start=False,
                                      stop=True).then_inc(x_summed, 1)
                        elif kind == "U":
                            pe.wait_ge(x_ready, j * C + c + 1)
                            if c or not first:
                                pe.wait_ge(u_ready, j * C + c)
                            pe.matmul(u_b[:, 0:P], Tf[:, q % 2, c - c0, :], Xs[:, :], start=True, stop=True).then_inc(u_summed, 1)
                        elif kind == "S":
                            i, b2, o0 = c - c0, q % 2, (c % 8) * RC
                            pe.wait_ge(u_ready, j * C + c + 1)
                            if c < C - 1:
                                pe.matmul(s_b[:, 0:P], nat[:, b2, 0, i, :], Us[:, :], start=True, stop=False)
                                pe.matmul(s_b[:, 0:P], nat[:, b2, 1, i, :], nat[:, b2, 2, i, :], start=False,
                                          stop=True).then_inc(s_summed, 1)
                            if c % 8 == 0 and (c or not first):
                                pe.wait_ge(o_ready, 3 * j + c // 8)
                            cols = slice(c * RC, (c + 1) * RC)
                            pe.matmul(o_b[:, o0:o0 + RC], Us[:, :], rbT[:, b2, i, :], start=True, stop=False)
                            if c < C - 1:
                                pe.matmul(o_b[:, o0:o0 + RC], S[:, c % 2, :], ar[:, 1, cols], start=False, stop=False)
                            else:
                                for b in range(NB):
                                    pe.matmul(o_b[:, b * NT:(b + 1) * NT], S_in[:, b, :],
                                              ar[:, 1, SEQ + b * NT:SEQ + (b + 1) * NT], start=False, stop=False,
                                              skip_group_check=True)
                            pe.matmul(o_b[:, o0:o0 + RC], nat[:, b2, 2, i, :], rkT[:, b2, i, :], start=False,
                                      stop=True).then_inc(o_summed, 1)
                            if c == C - 1:
                                pe.wait_ge(bk_seq_ready, j + 1)
                                pe.wait_ge(S_ready, j * NSR + c + 1)
                                for b in range(NB):
                                    dst = (s_b, xu_b)[b // 4][:, (b % 4) * P:(b % 4 + 1) * P]
                                    pe.matmul(dst, bk_seq[:, 0, b, :], Us[:, :], start=True, stop=False)
                                    last = pe.matmul(dst, bk_seq[:, 1, b, :], nat[:, b2, 2, i, :], start=False, stop=True)
                                    if b % 4 == 3:
                                        last.then_inc(s_summed, 1)
                    pe.wait_ge(o_ready, 3 * (j + 1))
                    pe.wait_ge(T_ready, (j + 1) * NTR)
                    pe.wait_ge(p_ready, (j + 1) * NP)
                    if more:
                        pe.wait_ge(bv_ready, j + 2)
                    sum3(mean[:, :], oT[:, 0:M], norm_summed)
                    pe.wait_ge(d_squared, j + 1)
                    sum3(mean[:, :], rn[:, :], norm_summed)

                for name in PREP:
                    prep(name, 0)
                pair(0, True, True)
                with pe.Fori(1, PAIRS - 1) as j:
                    pair(j, False, True)
                pair(PAIRS - 1, False, False)


MP = (TILES + 1) * P


def merge(nc, t):
    with ExitStack() as ctx:
        s = Stage(nc, ctx, "mg")
        br = s.sb("br", [P, 2, KD, M])
        mT = s.sb("mT", [P, KD, M])
        w = s.sb("w", [P, 2, 2, KD, P])
        gt = s.sb("gt", [P, 2, M])
        tmp = s.sb("tmp", [P, 2, M])
        acc = [s.ps(f"acc{n}", [P, 3, 512]) for n in range(2)]
        br_in, g_in = [s.sem(f"br_in{n}") for n in range(2)], s.sem("g_in")
        w_in = [s.sem(f"w_in{n}") for n in range(2)]
        gates_ready, gated, merged = s.sem("gates_ready"), s.sem("gated"), s.sem("merged")
        summed = [s.sem(f"summed{n}") for n in range(2)]
        w_out = s.sb("w_out", [P, 2, 4 * D])
        mod, mod_s = s.sb("mod", [P, 3, D]), s.sb("mod_s", [NS, 3, D])
        x = s.sb("x", [P, 2, D])
        c_in = s.sem("w_out_in")
        x_in = [s.sem(f"x_in{n}") for n in range(2)]
        with nc.Block() as block:
            @block.sync
            def _(sp):
                sp.dma_start(w[:, 0, :, :, :], t["w_br"][0]).then_inc(w_in[0], 16)
                sp.dma_start(br[:, 0, :, :].rearrange("p (h a) m -> p h a m", a=2),
                             t["ogT"].rearrange("h p a m -> p h a m")).then_inc(br_in[0], 16)
                sp.dma_start(br[:, 1, :, :], t["orT"].rearrange("j p m -> p j m")).then_inc(br_in[1], 16)
                sp.dma_start(w[:, 1, :, :, :], t["w_br"][1]).then_inc(w_in[1], 16)

                def gates(j):
                    for b in range(2):
                        sp.dma_start(gt[:, b, :], t["pT"][j + (50 + KD * b)]).then_inc(g_in, 16)

                gates(0)
                for n in range(2):
                    sp.dma_start(w_out[:, n, :], t["w_out"][n]).then_inc(c_in, 16)
                for n, row in enumerate((G1, A2, S2)):
                    load_mod(sp, t, mod[:, n, :], row, False, c_in)
                    load_mod(sp, t, mod_s[:, n, :], row, True, c_in)
                for n in range(2):
                    sp.dma_start(x[:, n, :], t["x"][n * P:(n + 1) * P, :]).then_inc(x_in[n], 16)
                with sp.Fori(0, KD // 2 - 1) as i:
                    for n in range(2):
                        sp.wait_ge(merged, i * 2 + n + 1)
                        gates(i * 2 + (n + 1))
                        sp.dma_start(w[:, n, :, :, :], t["w_br"][i * 2 + (n + 2)]).then_inc(w_in[n], 16)
                sp.wait_ge(merged, KD - 1)
                gates(KD - 1)

            @block.scalar
            def _(act):
                with act.Fori(0, KD) as i:
                    act.wait_ge(g_in, i * 32 + 32)
                    act.activation(gt[:, :, :], gt[:, :, :], ACT.Sigmoid).then_inc(gates_ready, 1)

            @block.vector
            def _(dve):
                g3 = lambda x: x.rearrange("p (g c) -> p g c", g=3)
                with dve.Fori(0, KD) as i:
                    dve.wait_ge(gates_ready, i + 1)
                    for b in range(2):
                        dve.wait_ge(summed[b], i + 1)
                        dve.tensor_tensor(g3(tmp[:, b, :]), acc[b][:, :, 0:G3], g3(gt[:, b, :]), ALU.mult).then_inc(gated, 1)
                    dve.wait_ge(gated, i * 2 + 2)
                    dve.tensor_tensor(mT[:, i, :], tmp[:, 0, :], tmp[:, 1, :], ALU.add).then_inc(merged, 1)
                    dve.wait_ge(merged, i + 1)

            @block.tensor
            def _(pe):
                def tiles(i, first):
                    for n in range(2):
                        pe.wait_ge(w_in[n], i * 16 + 16)
                        for b in range(2):
                            if first and not n:
                                pe.wait_ge(br_in[b], 16)
                            if not first or n:
                                pe.wait_ge(gated, i * 4 + (2 * n - 1 + b))
                            for g in range(3):
                                for k in range(KD):
                                    last = pe.matmul(acc[b][:, g, 0:G3], w[:, n, b, k, :],
                                                     br[:, b, k, g * G3:(g + 1) * G3], start=(k == 0), stop=(k == KD - 1))
                            last.then_inc(summed[b], 1)

                tiles(0, True)
                with pe.Fori(1, KD // 2) as i:
                    tiles(i, False)

        with ExitStack() as ctx2:
            s = Stage(nc, ctx2, "out")
            free = br[:, :, :, :].rearrange("p a k m -> p (a k m)")
            mt = free[:, 5 * D:7 * D].rearrange("p (n k c) -> p n k c", n=2, k=KD)
            x2 = free[:, 7 * D:9 * D].rearrange("p (n c) -> p n c", n=2)
            h2 = free[:, 9 * D:11 * D].rearrange("p (n c) -> p n c", n=2)
            sq = free[:, 11 * D:12 * D]
            ss = s.sb("ss", [P, 2])
            eps = s.sb("eps", [P, 1])
            (cleared, turned, y_summed, rstd1, rstd2, x2_ready, h2_ready, y_read, oc, oa) = (
                s.sem(n) for n in ("cleared", "mt_ready", "y_summed", "rstd1", "rstd2", "x2_ready",
                                   "h2_ready", "y_read", "vector_chain", "scalar_chain"))
            stored = [s.sem(f"stored{n}") for n in range(2)]
            with nc.Block() as block:
                @block.sync
                def _(sp):
                    def out(row0, rows, n):
                        sp.dma_start(t["x2"][bass.ds(row0, rows), :], x2[0:rows, n, :]).then_inc(stored[n], 16)
                        sp.dma_start(t["h2"][bass.ds(row0, rows), :], h2[0:rows, n, :]).then_inc(stored[n], 16)

                    with sp.Fori(0, TILES // 2 - 1) as i:
                        for n in range(2):
                            sp.wait_ge(h2_ready, i * 2 + n + 1)
                            out(i * (2 * P) + n * P, P, n)
                            sp.dma_start(x[:, n, :], t["x"][bass.ds(i * (2 * P) + (n + 2) * P, P), :]).then_inc(x_in[n], 16)
                    for n in range(2):
                        sp.wait_ge(h2_ready, TILES - 1 + n)
                        out(SEQ - (2 - n) * P, P, n)
                        if n == 0:
                            sp.dma_start(x[0:NS, 0, :], t["x"][SEQ:M, :]).then_inc(x_in[0], 16)
                    sp.wait_ge(h2_ready, TILES + 1)
                    out(SEQ, NS, 0)
                    for g in range(1, P // NS):
                        sp.dma_start(t["h2"][SEQ + g * NS:SEQ + (g + 1) * NS, :], h2[0:NS, 0, :]).then_inc(stored[0], 16)
                    sp.wait_ge(stored[0], 32 * (TILES // 2 + 1) + 16 * (P // NS - 1))
                    sp.wait_ge(stored[1], 32 * (TILES // 2))

                @block.scalar
                def _(act):
                    ch = Chain(act, oa)
                    act.wait_ge(cleared, 1)
                    act.copy(mt[:, 0, :, :], mT[:, :, 0:P]).then_inc(turned, 1)

                    def tile(i, n, rows, nxt, first=False):
                        if nxt is not None:
                            c0, r = nxt
                            if not first:
                                act.wait_ge(y_summed, i)
                            act.copy(mt[:, 1 - n, :, 0:r], mT[:, :, bass.ds(c0, r)]).then_inc(turned, 1)
                        act.wait_ge(y_summed, i + 1)
                        ch.link(act.activation(sq[0:rows, :].rearrange("p (g c) -> p g c", g=2), acc[n][0:rows, 0:2, :],
                                               ACT.Square, accum_out=ss[0:rows, 0:1]))
                        ch.link(act.activation(ss[0:rows, 0:1], ss[0:rows, 0:1], ACT.Ln, bias=eps[0:rows, :], scale=1.0 / D))
                        act.activation(ss[0:rows, 0:1], ss[0:rows, 0:1], ACT.Exp, scale=-0.5).then_inc(rstd1, 1)
                        act.wait_ge(x2_ready, i + 1)
                        ch.link(act.activation(sq[0:rows, :], x2[0:rows, n, :], ACT.Square, accum_out=ss[0:rows, 1:2]))
                        ch.link(act.activation(ss[0:rows, 1:2], ss[0:rows, 1:2], ACT.Ln, bias=eps[0:rows, :], scale=1.0 / D))
                        act.activation(ss[0:rows, 1:2], ss[0:rows, 1:2], ACT.Exp, scale=-0.5).then_inc(rstd2, 1)

                    tile(0, 0, P, (P, P), True)
                    with act.Fori(0, TILES // 2 - 1) as i:
                        ch.enter(i, 8)
                        for n in (1, 0):
                            j = i * 2 + (1 if n else 2)
                            tile(j, n, P, (j * P + P, P))
                        ch.leave(TILES // 2 - 1)
                    tile(TILES - 1, 1, P, (SEQ, NS))
                    tile(TILES, 0, NS, None)

                @block.vector
                def _(dve):
                    ch = Chain(dve, oc)
                    dve.memset(eps[:, :], NORM_EPS).then_inc(cleared, 1)
                    dve.wait_ge(c_in, 16 * (2 + 3 * (1 + NB)))

                    def tile(n, rows, m, i, stores, loads):
                        xr, x2r, h2r = x[0:rows, n, :], x2[0:rows, n, :], h2[0:rows, n, :]
                        dve.wait_ge(rstd1, i + 1)
                        if stores is not None:
                            dve.wait_ge(stored[n], stores)
                        g2 = lambda v: v.rearrange("p (g c) -> p g c", g=2)
                        ch.link(dve.scalar_tensor_tensor(out=g2(x2r), in0=acc[n][0:rows, 0:2, :], scalar=ss[0:rows, 0:1],
                                                         in1=g2(m[:, 0, :]), op0=ALU.mult, op1=ALU.mult))
                        dve.sem_inc(y_read, 1)
                        dve.wait_ge(x_in[n], loads)
                        dve.tensor_tensor(x2r, x2r, xr, ALU.add).then_inc(x2_ready, 1)
                        dve.wait_ge(rstd2, i + 1)
                        ch.link(dve.scalar_tensor_tensor(out=h2r, in0=x2r, scalar=ss[0:rows, 1:2], in1=m[:, 1, :],
                                                         op0=ALU.mult, op1=ALU.mult))
                        dve.tensor_tensor(h2r, h2r, m[:, 2, :], ALU.add).then_inc(h2_ready, 1)

                    for n in range(2):
                        tile(n, P, mod, n, None, 16)
                    with dve.Fori(1, TILES // 2) as i:
                        ch.enter(i - 1, 4)
                        for n in range(2):
                            tile(n, P, mod, i * 2 + n, i * 32, i * 16 + 16)
                        ch.leave(TILES // 2 - 1)
                    tile(0, NS, mod_s, TILES, 32 * (TILES // 2), 16 * (TILES // 2 + 1))

                @block.tensor
                def _(pe):
                    pe.wait_ge(c_in, 16 * (2 + 3 * (1 + NB)))

                    def tile(i, n, rows, first=False):
                        pe.wait_ge(turned, i + 1)
                        if not first:
                            pe.wait_ge(y_read, i - 1)
                        for c in range(2):
                            for k in range(KD):
                                c0 = (k % 4) * D + c * 512
                                last = pe.matmul(acc[n][0:rows, c, :], mt[:, n, k, 0:rows], w_out[:, k // 4, c0:c0 + 512],
                                                 start=(k == 0), stop=(k == KD - 1))
                        last.then_inc(y_summed, 1)

                    tile(0, 0, P, True)
                    tile(1, 1, P, True)
                    with pe.Fori(1, TILES // 2) as i:
                        for n in range(2):
                            tile(i * 2 + n, n, P)
                    tile(TILES, 0, NS)


HEADS, KEYS, TOP = 8, 128, 16
RING = TOP
GROUPS = P // NS
UNITS = TILES * HEADS
S_UNITS = HEADS // GROUPS
HALF = TOP // 2
LOWEST = -3.0e38


def peer(nc, t):
    with ExitStack() as ctx:
        s = Stage(nc, ctx, "peer")
        ident = s.sb("ident", [P, P])
        fold = s.sb("fold", [P, NS])
        iota = s.sb("iota", [P, TOP])
        zeros = s.sb("zeros", [1, 512])
        wq = s.sb("wq", [P, KD, 2 * HEADS * P])
        keys = s.sb("keys", [P, 2 * HEADS, KEYS])
        G2p, G2s = s.sb("G2p", [P, D]), s.sb("G2s", [NS, D])
        ring = s.sb("ring", [P, RING, D])
        h_next, h_now, hT = s.sb("h_next", [P, D]), s.sb("h_now", [P, D]), s.sb("hT", [P, KD, P])
        hT_smp = s.sb("hT_smp", [P, KD, P])
        x2 = s.sb("x2", [P, D])
        acc = s.sb("acc", [P, 2, D])
        y, sq = s.sb("y", [P, D]), s.sb("sq", [P, D])
        idx_all, w_all = s.sb("idx_all", [P, HEADS * TOP], U32), s.sb("w_all", [P, HEADS * TOP])
        idx_smp, w_smp = s.sb("idx_smp", [P, S_UNITS * TOP], U32), s.sb("w_smp", [P, S_UNITS * TOP])
        idx = [s.sb(f"idx{n}", [P, TOP], U32) for n in range(2)]
        w = [s.sb(f"w{n}", [P, TOP]) for n in range(2)]
        dots, act_d, coef = s.sb("dots", [P, TOP]), s.sb("act_d", [P, TOP]), s.sb("coef", [P, TOP])
        diag = s.sb("diag", [P, HALF, P])
        q, qT, sc = s.sb("q", [P, 2 * P]), s.sb("qT", [P, 2 * P]), s.sb("sc", [P, 2, KEYS])
        top, pos = s.sb("top", [P, 2, TOP]), s.sb("pos", [P, 2, TOP], U32)
        posf = s.sb("posf", [P, 2, TOP])
        cand = s.sb("cand", [P, TOP, TOP])
        best, j16, j2 = s.sb("best", [P, TOP]), s.sb("j16", [P, TOP], U32), s.sb("j2", [P, 2, TOP], U32)
        jf = s.sb("jf", [P, 2, TOP])
        hot = s.sb("hot", [P, 2, TOP, TOP])
        sel = s.sb("sel", [P, 2, TOP])
        ex, z = s.sb("ex", [P, TOP]), s.sb("z", [P, 2])
        ss, eps = s.sb("ss", [P, 1]), s.sb("eps", [P, 1])
        q_b, qT_b, s_b = s.ps("q_b"), s.ps("qT_b"), s.ps("s_b")
        h_b = [s.ps(f"h_b{n}") for n in range(2)]
        v_b = s.ps("v_b", [P, 2, 512])
        (consts_in, wq_in, wq_rest_in, cleared, h_in, x2_in, h_turned, hT_ready, h_moved, u_used, v_used, pe_used, dots_ready,
         gelu_ready, coef_ready, diag_ready, q_summed, q_ready, q_turned, qT_ready, s_summed, s_ready, best_ready,
         ex_ready, smp_ready, dealt, idx_ready, issued, v_summed, v_read, total_ready, folded, acc_ready, ms_ready, y_ready,
         y_stored, y_free, passed, passed_pe, own, own_act) = (s.sem(n) for n in (
             "consts_in wq_in wq_rest_in cleared h_in x2_in h_turned hT_ready h_moved u_used v_used pe_used dots_ready "
             "gelu_ready coef_ready diag_ready q_summed q_ready q_turned qT_ready s_summed s_ready best_ready "
             "ex_ready smp_ready dealt idx_ready issued v_summed v_read total_ready folded acc_ready ms_ready y_ready "
             "y_stored y_free passed passed_pe own own_act").split())
        landed = [s.sem(f"landed{n}") for n in range(RING)]
        CONSTS = 4 + NB
        LAST = UNITS - HEADS
        ROUTES = UNITS + HEADS

        with nc.Block() as block:
            @block.sync
            def _(sp):
                sp.dma_start(h_next[:, :], t["h2"][0:P, :]).then_inc(h_in, 16)
                sp.dma_start(ident[:, :], t["ident"]).then_inc(consts_in, 16)
                first = 2 * P
                sp.dma_start(wq[:, :, 0:first], t["peer_wq"][:, :, 0:first]).then_inc(wq_in, 16)
                sp.dma_start(keys[:, :, :], t["peer_keys"]).then_inc(wq_in, 16)
                sp.dma_start(iota[:, :], t["iota"].broadcast_to([P, TOP])).then_inc(consts_in, 16)
                sp.dma_start(fold[:, :], t["fold"]).then_inc(consts_in, 16)
                load_mod(sp, t, G2p, G2, False, consts_in)
                load_mod(sp, t, G2s, G2, True, consts_in)
                sp.wait_ge(wq_in, 32)
                sp.dma_start(wq[:, :, first:], t["peer_wq"][:, :, first:]).then_inc(wq_rest_in, 16)
                sp.dma_start(x2[:, :], t["x2"][0:P, :]).then_inc(x2_in, 16)

                def load_h(i):
                    sp.wait_ge(h_moved, i)
                    sp.dma_start(h_next[:, :], t["h2"][bass.ds(i * P, P), :]).then_inc(h_in, 16)

                def tile(i, rows):
                    sp.wait_ge(y_ready, i + 1)
                    sp.dma_start(t["y"][bass.ds(i * P, rows), :], y[0:rows, :]).then_inc(y_stored, 16)

                sp.sem_inc(y_free, 1)
                load_h(1)
                with sp.Fori(0, TILES - 1) as i:
                    load_h(i + 2)
                    tile(i, P)
                    sp.dma_start(x2[:, :], t["x2"][bass.ds((i + 1) * P, P), :]).then_inc(x2_in, 16)
                    sp.wait_ge(y_stored, i * 16 + 16)
                    sp.sem_inc(y_free, 1)
                tile(TILES - 1, P)
                sp.dma_start(x2[0:NS, :], t["x2"][SEQ:M, :]).then_inc(x2_in, 16)
                sp.wait_ge(y_stored, 16 * TILES)
                sp.sem_inc(y_free, 1)
                tile(TILES, NS)
                sp.wait_ge(y_stored, 16 * (TILES + 1))

            @block.gpsimd
            def _(pool):
                def unit(U, par):
                    pool.wait_ge(idx_ready, U + 1)
                    for k in range(TOP):
                        pool.wait_ge(pe_used if k % 2 else v_used, U * HALF + (k // 2 + 1))
                        pool.sem_inc(issued, 1)
                        pool.indirect_dma_start(
                            out=ring[:, k, :], out_offset=None, in_=t["peer_u"],
                            in_offset=bass.IndirectOffsetOnAxis(ap=idx[par][:, k:k + 1], axis=0)).then_inc(landed[k], 16)
                    for k in range(TOP):
                        pool.wait_ge(u_used, U * TOP + (k + 1))
                        pool.sem_inc(issued, 1)
                        pool.indirect_dma_start(
                            out=ring[:, k, :], out_offset=None, in_=t["peer_v"],
                            in_offset=bass.IndirectOffsetOnAxis(ap=idx[par][:, k:k + 1], axis=0)).then_inc(landed[k], 16)

                with pool.Fori(0, (UNITS + S_UNITS) // 2) as m:
                    for n in range(2):
                        unit(m * 2 + n, n)

            @block.scalar
            def _(act):
                ch = Chain(act, own_act)
                act.sem_inc(diag_ready, HALF)
                act.wait_ge(cleared, 2)
                act.wait_ge(consts_in, 16 * CONSTS)

                def turn_h(i, dst=hT):
                    act.wait_ge(h_turned, i + 1)
                    for n in range(2):
                        act.copy(dst[:, 4 * n:4 * n + 4, :],
                                 h_b[n][:, :].rearrange("p (k c) -> p k c", k=4)).then_inc(hT_ready, 1)

                def scores(R):
                    act.wait_ge(q_summed, R + 1)
                    act.copy(q[:, :], q_b[:, 0:2 * P]).then_inc(q_ready, 1)
                    act.wait_ge(q_turned, R + 1)
                    act.copy(qT[:, :], qT_b[:, 0:2 * P]).then_inc(qT_ready, 1)
                    act.wait_ge(s_summed, R + 1)
                    act.copy(sc[:, :, :].rearrange("p a n -> p (a n)"), s_b[:, 0:2 * KEYS]).then_inc(s_ready, 1)

                def exps(R):
                    act.wait_ge(best_ready, R + 1)
                    act.activation(ex[:, :], best[:, :], ACT.Exp, bias=z[:, 1:2], accum_out=z[:, 0:1]).then_inc(ex_ready, 1)

                def weigh(U):
                    act.wait_ge(dots_ready, U + 1)
                    act.wait_ge(diag_ready, U * HALF + HALF)
                    act.activation(act_d[:, :], dots[:, :], ACT.Gelu).then_inc(gelu_ready, 1)
                    act.wait_ge(coef_ready, U + 1)
                    for j in range(HALF):
                        act.wait_ge(pe_used, U * HALF + (j + 1))
                        act.activation(diag[:, j, :], ident[:, :], ACT.Copy,
                                       scale=coef[:, 2 * j + 1:2 * j + 2]).then_inc(diag_ready, 1)

                def finish(i, rows):
                    act.wait_ge(acc_ready, i + 1)
                    ch.link(act.activation(sq[0:rows, :], acc[0:rows, 0, :], ACT.Square, accum_out=ss[0:rows, :]))
                    ch.link(act.activation(ss[0:rows, :], ss[0:rows, :], ACT.Ln, bias=eps[0:rows, :], scale=1.0 / D))
                    act.activation(ss[0:rows, :], ss[0:rows, :], ACT.Exp, scale=-0.5).then_inc(ms_ready, 1)

                turn_h(0)
                scores(0)
                exps(0)
                act.copy(h_now[:, :], h_next[:, :]).then_inc(h_moved, 1)
                with act.Fori(0, TILES - 1) as i:
                    ch.enter(i, 2)
                    with act.Fori(0, HEADS - 1) as h:
                        scores(i * HEADS + h + 1)
                        weigh(i * HEADS + h)
                        exps(i * HEADS + h + 1)
                    turn_h(i + 1)
                    scores(i * HEADS + HEADS)
                    weigh(i * HEADS + (HEADS - 1))
                    exps(i * HEADS + HEADS)
                    act.copy(h_now[:, :], h_next[:, :]).then_inc(h_moved, 1)
                    finish(i, P)
                    ch.leave(TILES - 1)
                turn_h(TILES, hT_smp)
                with act.Fori(0, HEADS - 1) as h:
                    scores(h * 2 + (LAST + 1))
                    weigh(h + LAST)
                    exps(h * 2 + (LAST + 1))
                    scores(h * 2 + (LAST + 2))
                    exps(h * 2 + (LAST + 2))
                scores(ROUTES - 1)
                weigh(UNITS - 1)
                exps(ROUTES - 1)
                act.copy(h_now[:, :], h_next[:, :]).then_inc(h_moved, 1)
                finish(TILES - 1, P)
                for n in range(S_UNITS):
                    weigh(UNITS + n)
                finish(TILES, NS)

            @block.vector
            def _(dve):
                ch = Chain(dve, own)
                dve.memset(eps[:, :], NORM_EPS).then_inc(cleared, 1)
                dve.memset(zeros[:, :], 0.0).then_inc(cleared, 1)
                dve.sem_inc(v_used, HALF)
                dve.wait_ge(consts_in, 16 * CONSTS)

                def alone(ins):
                    ch.link(ins)
                    dve.sem_inc(passed, 1)

                def top16(vals, val, place):
                    for n in range(2):
                        o8 = slice(8 * n, 8 * n + 8)
                        alone(dve.max(val[:, o8], vals))
                        last = dve.max_index(place[:, o8], val[:, o8], vals)
                        if n == 0:
                            alone(last)
                            alone(dve.match_replace(vals, val[:, o8], vals, LOWEST))
                    return last

                def route_keys(R):
                    dve.wait_ge(s_ready, R + 1)
                    dve.sem_inc(passed, 1)
                    for n in range(2):
                        last = top16(sc[:, n, :], top[:, n, :], pos[:, n, :])
                    ch.link(last)

                def route_pairs(R, idx_to, w_to, to_pool):
                    dve.tensor_copy(posf[:, :, :], pos[:, :, :])
                    alone(dve.tensor_tensor(cand[:, :, :], top[:, 0, :].unsqueeze(2).broadcast_to([P, TOP, TOP]),
                                            top[:, 1, :].unsqueeze(1).broadcast_to([P, TOP, TOP]), ALU.add))
                    ch.link(top16(cand[:, :, :].rearrange("p a b -> p (a b)"), best, j16))
                    dve.tensor_scalar(z[:, 1:2], best[:, 0:1], -1.0, None, ALU.mult).then_inc(best_ready, 1)
                    dve.tensor_scalar(j2[:, 0, :], j16[:, :], 4, None, ALU.logical_shift_right)
                    ch.link(dve.tensor_scalar(j2[:, 1, :], j16[:, :], TOP - 1, None, ALU.bitwise_and))
                    ch.link(dve.tensor_copy(jf[:, :, :], j2[:, :, :]))
                    for n in range(2):
                        last = dve.tensor_tensor(hot[:, n, :, :], jf[:, n, :].unsqueeze(2).broadcast_to([P, TOP, TOP]),
                                                 iota[:, :].unsqueeze(1).broadcast_to([P, TOP, TOP]), ALU.is_equal)
                    ch.link(last)
                    for n in range(2):
                        last = dve.tensor_tensor(hot[:, n, :, :], hot[:, n, :, :],
                                                 posf[:, n, :].unsqueeze(1).broadcast_to([P, TOP, TOP]), ALU.mult)
                    ch.link(last)
                    ch.link(dve.tensor_reduce(sel[:, :, :], hot[:, :, :, :], AX.X, ALU.add))
                    dve.scalar_tensor_tensor(out=idx_to, in0=sel[:, 0, :], scalar=float(KEYS),
                                             in1=sel[:, 1, :], op0=ALU.mult,
                                             op1=ALU.add).then_inc(idx_ready if to_pool else smp_ready, 1)
                    dve.wait_ge(ex_ready, R + 1)
                    ch.link(dve.reciprocal(z[:, 0:1], z[:, 0:1]))
                    ch.link(dve.tensor_scalar(w_to, ex[:, :], z[:, 0:1], None, ALU.mult))

                def unit(U, weights, R=None, par=None):
                    for k in range(TOP):
                        dve.wait_ge(landed[k], U * 32 + 16)
                        dve.tensor_tensor_reduce(ring[:, k, :], ring[:, k, :], h_now[:, :], 1.0, 0.0,
                                                 ALU.mult, ALU.add, dots[:, k:k + 1]).then_inc(u_used, 1)
                    dve.wait_ge(u_used, U * TOP + TOP)
                    dve.sem_inc(dots_ready, 1)
                    if R is not None:
                        route_keys(R)
                    dve.wait_ge(gelu_ready, U + 1)
                    dve.wait_ge(v_used, U * HALF + HALF)
                    dve.tensor_tensor(coef[:, :], act_d[:, :], weights, ALU.mult).then_inc(coef_ready, 1)
                    if par is not None:
                        route_pairs(R, idx[par][:, :], w[par][:, :], True)
                    elif R is not None:
                        route_pairs(R, *samples_head(HEADS - 1), False)

                def add_v(U):
                    dve.wait_ge(coef_ready, U + 1)
                    for j in range(HALF):
                        k = 2 * j
                        dve.wait_ge(landed[k], U * 32 + 32)
                        if j < 2:
                            dve.wait_ge(v_used, U * HALF + HALF)
                        else:
                            dve.wait_ge(v_used, U * HALF + (HALF + j - 1))
                        dve.scalar_tensor_tensor(out=acc[:, j % 2, :], in0=ring[:, k, :], scalar=coef[:, k:k + 1],
                                                 in1=acc[:, j % 2, :], op0=ALU.mult, op1=ALU.add).then_inc(v_used, 1)

                def clear():
                    dve.memset(acc[:, :, :], 0.0).then_inc(own, 1)
                    ch.n += 1
                    dve.wait_ge(own, ch.base + ch.n)
                    dve.sem_inc(passed, 1)

                def total(i, units):
                    dve.wait_ge(v_used, units * HALF + HALF)
                    ch.link(dve.tensor_tensor(acc[:, 0, :], acc[:, 0, :], acc[:, 1, :], ALU.add))
                    dve.wait_ge(v_summed, i + 1)
                    ch.link(dve.tensor_tensor(acc[:, 0, :].rearrange("p (g c) -> p g c", g=2),
                                              acc[:, 0, :].rearrange("p (g c) -> p g c", g=2), v_b[:, :, :], ALU.add))

                def finish(i, rows, gain):
                    dve.sem_inc(acc_ready, 1)
                    dve.wait_ge(ms_ready, i + 1)
                    dve.wait_ge(x2_in, i * 16 + 16)
                    dve.wait_ge(y_free, i + 1)
                    ch.link(dve.scalar_tensor_tensor(out=y[0:rows, :], in0=acc[0:rows, 0, :], scalar=ss[0:rows, 0:1],
                                                     in1=gain, op0=ALU.mult, op1=ALU.mult))
                    dve.tensor_tensor(y[0:rows, :], y[0:rows, :], x2[0:rows, :], ALU.add).then_inc(y_ready, 1)

                def samples_head(h):
                    cols = bass.ds(h * TOP, TOP)
                    return idx_all[:, cols], w_all[:, cols]

                ROUTE = 22
                route_keys(0)
                route_pairs(0, idx[0][:, :], w[0][:, :], True)
                assert ch.n == ROUTE, ch.n
                ch0 = ch.n
                PER = 1 + HEADS * ROUTE + 3

                def tile_end(i, link0):
                    ch.base, ch.n = link0, 0
                    total(i, i * HEADS + HEADS)
                    dve.sem_inc(v_read, 1)
                    finish(i, P, G2p[:, :])
                    assert ch.n == 3

                with dve.Fori(0, TILES - 1) as i:
                    dve.wait_ge(h_moved, i + 1)
                    ch.base, ch.n = ch0 + i * PER, 0
                    clear()
                    with dve.Fori(0, HEADS // 2) as m:
                        ch.base, ch.n = ch0 + i * PER + 1 + m * (2 * ROUTE), 0
                        for n in range(2):
                            U = i * HEADS + m * 2 + n
                            unit(U, w[n][:, :], U + 1, 1 - n)
                            add_v(U)
                        assert ch.n == 2 * ROUTE, ch.n
                    tile_end(i, ch0 + i * PER + 1 + HEADS * ROUTE)

                def deal():
                    dve.wait_ge(smp_ready, HEADS)
                    for g in range(GROUPS):
                        rows = slice(g * NS, (g + 1) * NS)
                        dve.tensor_copy(w_smp[rows, :], w_all[rows, g:HEADS * TOP:GROUPS]).then_inc(dealt, 1)
                        dve.tensor_copy(idx_smp[rows, :], idx_all[rows, g:HEADS * TOP:GROUPS]).then_inc(dealt, 1)
                    dve.wait_ge(dealt, 2 * GROUPS)
                    dve.tensor_copy(idx[0][:, :], idx_smp[:, 0:TOP]).then_inc(idx_ready, 1)

                last = TILES - 1
                dve.wait_ge(h_moved, TILES)
                ch.base, ch.n = ch0 + last * PER, 0
                clear()

                def last_unit(h, par):
                    R = h * 2 + (LAST + 1)
                    unit(h + LAST, w[par][:, :], R, 1 - par)
                    route_keys(R + 1)
                    route_pairs(R + 1, *samples_head(h), False)
                    add_v(h + LAST)

                with dve.Fori(0, HEADS // 2 - 1) as m:
                    ch.base, ch.n = ch0 + last * PER + 1 + m * (4 * ROUTE), 0
                    for n in range(2):
                        last_unit(m * 2 + n, n)
                    assert ch.n == 4 * ROUTE
                ch.base, ch.n = ch0 + last * PER + 1 + (HEADS - 2) * 2 * ROUTE, 0
                last_unit(HEADS - 2, 0)
                unit(UNITS - 1, w[1][:, :], ROUTES - 1)
                deal()
                add_v(UNITS - 1)
                tile_end(last, ch0 + last * PER + 1 + (2 * HEADS - 1) * ROUTE)

                dve.wait_ge(h_moved, TILES + 1)
                ch.base, ch.n = ch0 + TILES * PER + (HEADS - 1) * ROUTE, 0
                clear()
                for n in range(S_UNITS):
                    unit(UNITS + n, w_smp[:, n * TOP:(n + 1) * TOP])
                    if n + 1 < S_UNITS:
                        dve.tensor_copy(idx[1 - n][:, :], idx_smp[:, (n + 1) * TOP:(n + 2) * TOP]).then_inc(idx_ready, 1)
                    add_v(UNITS + n)
                total(TILES, UNITS + S_UNITS)
                dve.sem_inc(total_ready, 1)
                dve.wait_ge(folded, 1)
                ch.link(dve.tensor_copy(acc[0:NS, 0, :].rearrange("p (g c) -> p g c", g=2), v_b[0:NS, :, :]))
                finish(TILES, NS, G2s[:, :])

            @block.tensor
            def _(pe):
                pe.sem_inc(pe_used, HALF)
                pe.wait_ge(cleared, 2)
                pe.wait_ge(consts_in, 16 * CONSTS)

                def turn_h(i):
                    pe.wait_ge(h_in, i * 16 + 16)
                    for k in range(KD):
                        last = pe.transpose(h_b[k // 4][:, (k % 4) * P:(k % 4 + 1) * P], h_next[:, k * P:(k + 1) * P],
                                            ident[:, :])
                    last.then_inc(h_turned, 1)
                    pe.wait_ge(hT_ready, i * 2 + 2)
                    pe.sem_inc(passed_pe, 1)

                def route(R, h, hT=hT):
                    for k in range(KD):
                        last = pe.matmul(q_b[:, 0:2 * P], hT[:, k, :], wq[:, k, bass.ds(h * (2 * P), 2 * P)],
                                         start=(k == 0), stop=(k == KD - 1))
                    last.then_inc(q_summed, 1)
                    pe.wait_ge(q_ready, R + 1)
                    for n in range(2):
                        last = pe.transpose(qT_b[:, n * P:(n + 1) * P], q[:, n * P:(n + 1) * P], ident[:, :])
                    last.then_inc(q_turned, 1)
                    pe.wait_ge(qT_ready, R + 1)
                    for n in range(2):
                        last = pe.matmul(s_b[:, n * KEYS:(n + 1) * KEYS], qT[:, n * P:(n + 1) * P],
                                         keys[:, bass.ds(h * 2 + n, 1), :].rearrange("p o n -> p (o n)"), start=True, stop=True)
                    last.then_inc(s_summed, 1)
                    pe.wait_ge(s_ready, R + 1)

                def zero_banks(start):
                    for c in range(2):
                        last = pe.matmul(v_b[:, c, :], zeros[:, 0:P], zeros[:, :], start=start, stop=not start)
                    return last

                def add_v(U):
                    for j in range(HALF):
                        k = 2 * j + 1
                        pe.wait_ge(diag_ready, U * HALF + (HALF + j + 1))
                        pe.wait_ge(landed[k], U * 32 + 32)
                        for c in range(2):
                            last = pe.matmul(v_b[:, c, :], diag[:, j, :], ring[:, k, c * 512:(c + 1) * 512],
                                             start=False, stop=False)
                        last.then_inc(pe_used, 1)

                pe.wait_ge(wq_in, 32)
                turn_h(0)
                route(0, 0)
                zero_banks(True)
                pe.wait_ge(wq_rest_in, 16)

                def tile_end(i):
                    zero_banks(False).then_inc(v_summed, 1)
                    pe.wait_ge(v_read, i + 1)
                    zero_banks(True)

                with pe.Fori(0, TILES - 1) as i:
                    with pe.Fori(0, HEADS - 1) as h:
                        route(i * HEADS + h + 1, h + 1)
                        add_v(i * HEADS + h)
                    turn_h(i + 1)
                    route(i * HEADS + HEADS, 0)
                    add_v(i * HEADS + (HEADS - 1))
                    tile_end(i)
                turn_h(TILES)
                with pe.Fori(0, HEADS - 1) as h:
                    route(h * 2 + (LAST + 1), h + 1)
                    route(h * 2 + (LAST + 2), h, hT_smp)
                    add_v(h + LAST)
                route(ROUTES - 1, HEADS - 1, hT_smp)
                add_v(UNITS - 1)
                tile_end(TILES - 1)
                for n in range(S_UNITS):
                    add_v(UNITS + n)
                zero_banks(False).then_inc(v_summed, 1)
                pe.wait_ge(total_ready, 1)
                for c in range(2):
                    last = pe.matmul(v_b[0:NS, c, :], fold[:, :], acc[:, 0, c * 512:(c + 1) * 512], start=True, stop=True)
                last.then_inc(folded, 1)


def scratch(nc, t):
    for name, shape in {"mod": [NSEQ, 6, D], "pT": [66, P, M], "gaT": [16, M],
                        "ogT": [GH, P, 2, M], "orT": [PAIRS, P, M],
                        "x2": [M, D], "h2": [MP, D]}.items():
        t[name] = nc.dram_tensor(name, shape, F32, kind="Internal").ap()


def build(nc, t):
    scratch(nc, t)
    for stage in (front, gla, rwkv, merge, peer):
        with nc.cleanup_on_exit():
            stage(nc, t)


OUTPUTS = {"y": [M, D], "new_gla_p": [GH, P, GV], "new_gla_s": [GH, P, NB, GV],
           "new_rw_p": [PAIRS, 2, RH, RH], "new_rw_s": [PAIRS, 2, RH, NB, RH],
           "new_shift": [PAIRS, 3, P, NSEQ], "new_shift_wg": [2, P, NSEQ]}


def masks():
    f = np.float32
    s, q = np.arange(P), np.arange(NS)
    same_chunk = s[:, None] // GC == s[None] // GC
    same_seq = q[:, None] // NT == q[None] // NT
    tok = np.arange(MW)
    head, pos = s // RH, s % RH
    same_head = head[:, None] == head[None]
    before = pos[:, None] < pos[None]
    seq_pos = (pos[:, None] // NT == pos[None] // NT) & (pos[:, None] < NS) & (pos[None] < NS)
    t = np.arange(RC)
    upto = pos[:, None] <= t[None]
    ones_joined = same_head & (pos[:, None] == pos[None] + 1) & (pos[None] % 2 == 0)
    joins = [same_head & (pos[:, None] // (2 * n) == pos[None] // (2 * n)) & (pos[:, None] // n % 2 == 0)
             & (pos[None] // n % 2 == 1) for n in (2 ** (l + 1) for l in range(LEVELS))]
    c = {
        "ident": s[:, None] == s[None],
        "iota": np.arange(TOP)[None],
        "fold": s[:, None] % NS == q[None],
        "starts": np.where(tok < SEQ, tok % GC != 0, tok % NT != 0)[None],
        "gla_mask": same_chunk & (s[:, None] <= s[None]),
        "gla_mask_s": same_seq & (q[:, None] <= q[None]),
        "seq_rows": q[:, None] // NT == np.arange(NB)[None],
        "rw_strict": np.stack([same_head & before, same_head & before & seq_pos], 1),
        "rw_incl": np.stack([upto, upto & (pos[:, None] // NT == t[None] // NT)], 1),
        "rw_first_l": ones_joined,
        "rw_first_u": ones_joined.T,
        "rw_join": np.stack(joins, 1),
        "rw_seq_cols": np.broadcast_to((pos[None] // NT == np.arange(NB)[:, None])[None], (P, NB, P)),
        "rw_seq_rows": pos[:, None] // NT == np.arange(NB)[None],
        "rw_heads": same_head,
    }
    c = {k: np.ascontiguousarray(v.astype(f)) for k, v in c.items()}
    c["rw_mean"] = c["rw_heads"] / f(RH)
    return c


def layout(i):
    o = {}
    o["x"] = np.concatenate([i["x_prompt"].reshape(SEQ, D), i["x_sample"].reshape(NS, D)])
    c = np.concatenate([i["c_prompt"], i["c_sample"]])
    o["cT"] = c.T.reshape(KD, P, NSEQ).transpose(1, 0, 2).reshape(P, KD * NSEQ)
    o["w_ada"] = i["w_ada"][0].reshape(KD, P, 12, 512).transpose(2, 1, 0, 3).reshape(12, P, KD * 512)
    o["b_ada"] = i["b_ada"]
    o["gains"] = np.concatenate([i["g_pre_mix"], i["g_post_mix"], i["g_pre_ffn"], i["g_post_ffn"]])
    w = i["w_in"][0]
    ga0 = 2 * GH * P + 2 * GH * GV
    rest = np.concatenate([w[:, :ga0], w[:, ga0 + 16:]], 1)
    o["w_in"] = rest.reshape(KD, P, 66, P).transpose(2, 1, 0, 3)
    o["w_ga"] = w[:, ga0:ga0 + 16].reshape(KD, P, 16).transpose(1, 0, 2)
    o["w_gate"] = i["w_gla_gate"][0].reshape(16, GH, P).transpose(1, 0, 2)
    o["gla_cst"] = np.concatenate([i["b_gla_gate"][0].reshape(GH, P, 1),
                                   i["g_gla_norm"][0].reshape(GH, 2, P).transpose(0, 2, 1)], 2)
    o["state_gla"] = i["state_gla"][0].transpose(1, 2, 0, 3)
    mu = i["mu_shift"][0].reshape(26, P)
    vec = [i[k][0].reshape(PAIRS, P) for k in ("rw_w0", "rw_a0", "rw_k_k", "rw_k_a", "rw_r_k", "rw_gn_w", "rw_gn_b")]
    o["rw_cst"] = np.stack([mu[0:8], mu[8:16], mu[16:24]] + vec).transpose(2, 1, 0)
    o["rw_mu_wg"] = mu[24:26].T
    sh = i["state_shift"][0].reshape(NB, 26, P)
    o["rw_sh_wg"] = sh[:, 24:26].transpose(2, 1, 0)
    o["rw_sh"] = sh[:, :24].reshape(NB, 3, PAIRS, P).transpose(2, 3, 1, 0)
    o["w2a2"] = np.concatenate([i["rw_w2"][0], i["rw_a2"][0]]).reshape(P, PAIRS, P).transpose(1, 0, 2)
    o["g2"] = i["rw_g2"][0].reshape(P, PAIRS, P).transpose(1, 0, 2)
    o["state_rwkv"] = i["state_rwkv"][0].reshape(NB, PAIRS, 2, RH, RH).transpose(1, 2, 4, 0, 3)
    wb = np.stack([i["w_b_gla"][0], i["w_b_rw"][0]])
    o["w_br"] = wb.reshape(2, KD, P, KD, P).transpose(3, 2, 0, 1, 4)
    o["w_out"] = i["w_out"][0].reshape(2, 4, P, D).transpose(0, 2, 1, 3).reshape(2, P, 4 * D)
    o["peer_wq"] = i["peer_wq"][0].reshape(KD, P, 2 * HEADS * P).transpose(1, 0, 2)
    o["peer_keys"] = i["peer_keys"][0].reshape(2 * HEADS, KEYS, P).transpose(2, 0, 1)
    o["peer_u"], o["peer_v"] = i["peer_u"][0], i["peer_v"][0]
    return {k: np.ascontiguousarray(v) for k, v in o.items()}


def kernel(**inputs):
    from concourse import bacc
    from concourse.bass_utils import run_bass_kernel_spmd

    nc = bacc.Bacc("TRN2", target_bir_lowering=False, num_devices=1)
    arrays = {**layout({k: np.asarray(v) for k, v in inputs.items()}), **masks()}
    t = {k: nc.dram_tensor(f"in_{k}", v.shape, F32, kind="ExternalInput").ap() for k, v in arrays.items()}
    for k, shape in OUTPUTS.items():
        t[k] = nc.dram_tensor(f"out_{k}", shape, F32, kind="ExternalOutput").ap()
    build(nc, t)
    r = run_bass_kernel_spmd(nc, [{f"in_{k}": v for k, v in arrays.items()}], core_ids=[0]).results[0]
    r = {k: r[f"out_{k}"] for k in OUTPUTS}
    y = r["y"]
    shift = r["new_shift"].transpose(3, 1, 0, 2).reshape(NSEQ, 3 * PAIRS * P)
    shift = np.concatenate([shift, r["new_shift_wg"].transpose(2, 0, 1).reshape(NSEQ, 2 * P)], 1)
    return (y[:SEQ].reshape(1, SEQ, D), y[SEQ:].reshape(NB, NT, D),
            r["new_gla_p"].reshape(1, 1, GH, P, GV),
            r["new_rw_p"].transpose(0, 1, 3, 2).reshape(1, 1, 2 * PAIRS, RH, RH),
            shift[0].reshape(1, 1, -1),
            r["new_gla_s"].transpose(2, 0, 1, 3).reshape(1, NB, GH, P, GV),
            r["new_rw_s"].transpose(3, 0, 1, 4, 2).reshape(1, NB, 2 * PAIRS, RH, RH),
            shift[1:].reshape(1, NB, -1))
```
